# Optimizing a Trainium2 kernel written in Bass

```python
import jax, jax.numpy as jnp
from jax import lax
import numpy as np
import math

D_MODEL = 1024
BATCH = 1
SEQ = 256
DEPTH = 1

CHUNK = 64
HEAD_DIM = 64
A_HEADS = 4
A_LEFT_CHUNKS = 8
A_MAX_REL = 128
B_HEADS = 4
C_HEADS = 4
IDX_HEADS = 4
IDX_DIM = 64
TOPK_MAX = 256
N_BRANCH = 3
MIX_W = 256
D_FF = 2816
CONV_W = 3
Q_BLOCK = 128
ROPE_THETA = 10000.0
EPS = 1e-6
NEG = -1e30

COL_SIZES = (MIX_W, MIX_W, MIX_W,
             MIX_W, MIX_W, MIX_W, B_HEADS,
             MIX_W, HEAD_DIM, HEAD_DIM,
             IDX_HEADS * IDX_DIM, IDX_DIM, IDX_HEADS,
             N_BRANCH * D_MODEL)
N_IN = sum(COL_SIZES)


def _rmsnorm(x, g):
    xf = x.astype(jnp.float32)
    y = xf * lax.rsqrt(jnp.mean(xf * xf, axis=-1, keepdims=True) + EPS)
    return (y * g.astype(jnp.float32)).astype(x.dtype)

def _rope(x, cos, sin):
    xf = x.astype(jnp.float32)
    x1, x2 = jnp.split(xf, 2, axis=-1)
    c = cos[None, :, None, :]
    s = sin[None, :, None, :]
    return jnp.concatenate([x1 * c - x2 * s, x1 * s + x2 * c], axis=-1).astype(x.dtype)

def _blocks_to_seq(out):
    nb, b, blk, h, d = out.shape
    return out.transpose(1, 0, 2, 3, 4).reshape(b, nb * blk, h, d)

def _chunk_band_attention(q, k, v, rel_table):
    S = q.shape[1]
    dh = q.shape[-1]
    n_chunks = S // CHUNK
    pad = A_LEFT_CHUNKS * CHUNK
    band = pad + CHUNK
    kp = jnp.pad(k, ((0, 0), (pad, 0), (0, 0), (0, 0)))
    vp = jnp.pad(v, ((0, 0), (pad, 0), (0, 0), (0, 0)))
    qi = jnp.arange(CHUNK)
    kj = jnp.arange(band)
    rel = qi[:, None] + pad - kj[None, :]
    bias = rel_table[:, jnp.clip(rel, -A_MAX_REL, A_MAX_REL) + A_MAX_REL].astype(jnp.float32)
    scale = dh ** -0.5

    def one_chunk(n):
        start = n * CHUNK
        qc = lax.dynamic_slice_in_dim(q, start, CHUNK, axis=1)
        kc = lax.dynamic_slice_in_dim(kp, start, band, axis=1)
        vc = lax.dynamic_slice_in_dim(vp, start, band, axis=1)
        s = jnp.einsum('bqhd,bkhd->bhqk', qc, kc).astype(jnp.float32) * scale + bias
        valid = (start - pad + kj) >= 0
        s = jnp.where(valid[None, None, None, :], s, NEG)
        p = jax.nn.softmax(s, axis=-1).astype(v.dtype)
        return jnp.einsum('bhqk,bkhd->bqhd', p, vc)

    return _blocks_to_seq(lax.map(one_chunk, jnp.arange(n_chunks)))

def _forgetting_attention(q, k, v, log_f):
    S = q.shape[1]
    dh = q.shape[-1]
    cum = jnp.cumsum(log_f, axis=1).transpose(0, 2, 1)
    kpos = jnp.arange(S)
    scale = dh ** -0.5

    def one_block(i):
        start = i * Q_BLOCK
        qb = lax.dynamic_slice_in_dim(q, start, Q_BLOCK, axis=1)
        cq = lax.dynamic_slice_in_dim(cum, start, Q_BLOCK, axis=2)
        s = jnp.einsum('bqhd,bkhd->bhqk', qb, k).astype(jnp.float32) * scale
        s = s + cq[..., :, None] - cum[:, :, None, :]
        qpos = start + jnp.arange(Q_BLOCK)
        s = jnp.where((kpos[None, :] <= qpos[:, None])[None, None], s, NEG)
        p = jax.nn.softmax(s, axis=-1).astype(v.dtype)
        return jnp.einsum('bhqk,bkhd->bqhd', p, v)

    return _blocks_to_seq(lax.map(one_block, jnp.arange(S // Q_BLOCK)))

def _indexed_sparse_attention(q, k, v, q_idx, k_idx, w_idx):
    S = q.shape[1]
    dh = q.shape[-1]
    topk = min(TOPK_MAX, S // 4)
    chunk_k = jnp.arange(S) // CHUNK
    scale = dh ** -0.5

    def one_block(i):
        start = i * Q_BLOCK
        qb = lax.dynamic_slice_in_dim(q, start, Q_BLOCK, axis=1)
        qib = lax.dynamic_slice_in_dim(q_idx, start, Q_BLOCK, axis=1)
        wb = lax.dynamic_slice_in_dim(w_idx, start, Q_BLOCK, axis=1).astype(jnp.float32)
        logits = jnp.einsum('bqhd,bkd->bqhk', qib, k_idx).astype(jnp.float32)
        score = jnp.einsum('bqh,bqhk->bqk', wb, jax.nn.relu(logits))
        chunk_q = (start + jnp.arange(Q_BLOCK)) // CHUNK
        adm = chunk_k[None, :] <= chunk_q[:, None]
        score = jnp.where(adm[None], score, NEG)
        _, sel = lax.top_k(score, topk)
        sel_ok = chunk_k[sel] <= chunk_q[None, :, None]
        k_sel = jax.vmap(lambda kk, ii: kk[ii])(k, sel)
        v_sel = jax.vmap(lambda vv, ii: vv[ii])(v, sel)
        s = jnp.einsum('bqhd,bqkd->bhqk', qb, k_sel).astype(jnp.float32) * scale
        s = jnp.where(sel_ok[:, None], s, NEG)
        p = jax.nn.softmax(s, axis=-1).astype(v.dtype)
        return jnp.einsum('bhqk,bqkd->bqhd', p, v_sel)

    return _blocks_to_seq(lax.map(one_block, jnp.arange(S // Q_BLOCK)))

def _hybrid_mixer(h, w_in, b_gate, rel_table, b_forget, w_branch, w_out, cos, sin):
    B_, S, _ = h.shape
    z = h @ w_in
    offs = np.cumsum(np.array(COL_SIZES))[:-1].tolist()
    (qa, ka, va, qb, kb, vb, fb, qc, kc, vc, qi, ki, wi, zg) = jnp.split(z, offs, axis=-1)
    heads = lambda t, n: t.reshape(B_, S, n, -1)

    ya = _chunk_band_attention(heads(qa, A_HEADS), heads(ka, A_HEADS), heads(va, A_HEADS), rel_table)

    log_f = jax.nn.log_sigmoid(fb.astype(jnp.float32) + b_forget.astype(jnp.float32))
    yb = _forgetting_attention(heads(qb, B_HEADS), heads(kb, B_HEADS), heads(vb, B_HEADS), log_f)

    qc_r = _rope(heads(qc, C_HEADS), cos, sin)
    kc_r = _rope(kc[:, :, None, :], cos, sin)[:, :, 0, :]
    qi_r = _rope(heads(qi, IDX_HEADS), cos, sin) * (IDX_DIM ** -0.5)
    ki_r = _rope(ki[:, :, None, :], cos, sin)[:, :, 0, :]
    wi_s = wi * (IDX_HEADS ** -0.5)
    yc = _indexed_sparse_attention(qc_r, kc_r, vc, qi_r, ki_r, wi_s)

    gates = jax.nn.sigmoid(zg.reshape(B_, S, N_BRANCH, D_MODEL) + b_gate)
    merged = (gates[:, :, 0] * (ya.reshape(B_, S, MIX_W) @ w_branch[0])
              + gates[:, :, 1] * (yb.reshape(B_, S, MIX_W) @ w_branch[1])
              + gates[:, :, 2] * (yc.reshape(B_, S, MIX_W) @ w_branch[2]))
    return merged @ w_out

def _conv_ffn(h, w_up, conv_w, conv_b, w_down):
    a, g = jnp.split(h @ w_up, 2, axis=-1)
    a = lax.conv_general_dilated(a, conv_w[:, None, :], window_strides=(1,),
                                 padding=[(CONV_W - 1, 0)],
                                 dimension_numbers=('NWC', 'WIO', 'NWC'),
                                 feature_group_count=D_FF) + conv_b
    return (jax.nn.gelu(a) * g) @ w_down

def first_inputs(seed: int = 0) -> dict:
    key = jax.random.key(seed)
    ks = jax.random.split(key, 16)
    f32 = jnp.float32
    nrm = lambda k, shape, s: jax.random.normal(k, shape, f32) * s
    return {
        'x': nrm(ks[0], (BATCH, SEQ, D_MODEL), 1.0),
        'c': nrm(ks[1], (BATCH, D_MODEL), 1.0),
        'w_ada': nrm(ks[2], (DEPTH, D_MODEL, 6 * D_MODEL), D_MODEL ** -0.5),
        'b_ada': nrm(ks[3], (DEPTH, 6 * D_MODEL), 0.01),
        'norm_g': 1.0 + nrm(ks[4], (DEPTH, 4, D_MODEL), 0.05),
        'w_in': nrm(ks[5], (DEPTH, D_MODEL, N_IN), D_MODEL ** -0.5),
        'b_gate': nrm(ks[6], (DEPTH, N_BRANCH, D_MODEL), 0.01),
        'rel_table': nrm(ks[7], (DEPTH, A_HEADS, 2 * A_MAX_REL + 1), 0.2),
        'b_forget': jax.random.uniform(ks[8], (DEPTH, B_HEADS), f32, 1.0, 4.0),
        'w_branch': nrm(ks[9], (DEPTH, N_BRANCH, MIX_W, D_MODEL), MIX_W ** -0.5),
        'w_out': nrm(ks[10], (DEPTH, D_MODEL, D_MODEL), D_MODEL ** -0.5),
        'w_up': nrm(ks[11], (DEPTH, D_MODEL, 2 * D_FF), D_MODEL ** -0.5),
        'conv_w': nrm(ks[12], (DEPTH, CONV_W, D_FF), CONV_W ** -0.5),
        'conv_b': nrm(ks[13], (DEPTH, D_FF), 0.01),
        'w_down': nrm(ks[14], (DEPTH, D_FF, D_MODEL), D_FF ** -0.5),
    }

def first_block(x, c, w_ada, b_ada, norm_g, w_in, b_gate, rel_table, b_forget, w_branch, w_out,
              w_up, conv_w, conv_b, w_down):
    S = x.shape[1]
    pos = jnp.arange(S, dtype=jnp.float32)
    inv_freq = ROPE_THETA ** (-jnp.arange(0, HEAD_DIM, 2, dtype=jnp.float32) / HEAD_DIM)
    ang = pos[:, None] * inv_freq[None, :]
    cos, sin = jnp.cos(ang), jnp.sin(ang)
    c_act = jax.nn.silu(c)
    for l in range(DEPTH):
        mod = (c_act @ w_ada[l] + b_ada[l])[:, None, :]
        sh1, sc1, g1, sh2, sc2, g2 = jnp.split(mod, 6, axis=-1)
        h = _rmsnorm(x, norm_g[l, 0]) * (1.0 + sc1) + sh1
        y = _hybrid_mixer(h, w_in[l], b_gate[l], rel_table[l], b_forget[l], w_branch[l], w_out[l], cos, sin)
        x = x + g1 * _rmsnorm(y, norm_g[l, 1])
        h = _rmsnorm(x, norm_g[l, 2]) * (1.0 + sc2) + sh2
        y = _conv_ffn(h, w_up[l], conv_w[l], conv_b[l], w_down[l])
        x = x + g2 * _rmsnorm(y, norm_g[l, 3])
    return x


DEPTH_2 = 2

N_A_LAYERS = (DEPTH_2 + 1) // 2
N_B_LAYERS = DEPTH_2 // 2
DEEPNORM_ALPHA = (2.0 * DEPTH_2) ** 0.25
DEEPNORM_BETA = (8.0 * DEPTH_2) ** -0.25
LN_EPS = 1e-5
RMS_EPS = 1e-5

GLA_HEADS = 4
GLA_DK_TOTAL = D_MODEL // 2
GLA_DV_TOTAL = D_MODEL
GLA_DK = GLA_DK_TOTAL // GLA_HEADS
GLA_DV = GLA_DV_TOTAL // GLA_HEADS
GLA_GATE_RANK = 16
GLA_GATE_TAU = 16.0
GLA_CHUNK = 64
GLA_IN = 2 * GLA_DK_TOTAL + 2 * GLA_DV_TOTAL + GLA_GATE_RANK

SWA_GROUPS = ((128, 1), (512, 4), (2048, 16))
SWA_N_GROUPS = len(SWA_GROUPS)
SWA_HEAD_DIM = 128
SWA_Q_HEADS = 8
SWA_KV_HEADS = 2
SWA_REP = SWA_Q_HEADS // SWA_KV_HEADS
SWA_OUT = SWA_Q_HEADS * SWA_HEAD_DIM
SWA_Q_TOTAL = SWA_N_GROUPS * SWA_OUT
SWA_IN = SWA_Q_TOTAL + SWA_OUT
SWA_KV_HALF = SWA_N_GROUPS * SWA_KV_HEADS * SWA_HEAD_DIM
SWA_KV_TOTAL = 2 * SWA_KV_HALF
SWA_BLOCK = 128


def layer_norm(x, g, b):
    x32 = x.astype(jnp.float32)
    mu = jnp.mean(x32, axis=-1, keepdims=True)
    xc = x32 - mu
    var = jnp.mean(xc * xc, axis=-1, keepdims=True)
    return (xc * lax.rsqrt(var + LN_EPS) * g.astype(jnp.float32) + b.astype(jnp.float32)).astype(x.dtype)

def rope(x, pos):
    e = x.shape[-1]
    half = e // 2
    inv = ROPE_THETA ** (-(jnp.arange(half, dtype=jnp.float32) * 2.0) / e)
    ang = pos.astype(jnp.float32)[:, None] * inv[None, :]
    cos = jnp.cos(ang)[None, :, None, :]
    sin = jnp.sin(ang)[None, :, None, :]
    x32 = x.astype(jnp.float32)
    x1, x2 = x32[..., :half], x32[..., half:]
    return jnp.concatenate([x1 * cos - x2 * sin, x2 * cos + x1 * sin], axis=-1)

def gla_chunked(q, k, v, log_a):
    bsz, s, h, dk = q.shape
    dv = v.shape[-1]
    c = GLA_CHUNK
    n = s // c

    def to_chunks(t):
        return t.reshape(bsz, n, c, h, t.shape[-1]).transpose(1, 0, 3, 2, 4)

    qc_all, kc_all, vc_all = to_chunks(q), to_chunks(k), to_chunks(v)
    b_all = jnp.cumsum(to_chunks(log_a), axis=3)
    causal = jnp.tril(jnp.ones((c, c), dtype=bool))[None, None, :, :, None]

    def step(state, inp):
        qc, kc, vc, bc = inp
        o_inter = jnp.einsum('bhcd,bhde->bhce', qc * jnp.exp(bc), state)
        diff = bc[:, :, :, None, :] - bc[:, :, None, :, :]
        decay = jnp.where(causal, jnp.exp(jnp.where(causal, diff, 0.0)), 0.0)
        att = jnp.einsum('bhid,bhjd,bhijd->bhij', qc, kc, decay)
        o_intra = jnp.einsum('bhij,bhje->bhie', att, vc)
        b_last = bc[:, :, -1:, :]
        new_state = jnp.exp(b_last[:, :, 0, :])[..., None] * state + \
            jnp.einsum('bhcd,bhce->bhde', kc * jnp.exp(b_last - bc), vc)
        return new_state, o_inter + o_intra

    state0 = jnp.zeros((bsz, h, dk, dv), dtype=jnp.float32)
    _, o = lax.scan(step, state0, (qc_all, kc_all, vc_all, b_all))
    return o.transpose(1, 0, 3, 2, 4).reshape(bsz, s, h, dv)

def gla_mixer(x, w_in, w_a2, b_a2, norm_g, w_out):
    bsz, s, _ = x.shape
    proj = x @ w_in
    q, k, v, g, a_lr = jnp.split(
        proj, [GLA_DK_TOTAL, 2 * GLA_DK_TOTAL, 2 * GLA_DK_TOTAL + GLA_DV_TOTAL,
               2 * GLA_DK_TOTAL + 2 * GLA_DV_TOTAL], axis=-1)
    q = q.astype(jnp.float32).reshape(bsz, s, GLA_HEADS, GLA_DK) * (GLA_DK ** -0.5)
    k = k.astype(jnp.float32).reshape(bsz, s, GLA_HEADS, GLA_DK)
    v = v.astype(jnp.float32).reshape(bsz, s, GLA_HEADS, GLA_DV)
    log_a = jax.nn.log_sigmoid((a_lr @ w_a2 + b_a2).astype(jnp.float32)) / GLA_GATE_TAU
    log_a = log_a.reshape(bsz, s, GLA_HEADS, GLA_DK)
    o = gla_chunked(q, k, v, log_a)
    o = o * lax.rsqrt(jnp.mean(o * o, axis=-1, keepdims=True) + RMS_EPS)
    o = o.reshape(bsz, s, GLA_DV_TOTAL) * norm_g.astype(jnp.float32)
    return (o.astype(x.dtype) * jax.nn.silu(g)) @ w_out

def shared_kv(x, w_kv):
    bsz, s, _ = x.shape
    pos = jnp.arange(s)
    kv = x @ w_kv
    k, v = jnp.split(kv, [SWA_KV_HALF], axis=-1)
    k = rope(k.reshape(bsz, s, SWA_N_GROUPS * SWA_KV_HEADS, SWA_HEAD_DIM), pos)
    k = k.reshape(bsz, s, SWA_N_GROUPS, SWA_KV_HEADS, SWA_HEAD_DIM)
    v = v.astype(jnp.float32).reshape(bsz, s, SWA_N_GROUPS, SWA_KV_HEADS, SWA_HEAD_DIM)
    return k, v

def dilated_window_attention(q, k, v, window, dilation):
    bsz, s, hq, e = q.shape
    hkv = k.shape[2]
    rep = hq // hkv
    blk = SWA_BLOCK
    w_sub = window // dilation
    span = dilation * blk
    seq_pad = -(-s // span) * span
    n_sub = seq_pad // dilation
    nb = n_sub // blk

    def to_strided(t):
        t = jnp.pad(t, ((0, 0), (0, seq_pad - s), (0, 0), (0, 0)))
        t = t.reshape(bsz, n_sub, dilation, t.shape[2], e).transpose(0, 2, 1, 3, 4)
        return t.reshape(bsz, dilation, nb, blk, t.shape[3], e)

    qb = to_strided(q).reshape(bsz, dilation, nb, blk, hkv, rep, e)
    kb, vb = to_strided(k), to_strided(v)

    def with_prev(t):
        prev = jnp.pad(t, ((0, 0), (0, 0), (1, 0), (0, 0), (0, 0), (0, 0)))[:, :, :-1]
        return jnp.concatenate([prev, t], axis=3)

    kcat, vcat = with_prev(kb), with_prev(vb)
    scores = jnp.einsum('brnqgpe,brnkge->brngpqk', qb, kcat)
    qi = jnp.arange(blk)[:, None]
    kj = jnp.arange(2 * blk)[None, :]
    rel = blk + qi - kj
    band = (rel >= 0) & (rel <= w_sub)
    mask = band[None] & ((jnp.arange(nb)[:, None, None] > 0) | (kj[None] >= blk))
    scores = jnp.where(mask[None, None, :, None, None], scores, -jnp.inf)
    m = jnp.max(scores, axis=-1, keepdims=True)
    p = jnp.exp(scores - m)
    den = jnp.sum(p, axis=-1)
    o = jnp.einsum('brngpqk,brnkge->brnqgpe', p, vcat) / jnp.moveaxis(den, -1, 3)[..., None]
    lse = jnp.moveaxis(m[..., 0] + jnp.log(den), -1, 3)

    def from_strided(t):
        t = t.reshape((bsz, dilation, n_sub) + t.shape[6 - 2 + 1:] if False else (bsz, dilation, n_sub, -1))
        return t

    o = o.reshape(bsz, dilation, n_sub, hq, e).transpose(0, 2, 1, 3, 4).reshape(bsz, seq_pad, hq, e)[:, :s]
    lse = lse.reshape(bsz, dilation, n_sub, hq).transpose(0, 2, 1, 3).reshape(bsz, seq_pad, hq)[:, :s]
    return o, lse

def dilated_mixer(x, w_in, w_out, k_sh, v_sh):
    bsz, s, _ = x.shape
    pos = jnp.arange(s)
    proj = x @ w_in
    q, g = jnp.split(proj, [SWA_Q_TOTAL], axis=-1)
    q = rope(q.reshape(bsz, s, SWA_N_GROUPS * SWA_Q_HEADS, SWA_HEAD_DIM), pos) * (SWA_HEAD_DIM ** -0.5)
    q = q.reshape(bsz, s, SWA_N_GROUPS, SWA_Q_HEADS, SWA_HEAD_DIM)
    outs, lses = [], []
    for gi, (window, dilation) in enumerate(SWA_GROUPS):
        o_g, lse_g = dilated_window_attention(q[:, :, gi], k_sh[:, :, gi], v_sh[:, :, gi], window, dilation)
        outs.append(o_g)
        lses.append(lse_g)
    wts = jax.nn.softmax(jnp.stack(lses, axis=0), axis=0)
    o = jnp.sum(wts[..., None] * jnp.stack(outs, axis=0), axis=0)
    o = o.reshape(bsz, s, SWA_OUT)
    return (o.astype(x.dtype) * jax.nn.silu(g)) @ w_out

def second_inputs(seed: int = 0) -> dict:
    key = jax.random.key(seed)
    ks = jax.random.split(key, 12)
    f32 = jnp.float32
    x = jax.random.normal(ks[0], (BATCH, SEQ, D_MODEL), f32)
    gla_w_in = jax.random.normal(ks[1], (N_A_LAYERS, D_MODEL, GLA_IN), f32) * D_MODEL ** -0.5
    gla_w_a2 = jax.random.normal(ks[2], (N_A_LAYERS, GLA_GATE_RANK, GLA_DK_TOTAL), f32) * GLA_GATE_RANK ** -0.5
    gla_b_a2 = jax.random.normal(ks[3], (N_A_LAYERS, GLA_DK_TOTAL), f32) * 0.1
    gla_norm_g = 1.0 + 0.02 * jax.random.normal(ks[4], (N_A_LAYERS, GLA_DV_TOTAL), f32)
    gla_w_out = jax.random.normal(ks[5], (N_A_LAYERS, GLA_DV_TOTAL, D_MODEL), f32) * (GLA_DV_TOTAL ** -0.5 * DEEPNORM_BETA)
    w_kv = jax.random.normal(ks[6], (D_MODEL, SWA_KV_TOTAL), f32) * D_MODEL ** -0.5
    swa_w_in = jax.random.normal(ks[7], (N_B_LAYERS, D_MODEL, SWA_IN), f32) * D_MODEL ** -0.5
    swa_w_out = jax.random.normal(ks[8], (N_B_LAYERS, SWA_OUT, D_MODEL), f32) * (SWA_OUT ** -0.5 * DEEPNORM_BETA)
    ln_g = 1.0 + 0.02 * jax.random.normal(ks[9], (DEPTH_2, D_MODEL), f32)
    ln_b = 0.02 * jax.random.normal(ks[10], (DEPTH_2, D_MODEL), f32)
    return {"x": x, "gla_w_in": gla_w_in, "gla_w_a2": gla_w_a2, "gla_b_a2": gla_b_a2,
            "gla_norm_g": gla_norm_g, "gla_w_out": gla_w_out, "w_kv": w_kv,
            "swa_w_in": swa_w_in, "swa_w_out": swa_w_out, "ln_g": ln_g, "ln_b": ln_b}

def second_block(x, gla_w_in, gla_w_a2, gla_b_a2, gla_norm_g, gla_w_out, w_kv,
              swa_w_in, swa_w_out, ln_g, ln_b):
    k_sh = None
    v_sh = None
    for layer in range(DEPTH_2):
        if layer < N_A_LAYERS:
            y = gla_mixer(x, gla_w_in[layer], gla_w_a2[layer], gla_b_a2[layer],
                          gla_norm_g[layer], gla_w_out[layer])
        else:
            if layer == N_A_LAYERS:
                k_sh, v_sh = shared_kv(x, w_kv)
            i = layer - N_A_LAYERS
            y = dilated_mixer(x, swa_w_in[i], swa_w_out[i], k_sh, v_sh)
        x = layer_norm(DEEPNORM_ALPHA * x + y, ln_g[layer], ln_b[layer])
    return x


def setup_inputs(seed=0):
    out = dict(first_inputs(seed))
    for name, value in second_inputs(seed + 1).items():
        if name != "x":
            out[name + "_2"] = value
    return out


def reference(
    x, c, w_ada, b_ada, norm_g, w_in, b_gate, rel_table, b_forget, w_branch, w_out, w_up,
    conv_w, conv_b, w_down, gla_w_in_2, gla_w_a2_2, gla_b_a2_2, gla_norm_g_2, gla_w_out_2,
    w_kv_2, swa_w_in_2, swa_w_out_2, ln_g_2, ln_b_2,
):
    x = first_block(
        x, c, w_ada, b_ada, norm_g, w_in, b_gate, rel_table, b_forget, w_branch, w_out, w_up,
        conv_w, conv_b, w_down,
    )
    return second_block(
        x, gla_w_in_2, gla_w_a2_2, gla_b_a2_2, gla_norm_g_2, gla_w_out_2, w_kv_2, swa_w_in_2,
        swa_w_out_2, ln_g_2, ln_b_2,
    )


_drawn_inputs = setup_inputs


def setup_inputs(seed=0):
    import zlib

    import numpy as np

    out = dict(_drawn_inputs(seed))
    spreads = {}
    factors = {'b_gate': 8.0, 'rel_table': 2.719, 'conv_b': 8.0, 'gla_b_a2_2': 4.975, 'gla_norm_g_2': 8.0}
    for name, (base, spread) in spreads.items():
        noise = np.random.default_rng([zlib.crc32(name.encode()), seed]).standard_normal(out[name].shape)
        drawn = base * np.exp(spread * noise) if base else spread * noise
        out[name] = __import__('jax').numpy.asarray(drawn.astype(out[name].dtype))
    for name, factor in factors.items():
        out[name] = (out[name] * factor).astype(out[name].dtype)
    return out
```

```python
import concourse.bass as bass
from concourse import mybir
from contextlib import ExitStack

D, T, P = 1024, 256, 128
KT = D // P
D_FF = 2816
FT = D_FF // P
NEG = -1.0e30
TAKEN = -3.0e38
ALPHA = 4.0 ** 0.25
RAW, SPL, NB = 4, 3, 3
CW = 2048

COLS = {}
_at = 0
for _n, _w in (("c", 8), ("b_ada", 48), ("norm_g", 32), ("b_gate", 24), ("conv_w", 66), ("conv_b", 22),
               ("b_a2", 4), ("gla_g", 8), ("ln_g", 16), ("ln_b", 16), ("b_forget", 1), ("eps6", 1), ("eps5", 1)):
    COLS[_n] = (_at, _at + _w)
    _at += _w
NCOL = _at

QC, QI, KK, MISC, QA, KA, VA, QB, KB, VB = range(10)
ZG = 10
BRANCH = ZG + 12
WOUT = BRANCH + 3
UP = WOUT + 4
DOWN = UP + 22
GQ = DOWN + 12
GK = GQ + 2
GA = GK + 2
GV = GA + 1
GG = GV + 4
GOUT = GG + 4
SK = GOUT + 4
SV = SK + 3
SWA = SV + 3
SOUT = SWA + 16
NC = SOUT + 4
MW = 72
NADA = 24
ADA_STEPS = [0, 1, 2, 3, 4, 5, 6, 6, 7, 8, 8, 9] + list(range(10, 22)) + [UP + 2 + 3 * i + j for i in range(4) for j in range(2)]
ADA_START = {8 + i: ADA_STEPS[2 * i] for i in range(16)}
ADA_END = {8 + i: ADA_STEPS[2 * i + 1] for i in range(16)}
ADA_USE = {ADA_END[a + 1] + 3: a for a in range(8, 24, 2)}
ADA_AT = {8: 0, 9: 1, 10: 2, 11: 0, 12: 1, 13: 2, 14: 1, 15: "sq", 16: "y", 17: "sq", 18: "y", 19: "sq",
          20: "y", 21: "sq", 22: "y", 23: "sq"}


def kt_of(c):
    if c == MISC:
        return KT, MW
    if c == GA:
        return KT, 16
    if BRANCH <= c < WOUT:
        return 2, 1024
    if DOWN <= c < GQ:
        return (8, 8, 6)[(c - DOWN) % 3], 256
    return KT, 256


def results_of(c):
    if BRANCH <= c < WOUT:
        return 4
    if DOWN <= c < GQ:
        return 2 if (c - DOWN) % 3 == 2 else 0
    return 1


def drainer_of(c):
    if c < MISC or BRANCH <= c < WOUT or (UP <= c < DOWN and (c - UP) % 2 == 1):
        return "dve"
    if GOUT <= c < SV or c >= SOUT or (SWA <= c < SOUT and (c - SWA) % 4 != 3):
        return "dve"
    return "act"


CHUNK_MARK, FIRST_RESULT, RESULT_MARK, RESULT_DRAIN = [], [], [], []
_m, _n = 0, {"act": 0, "dve": 0}
for _c in range(NC):
    FIRST_RESULT.append(len(RESULT_MARK))
    for _i in range(results_of(_c)):
        _m += 1
        RESULT_MARK.append(_m)
        _n[drainer_of(_c)] += 1
        RESULT_DRAIN.append((drainer_of(_c), _n[drainer_of(_c)]))
    if not results_of(_c):
        _m += 1
    CHUNK_MARK.append(_m)

STREAM = [("ada", a) for a in range(8)]
for _c in range(NC):
    STREAM.append(("w", _c))
    STREAM += [("ada", _a) for _a in range(8, NADA) if ADA_START[_a] + 2 == _c]
RING = [e for e in STREAM if e[0] == "w" or e[1] < 8]
RAW_OF = {e: i for i, e in enumerate(RING)}


def pieces(c, W):
    w_in, w_branch, w_out, w_up, w_down, gla_in, gla_out, w_kv, swa_in, swa_out = W

    def cols(m, a, n):
        return m[:, a:a + n].rearrange("(k p) n -> p k n", p=P)

    if c == QC:
        return [(0, cols(w_in, 1540, 256))]
    if c == QI:
        return [(0, cols(w_in, 1924, 256))]
    if c == KK:
        return [(0, cols(w_in, 1796, 64)), (64, cols(w_in, 1796, 64)),
                (128, cols(w_in, 2180, 64)), (192, cols(w_in, 2180, 64))]
    if c == MISC:
        return [(0, cols(w_in, 1860, 64)), (64, cols(w_in, 1536, 4)), (68, cols(w_in, 2244, 4))]
    if c < ZG:
        return [(0, cols(w_in, 256 * (c - QA), 256))]
    if c < BRANCH:
        return [(0, cols(w_in, 2248 + 256 * (c - ZG), 256))]
    if c < WOUT:
        return [(0, cols(w_branch[c - BRANCH], 0, 1024))]
    if c < UP:
        return [(0, cols(w_out, 256 * (c - WOUT), 256))]
    if c < DOWN:
        j, g = (c - UP) // 2, (c - UP) % 2
        return [(0, cols(w_up, D_FF * g + 256 * j, 256))]
    if c < GQ:
        j, kg = (c - DOWN) // 3, (c - DOWN) % 3
        kt = kt_of(c)[0]
        return [(0, w_down[kg * 8 * P:(kg * 8 + kt) * P, 256 * j:256 * j + 256]
                 .rearrange("(k p) n -> p k n", p=P))]
    if c < GA:
        return [(0, cols(gla_in, 256 * (c - GQ), 256))]
    if c == GA:
        return [(0, cols(gla_in, 3072, 16))]
    if c < GOUT:
        return [(0, cols(gla_in, 1024 + 256 * (c - GV), 256))]
    if c < SK:
        return [(0, cols(gla_out, 256 * (c - GOUT), 256))]
    if c < SWA:
        return [(0, cols(w_kv, 256 * (c - SK), 256))]
    if c < SOUT:
        pair, g = (c - SWA) // 4, (c - SWA) % 4
        return [(0, cols(swa_in, 1024 * g + 256 * pair, 256))]
    return [(0, cols(swa_out, 256 * (c - SOUT), 256))]


def build(nc, xT, cols_d, ident_d, rope1_d, rope2_d, amask_d, cmask_d, tri_d, dmask_d, sel_d, rel_d, w_a2_d,
          w_ada, w_in, w_branch, w_out, w_up, w_down, gla_in, gla_out, w_kv, swa_in, swa_out, out_d):
    f32, f32r = mybir.dt.float32, mybir.dt.float32r
    ALU, ACT = mybir.AluOpType, mybir.ActivationFunctionType
    W = (w_in, w_branch, w_out, w_up, w_down, gla_in, gla_out, w_kv, swa_in, swa_out)
    ctx = ExitStack()
    with ctx:
        def sb(name, shape, dt=f32, at=ctx):
            return at.enter_context(nc.sbuf_tensor(name, shape, dt))

        def sem(name):
            return ctx.enter_context(nc.semaphore(name))

        raw = [sb(f"raw{i}", [P, CW]) for i in range(RAW)]
        whi = [sb(f"whi{i}", [P, CW], f32r) for i in range(SPL)]
        wlo = [sb(f"wlo{i}", [P, CW], f32r) for i in range(SPL)]
        hhi = sb("hhi", [P, KT, T], f32r)
        hlo = sb("hlo", [P, KT, T], f32r)
        x = sb("x", [P, KT, T])
        y = sb("y", [P, KT, T])
        sq = sb("sq", [P, KT, T])
        tb = sb("tb", [P, KT, T])
        cols = sb("cols", [P, NCOL])
        ident = sb("ident", [P, P])
        meanw = sb("meanw", [P, P])
        headw = sb("headw", [P, P])
        mod = sb("mod", [P, 48])
        cact = sb("cact", [P, 8])
        ones = sb("ones", [P, 1])
        one = sb("one", [P, 1])
        adasum = sb("adasum", [P, 4, T])
        pcol = sb("pcol", [P, 4, 8])
        bgh = sb("bgh", [P, 24])
        ggh = sb("ggh", [P, 8])
        rstd = sb("rstd", [P, T])
        logvar = sb("logvar", [P, T])

        with ExitStack() as st:
            gates = sb("gates", [P, 24, T], at=st)
            qkv = {n: sb(f"m_{n}", [P, 2, T], at=st) for n in ("qa", "ka", "va", "qb", "kb", "vb", "qc", "qi", "kk")}
            misc = sb("misc", [P, 2, MW], at=st)
            wis = sb("wis", [P, 2, 4], at=st)
            rope1 = sb("rope1", [P, 2, T], at=st)
            amask = sb("amask", [P, 384], at=st)
            cmask = sb("cmask", [P, 384], at=st)
            sel = sb("sel", [4, 512], at=st)
            biasA = sb("biasA", [P, 4, 384], at=st)
            best8 = sb("best8", [P, 8], at=st)
            usc = sb("usc", [P, 2, T], at=st)
            up = sb("up", [P, 3, T], at=st)
            upT = sb("upT", [P, 2, T], at=st)
            unmax = sb("unmax", [P, 4], at=st)
            uden = sb("uden", [P, 4], at=st)
            urec = sb("urec", [P, 4], at=st)
            yhi = sb("yhi", [P, 3, 512], f32r, at=st)
            ylo = sb("ylo", [P, 3, 512], f32r, at=st)
        biasB = tb[:, 0:6, :].rearrange("p a b -> p (a b)").rearrange("p (h n) -> p h n", h=4)
        biasC = tb[:, 6:8, :].rearrange("p a b -> p (a b)")[:, 0:384]
        xsw = sq[:, 0:2, :]
        relu = sq[:, 2:4, :]
        left = sq[:, 4:6, :]
        score = sq[:, 6:8, :].rearrange("p a b -> p (a b)")[:, 0:384]
        gtmp = sq[:, 0:4, :].rearrange("p a b -> p (a b)").rearrange("p (r n) -> p r n", r=2)
        fgate = y[0:4, 0:5, :]
        fones = y[0:4, 5, :]

        with ExitStack() as st:
            uhi = sb("uhi", [P, FT, T], f32r, at=st)
            ulo = sb("ulo", [P, FT, T], f32r, at=st)
            aseq = sb("aseq", [P, 2, 2, T + 2], at=st)
            conv = sb("conv", [P, 2, 2, T], at=st)
            gelu = sb("gelu", [P, 2, 2, T], at=st)

        with ExitStack() as st:
            gq = sb("gq", [P, 4, T], at=st)
            gk = sb("gk", [P, 4, T], at=st)
            alrT = sb("alrT", [16, T], at=st)
            alr = sb("alr", [P, 2, 16], at=st)
            wa2 = sb("wa2", [16, 512], at=st)
            keep = sb("keep", [P, 1024], at=st)
            cum = sb("cum", [P, 1024], at=st)
            ekI = sb("ekI", [P, 2560], at=st)
            qI = sb("qI", [P, 1024], at=st)
            qdec = sb("qdec", [P, 1024], at=st)
            kdec = sb("kdec", [P, 1024], at=st)
            kdT = sb("kdT", [P, 2, 4, P], at=st)
            elast = sb("elast", [P, 16], at=st)
            gv = sb("gv", [P, 2, 1024], at=st)
            gs = sb("gs", [P, KT, T], at=st)
            tri = sb("tri", [P, 64], at=st)
            att = sb("att", [P, 4, 4, 64], at=st)
            state = sb("state", [P, 4, T], at=st)
            gth = sb("gth", [P, 512], at=st)
            grs = ekI[:, 0:1024].rearrange("p (h t) -> p h t", h=4)
        glz = sq[:, 0:4, :].rearrange("p a b -> p (a b)")
        gla = sq[:, 4:8, :].rearrange("p a b -> p (a b)")
        gdf = tb[:, 0:4, :].rearrange("p a b -> p (a b)")
        gdg = tb[:, 4:8, :].rearrange("p a b -> p (a b)")

        with ExitStack() as st:
            sk = sb("sk", [P, 6, T], at=st)
            sv = sb("sv", [P, 2, 768], at=st)
            sqr = sb("sqr", [P, 2, 6, T], at=st)
            sgs = sb("sgs", [P, 2, 2, T], at=st)
            sth = sb("sth", [P, 512], at=st)
            dmask = sb("dmask", [P, 1152], at=st)
            rope2 = sb("rope2", [P, 2, T], at=st)
            dsc = sb("dsc", [P, 2, 768], at=st)
            dp = sb("dp", [P, 2, 768], at=st)
            dpT = sb("dpT", [P, 2, 768], at=st)
            dnmax = sb("dnmax", [P, 4], at=st)
            dden = sb("dden", [P, 4], at=st)
            drec = sb("drec", [P, 4], at=st)
            of = sb("of", [P, 2, P], at=st)
            ohi = sb("ohi", [P, KT, T], f32r, at=st)
            olo = sb("olo", [P, KT, T], f32r, at=st)

        res = [ctx.enter_context(nc.psum_tensor(f"res{i}", [P, 512], f32)) for i in range(NB)]
        pS = ctx.enter_context(nc.psum_tensor("pS", [P, 1024], f32))
        pT = ctx.enter_context(nc.psum_tensor("pT", [P, 1024], f32))
        pX = ctx.enter_context(nc.psum_tensor("pX", [P, 512], f32))
        stat = pX[:, 0:T]
        pmod = pX[:, T:T + 48]
        pO = pT[:, 512:1024]

        raw_full = [sem(f"raw_full{i}") for i in range(RAW)]
        hi_ready, lo_dve, lo_pool = sem("hi_ready"), sem("lo_dve"), sem("lo_pool")
        product_done, drained_act, drained_dve = sem("product_done"), sem("drained_act"), sem("drained_dve")
        drained = {"act": drained_act, "dve": drained_dve}
        ada_full = [sem(f"ada_full{i}") for i in range(3)]
        ada_summed, ada_pooled, ada_used, mod_ready = (
            sem(n) for n in ("ada_summed", "ada_pooled", "ada_used", "mod_ready"))
        x_in, const_in, mixc_in, glac_in, swac_in = (sem(n) for n in ("x_in", "const_in", "mixc_in", "glac_in", "swac_in"))
        const_set, cact_ready, cact_th = sem("const_set"), sem("cact_ready"), sem("cact_th")
        dve_self, act_self, pool_self = sem("dve_self"), sem("act_self"), sem("pool_self")
        NORMS = ("n1", "n2", "n3", "n4", "n5", "n6")
        squares = {n: sem(f"{n}_squares") for n in NORMS}
        mean_known = {n: sem(f"{n}_mean") for n in NORMS}
        dev_known = {n: sem(f"{n}_dev") for n in NORMS}
        rstd_known = {n: sem(f"{n}_rstd") for n in NORMS}
        scaled = {n: sem(f"{n}_scaled") for n in NORMS}
        in_hi = {n: sem(f"{n}_hi") for n in NORMS}
        in_lo = {n: sem(f"{n}_lo") for n in NORMS}
        centered = {n: sem(f"{n}_centered") for n in ("n5", "n6")}
        summed = {n: sem(f"{n}_summed") for n in ("n5", "n6")}
        moved_half = sem("moved_half")
        sin_done = sem("sin_done")
        roped = sem("roped")
        evac = sem("evac")
        wis_ready = sem("wis_ready")
        idx_done, idx_relu, idx_acc = sem("idx_done"), sem("idx_relu"), sem("idx_acc")
        fT_done, fz_ready, flog_ready, fcum_ready = sem("fT_done"), sem("fz_ready"), sem("flog_ready"), sem("fcum_ready")
        bB_done, bB_ready = sem("bB_done"), sem("bB_ready")
        qk_done, smax_done, exp_done, norm_done = sem("qk_done"), sem("smax_done"), sem("exp_done"), sem("norm_done")
        tr_done, pT_ready, pv_done, y_hi, y_lo = sem("tr_done"), sem("pT_ready"), sem("pv_done"), sem("y_hi"), sem("y_lo")
        gated, merged, mg_hi, mg_lo = sem("gated"), sem("merged"), sem("mg_hi"), sem("mg_lo")
        a_ready, conv_done, gelu_done, u_full, u_hi, u_lo = (
            sem(n) for n in ("a_ready", "conv_done", "gelu_done", "u_full", "u_hi", "u_lo"))
        g_evac, alr_T, alrT_ready, la_done, z_ready, loga_ready, cum_ready = (
            sem(n) for n in ("g_evac", "alr_T", "alrT_ready", "la_done", "z_ready", "loga_ready", "cum_ready"))
        gdiff, gexp, gfac, kd_T, kdT_ready, att_done, att_ready = (
            sem(n) for n in ("gdiff", "gexp", "gfac", "kd_T", "kdT_ready", "att_done", "att_ready"))
        o_done, o_ready, upd_done, state_ready, osq, hmean, hdev, hrstd, gs_ready, gth_ready = (
            sem(n) for n in ("o_done", "o_ready", "upd_done", "state_ready", "osq", "hmean", "hdev", "hrstd", "gs_ready", "gth_ready"))
        go_hi, go_lo, go_full = sem("go_hi"), sem("go_lo"), sem("go_full")
        sv_ready, sg_ready, sth_ready = sem("sv_ready"), sem("sg_ready"), sem("sth_ready")
        d_qk, d_max, d_exp, d_norm, d_tr, d_pT, d_pv, d_of, d_hi, d_lo = (
            sem(f"d_{n}") for n in ("qk", "max", "exp", "norm", "tr", "pT", "pv", "of", "hi", "lo"))
        out_ready, out_stored = sem("out_ready"), sem("out_stored")
        pad_set = sem("pad_set")

        block = ctx.enter_context(nc.Block())

        def col(name, k, n=1):
            a = COLS[name][0] + k
            return cols[:, a:a + n]

        def wait_raw(eng, e):
            i = RAW_OF[e]
            n = sum(16 * (len(pieces(RING[j][1], W)) if RING[j][0] == "w" else 1)
                    for j in range(i % RAW, i + 1, RAW))
            eng.wait_ge(raw_full[i % RAW], n)

        def ada_buffer(a):
            at = ADA_AT[a]
            return (y if at == "y" else sq if at == "sq" else gates[:, 8 * at:8 * at + 8, :]
                    )[:, :, :].rearrange("p a b -> p (a b)")

        @block.sync
        def _(sp):
            sp.dma_start(cols[:, :], cols_d).then_inc(const_in, 16)
            sp.dma_start(ident[:, :], ident_d).then_inc(const_in, 16)
            for kind, n in STREAM:
                if kind == "ada" and n >= 8:
                    if n >= 11:
                        sp.wait_ge(ada_pooled, n - 10 if n < 14 else n - 9)
                    if n == 15:
                        sp.wait_ge(bB_ready, 4)
                    if n == 16:
                        sp.wait_ge(bB_done, 4)
                    if n == 20:
                        sp.wait_ge(scaled["n2"], KT)
                    if n == 21:
                        sp.wait_ge(mean_known["n3"], 1)
                    sp.dma_start(ada_buffer(n).rearrange("p (k n) -> p k n", k=KT),
                                 w_ada[:, 256 * n:256 * n + 256].rearrange("(k p) n -> p k n", p=P)
                                 ).then_inc(ada_full[n % 3], 16)
                    continue
                i = RAW_OF[kind, n]
                if i == 2:
                    for k in range(0, KT, 4):
                        sp.dma_start(x[:, k:k + 4, :], xT[:, k:k + 4, :]).then_inc(x_in, 16)
                if i >= RAW:
                    before, m = RING[i - RAW]
                    if before == "ada":
                        sp.wait_ge(ada_used, m + 1)
                    else:
                        sp.wait_ge(lo_dve, m + 1)
                        sp.wait_ge(lo_pool, m + 1)
                dst = raw[i % RAW]
                if kind == "ada":
                    sp.dma_start(dst[:, :].rearrange("p (k n) -> p k n", k=KT),
                                 w_ada[:, 256 * n:256 * n + 256].rearrange("(k p) n -> p k n", p=P)
                                 ).then_inc(raw_full[i % RAW], 16)
                else:
                    kt, w = kt_of(n)
                    view = dst[:, 0:kt * w].rearrange("p (k n) -> p k n", k=kt)
                    for at, src in pieces(n, W):
                        sp.dma_start(view[:, :, at:at + src.shape[2]], src).then_inc(raw_full[i % RAW], 16)
            for k in range(KT // 2):
                sp.wait_ge(out_ready, k + 1)
                sp.dma_start(out_d[:, 2 * k:2 * k + 2, :], x[:, 2 * k:2 * k + 2, :]).then_inc(out_stored, 16)
            sp.wait_ge(out_stored, 16 * (KT // 2))

        def dve_part(c):
            kt, w = kt_of(c)
            if c < WOUT:
                return kt * w * 7 // 8 // 2 * 2
            return kt * w * 3 // 4 // 2 * 2

        @block.gpsimd
        def _(pool):
            pool_count = [0]

            def own(ins):
                ins.then_inc(pool_self, 1)
                pool_count[0] += 1
                pool.wait_ge(pool_self, pool_count[0])

            def low(c):
                if c >= NC:
                    return
                kt, w = kt_of(c)
                a, b = dve_part(c), kt * w
                pool.wait_ge(hi_ready, c + 1)
                if c >= SPL:
                    pool.wait_ge(product_done, CHUNK_MARK[c - SPL])
                nc.gpsimd.tensor_tensor(wlo[c % SPL][:, a:b], raw[RAW_OF["w", c] % RAW][:, a:b],
                                        whi[c % SPL][:, a:b].bitcast(f32), ALU.subtract).then_inc(lo_pool, 1)

            rope_n = [0]

            def sine(c, table):
                pool.wait_ge(moved_half, RH[c])
                nc.gpsimd.tensor_tensor(xsw, xsw, table[:, 1:2, :].to_broadcast([P, 2, T]), ALU.mult).then_inc(sin_done, 1)

            def ada_half(a, second):
                r = ada_buffer(a)
                w = r.rearrange("p (k n) -> p k n", k=KT)
                if not second:
                    pool.wait_ge(ada_full[a % 3], 16 * ((a - 8) // 3 + 1))
                    own(nc.gpsimd.tensor_tensor(w, w, cact[:, :, None].to_broadcast([P, KT, T]), ALU.mult))
                    return
                own(nc.gpsimd.tensor_tensor(r[:, 0:1024], r[:, 0:1024], r[:, 1024:2048], ALU.add))
                own(nc.gpsimd.tensor_tensor(r[:, 0:512], r[:, 0:512], r[:, 512:1024], ALU.add))
                if a >= 12:
                    pool.wait_ge(ada_used, a - 3)
                nc.gpsimd.tensor_tensor(adasum[:, a % 4, :], r[:, 0:256], r[:, 256:512], ALU.add).then_inc(ada_pooled, 1)

            nc.gpsimd.memset(meanw[:, :], 1.0 / D).then_inc(const_set, 1)
            nc.gpsimd.memset(headw[:, :], 1.0 / 256).then_inc(const_set, 1)
            nc.gpsimd.memset(ones[:, :], 1.0).then_inc(const_set, 1)
            for dst, src in ((rope1[:, :, :], rope1_d), (amask[:, :], amask_d), (cmask[:, :], cmask_d),
                             (sel[:, :], sel_d), (biasA[:, :, :], rel_d)):
                pool.dma_start(dst, src).then_inc(mixc_in, 16)
            pool.wait_ge(mixc_in, 80)
            for c in range(SPL):
                low(c)
            for c in range(1, NC + 1):
                if BRANCH < c - 1 < WOUT:
                    for j in range(4):
                        n = 4 * (c - 1 - BRANCH) + j
                        pool.wait_ge(gated, n + 1)
                        nc.gpsimd.tensor_tensor(y[:, 2 * j:2 * j + 2, :], y[:, 2 * j:2 * j + 2, :],
                                                gtmp[:, n % 2, :].rearrange("p (a b) -> p a b", a=2), ALU.add
                                                ).then_inc(merged, 1)
                for i, step in enumerate(ADA_STEPS):
                    if step == c - 1:
                        ada_half(8 + i // 2, i % 2)
                low(c + 2)
                if c - 1 <= KK:
                    sine(c - 1, rope1)
                if c - 1 == UP - 1:
                    pool.wait_ge(product_done, CHUNK_MARK[UP - 1])
                    nc.gpsimd.memset(aseq[:, :, :, 0:2], 0.0).then_inc(pad_set, 1)
                if c - 1 == GQ - 1:
                    pool.wait_ge(product_done, CHUNK_MARK[GQ - 1])
                    pool.dma_start(wa2[:, :], w_a2_d).then_inc(glac_in, 16)
                    pool.dma_start(tri[:, :], tri_d).then_inc(glac_in, 16)
                    own(nc.gpsimd.memset(keep[:, :], 1.0))
                    nc.gpsimd.memset(keep[:, :].rearrange("p (n c) -> p n c", c=64)[:, :, 0:1], 0.0).then_inc(pad_set, 1)
                    nc.gpsimd.memset(att[:, :, :, :], 0.0).then_inc(pad_set, 1)
                if c - 1 == SK - 1:
                    pool.wait_ge(product_done, CHUNK_MARK[SK - 1])
                    pool.dma_start(rope2[:, :, :], rope2_d).then_inc(swac_in, 16)
                    pool.dma_start(dmask[:, :], dmask_d).then_inc(swac_in, 16)
                    pool.wait_ge(swac_in, 32)
                if c - 1 in RH and c - 1 > KK:
                    sine(c - 1, rope2)

        @block.scalar
        def _(act):
            act_count = [0]

            def own(ins):
                ins.then_inc(act_self, 1)
                act_count[0] += 1
                act.wait_ge(act_self, act_count[0])

            def high(c):
                if c >= NC:
                    return
                kt, w = kt_of(c)
                wait_raw(act, ("w", c))
                if c >= SPL:
                    act.wait_ge(product_done, CHUNK_MARK[c - SPL])
                    act.wait_ge(lo_pool, c - SPL + 1)
                    act.wait_ge(lo_dve, c - SPL + 1)
                nc.scalar.activation(whi[c % SPL][:, 0:kt * w], raw[RAW_OF["w", c] % RAW][:, 0:kt * w],
                                     ACT.Copy).then_inc(hi_ready, 1)

            def result(r):
                act.wait_ge(product_done, RESULT_MARK[r])
                return res[r % NB]

            def swap(c, block_rows):
                ps = result(FIRST_RESULT[c])
                if RI[c] > 0:
                    act.wait_ge(roped, RI[c])
                n = P // block_rows
                for i in range(n):
                    a, b = i * block_rows, (i ^ 1) * block_rows
                    nc.scalar.activation(xsw[a:a + block_rows, :, :].rearrange("p a b -> p (a b)"),
                                         ps[b:b + block_rows, :], ACT.Copy).then_inc(moved_half, 1)

            def norm_dev(n, eps):
                own(nc.scalar.activation(one[:, :], col("eps5", 0), ACT.Ln))
                act.wait_ge(mean_known[n], 2 if n in centered else 1)
                nc.scalar.activation(logvar[:, :], stat, ACT.Ln, bias=col(eps, 0)).then_inc(dev_known[n], 1)
                act.wait_ge(dev_known[n], 1)
                nc.scalar.activation(rstd[:, :], logvar[:, :], ACT.Exp, scale=-0.5).then_inc(rstd_known[n], 1)

            def split_hi(n, src, bias=None, first=0):
                for k in range(KT):
                    act.wait_ge(scaled[n], first + k + 1)
                    if bias is None:
                        nc.scalar.activation(hhi[:, k, :], src[:, k, :], ACT.Copy).then_inc(in_hi[n], 1)
                    else:
                        nc.scalar.activation(hhi[:, k, :], src[:, k, :], ACT.Identity, bias=bias(k)).then_inc(in_hi[n], 1)

            act.wait_ge(const_in, 32)
            nc.scalar.activation(cact[:, :], col("c", 0, 8), ACT.Silu).then_inc(cact_ready, 1)
            act.wait_ge(x_in, 32)
            for k in range(KT):
                nc.scalar.activation(sq[:, k, :], x[:, k, :], ACT.Square).then_inc(squares["n1"], 1)
            norm_dev("n1", "eps6")
            high(0)
            split_hi("n1", tb, lambda k: mod[:, k:k + 1])
            for c in range(1, SPL):
                high(c)

            TAIL = 3
            for c in range(1, NC + 1):
                high(c + 2)
                b = c - 1
                if b <= KK:
                    swap(b, 32)
                elif b < ZG:
                    ps = result(FIRST_RESULT[b])
                    if b == MISC:
                        for t in range(2):
                            nc.scalar.activation(misc[:, t, :], ps[:, t * 256:t * 256 + MW], ACT.Copy
                                                 ).then_inc(drained_act if t else act_self, 1)
                        act_count[0] += 1
                    else:
                        dst = qkv[("qa", "ka", "va", "qb", "kb", "vb")[b - QA]]
                        nc.scalar.activation(dst[:, :, :].rearrange("p a b -> p (a b)"), ps[:, :], ACT.Copy
                                             ).then_inc(drained_act, 1)
                    if QA <= b < QA + 4:
                        for e in (2 * (b - QA), 2 * (b - QA) + 1):
                            nk = P * (e // 4 + 1)
                            act.wait_ge(idx_done, e + 1)
                            if e == 0:
                                act.wait_ge(roped, 3)
                            if e >= 2:
                                act.wait_ge(idx_acc, e - 1)
                            nc.scalar.activation(relu[:, e % 2, 0:nk], pS[:, 512 * (e % 2):512 * (e % 2) + nk],
                                                 ACT.Relu, scale=0.125).then_inc(idx_relu, 1)
                    if b == VA:
                        act.wait_ge(fz_ready, 1)
                        own(nc.scalar.activation(fgate[:, 1, :], fgate[:, 0, :], ACT.Abs))
                        own(nc.scalar.activation(fgate[:, 2, :], fgate[:, 1, :], ACT.Exp, scale=-1.0))
                        nc.scalar.activation(fgate[:, 3, :], fgate[:, 2, :], ACT.Ln, bias=1.0).then_inc(flog_ready, 1)
                elif b < BRANCH:
                    ps = result(FIRST_RESULT[b])
                    if b == ZG:
                        act.wait_ge(ada_pooled, 6)
                    if b == ZG + 4:
                        act.wait_ge(ada_pooled, 7)
                    for i in range(2):
                        n = 2 * (b - ZG) + i
                        nc.scalar.activation(gates[:, n, :], ps[:, i * T:i * T + T], ACT.Tanh,
                                             bias=bgh[:, n:n + 1], scale=0.5).then_inc(drained_act if i else act_self, 1)
                    act_count[0] += 1

                def unit_slot(s):
                    if s % 8 == 3 and s > 8:
                        m = s // 8 - 1
                        act.wait_ge(pv_done, 8 * m + 8)
                        nc.scalar.activation(yhi[:, m, :], pO, ACT.Copy).then_inc(y_hi, 1)
                    if s < 24:
                        t = s % 8 // 4
                        nk = P * (t + 1)
                        act.wait_ge(smax_done, s + 1)
                        if s >= 3:
                            act.wait_ge(tr_done, s - 2)
                        nc.scalar.activation(up[:, s % 3, 0:nk], usc[:, s % 2, 0:nk], ACT.Exp, scale=-1.0,
                                             bias=unmax[:, s % 4:s % 4 + 1],
                                             accum_out=uden[:, s % 4:s % 4 + 1]).then_inc(exp_done, 1)
                    u = s - 2
                    if 0 <= u < 24:
                        nk = P * (u % 8 // 4 + 1)
                        act.wait_ge(tr_done, u + 1)
                        if u >= 2:
                            act.wait_ge(pv_done, u - 1)
                        nc.scalar.activation(upT[:, u % 2, 0:nk], pT[:, 256 * (u % 2):256 * (u % 2) + nk], ACT.Copy
                                             ).then_inc(pT_ready, 1)

                if ZG <= c < BRANCH:
                    unit_slot(2 * (c - ZG))
                    unit_slot(2 * (c - ZG) + 1)
                if c == BRANCH:
                    for s in (24, 25, 26, 27):
                        unit_slot(s)
                if b == WOUT - 1:
                    for j in range(4):
                        act.wait_ge(merged, 5 + j)
                        nc.scalar.activation(hhi[:, 2 * j:2 * j + 2, :], y[:, 2 * j:2 * j + 2, :], ACT.Copy, scale=0.5
                                             ).then_inc(mg_hi, 1)
                if WOUT <= b < UP:
                    j = b - WOUT
                    ps = result(FIRST_RESULT[b])
                    nc.scalar.activation(sq[:, 2 * j:2 * j + 2, :].rearrange("p a b -> p (a b)"), ps[:, :], ACT.Square
                                         ).then_inc(squares["n2"], 1)
                    act.wait_ge(mg_lo, 4)
                    nc.scalar.activation(y[:, 2 * j:2 * j + 2, :].rearrange("p a b -> p (a b)"), ps[:, :], ACT.Copy
                                         ).then_inc(drained_act, 1)
                if b == UP - 1:
                    norm_dev("n2", "eps6")
                    for k in range(KT):
                        act.wait_ge(scaled["n2"], k + 1)
                        nc.scalar.activation(sq[:, k, :], x[:, k, :], ACT.Square).then_inc(squares["n3"], 1)
                    norm_dev("n3", "eps6")
                    split_hi("n3", tb, lambda k: mod[:, 24 + k:25 + k])
                if UP <= b < DOWN:
                    j = (b - UP) // 2
                    if (b - UP) % 2 == 0:
                        ps = result(FIRST_RESULT[b])
                        if j == 0:
                            act.wait_ge(pad_set, 1)
                        if j >= 2:
                            act.wait_ge(conv_done, j - 1)
                        nc.scalar.activation(aseq[:, j % 2, :, 2:T + 2], ps[:, :].rearrange("p (a b) -> p a b", a=2),
                                             ACT.Copy).then_inc(drained_act, 1)
                        act.wait_ge(conv_done, j + 1)
                        if j >= 2:
                            act.wait_ge(u_full, j - 1)
                        nc.scalar.activation(gelu[:, j % 2, :, :], conv[:, j % 2, :, :], ACT.Gelu_apprx_tanh
                                             ).then_inc(gelu_done, 1)
                    else:
                        act.wait_ge(u_full, j + 1)
                        nc.scalar.activation(uhi[:, 2 * j:2 * j + 2, :], gelu[:, j % 2, :, :], ACT.Copy).then_inc(u_hi, 1)
                if DOWN <= b < GQ and (b - DOWN) % 3 == 2:
                    j = (b - DOWN) // 3
                    if j == 0:
                        act.wait_ge(ada_pooled, 16)
                    for i in range(2):
                        ps = result(FIRST_RESULT[b] + i)
                        nc.scalar.activation(sq[:, 2 * j + i, :], ps[:, 0:T], ACT.Square).then_inc(squares["n4"], 1)
                        nc.scalar.activation(y[:, 2 * j + i, :], ps[:, 0:T], ACT.Copy).then_inc(drained_act, 1)
                if b == GQ - 1:
                    norm_dev("n4", "eps6")
                    split_hi("n4", x)
                if GQ <= b < GA:
                    j = (b - GQ) % 2
                    ps = result(FIRST_RESULT[b])
                    dst = gq if b < GK else gk
                    nc.scalar.activation(dst[:, 2 * j:2 * j + 2, :].rearrange("p a b -> p (a b)"), ps[:, :], ACT.Copy,
                                         scale=P ** -0.5 if b < GK else 1.0).then_inc(drained_act, 1)
                if b == GA:
                    ps = result(FIRST_RESULT[b])
                    for t in range(2):
                        nc.scalar.activation(alr[:, t, :], ps[:, 256 * t:256 * t + 16], ACT.Copy
                                             ).then_inc(drained_act if t else act_self, 1)
                    act_count[0] += 1
                    act.wait_ge(alr_T, 2)
                    nc.scalar.activation(alrT[:, :], pT[0:16, 0:T], ACT.Copy).then_inc(alrT_ready, 1)
                    act.wait_ge(z_ready, 4)
                    own(nc.scalar.activation(gla, glz, ACT.Abs))
                    own(nc.scalar.activation(gla, gla, ACT.Exp, scale=-1.0))
                    nc.scalar.activation(gla, gla, ACT.Ln, bias=1.0).then_inc(loga_ready, 1)
                if GV <= b < GG:
                    j = b - GV
                    ps = result(FIRST_RESULT[b])
                    nc.scalar.activation(gv[:, :, 256 * j:256 * j + 256], ps[:, :].rearrange("p (t n) -> p t n", t=2),
                                         ACT.Copy).then_inc(drained_act, 1)
                if b == GV:
                    act.wait_ge(cum_ready, 1)
                    nc.scalar.activation(qdec[:, :], cum[:, :], ACT.Exp, scale=1.0 / 16).then_inc(gexp, 1)
                    nc.scalar.activation(elast[:, :], cum[:, :].rearrange("p (n c) -> p n c", c=64)[:, :, 63],
                                         ACT.Exp, scale=1.0 / 16).then_inc(gexp, 1)
                    act.wait_ge(gdiff, 1)
                    nc.scalar.activation(kdec[:, :], gdf, ACT.Exp, scale=1.0 / 16).then_inc(gexp, 1)
                    act.wait_ge(gdiff, 2)
                    nc.scalar.activation(qI[:, :], gdg, ACT.Exp, scale=1.0 / 16).then_inc(gexp, 1)
                if b == GV + 1:
                    act.wait_ge(gdiff, 6)
                    nc.scalar.activation(ekI[:, :], ekI[:, :], ACT.Exp, scale=1.0 / 16).then_inc(gexp, 1)
                if b == GV + 2:
                    for t in range(2):
                        act.wait_ge(kd_T, 4 * t + 4)
                        nc.scalar.activation(kdT[:, t, :, :].rearrange("p h n -> p (h n)"), pT[:, 512 * t:512 * t + 512],
                                             ACT.Copy).then_inc(kdT_ready, 1)
                if GG <= b < GOUT:
                    j = b - GG
                    ps = result(FIRST_RESULT[b])
                    if j:
                        act.wait_ge(gs_ready, j)
                    nc.scalar.activation(gth[:, :], ps[:, :], ACT.Tanh, scale=0.5).then_inc(gth_ready, 1)
                    for i in range(2):
                        nc.scalar.activation(gs[:, 2 * j + i, :], ps[:, i * T:i * T + T], ACT.Copy,
                                             scale=ggh[:, 2 * j + i:2 * j + i + 1]
                                             ).then_inc(drained_act if i else act_self, 1)
                    act_count[0] += 1
                    act.wait_ge(o_done, j + 1)
                    nc.scalar.activation(y[:, :, 64 * j:64 * j + 64], pS[:, 512 * (j % 2):512 * (j % 2) + 512]
                                         .rearrange("p (n i) -> p n i", n=8), ACT.Copy).then_inc(act_self, 1)
                    nc.scalar.activation(sq[:, :, 64 * j:64 * j + 64], pS[:, 512 * (j % 2):512 * (j % 2) + 512]
                                         .rearrange("p (n i) -> p n i", n=8), ACT.Square).then_inc(o_ready, 1)
                    act_count[0] += 1
                    act.wait_ge(act_self, act_count[0])
                    act.wait_ge(o_ready, j + 1)
                if b == GOUT - 1:
                    own(nc.scalar.activation(one[:, :], col("eps5", 0), ACT.Ln))
                    for h in range(4):
                        act.wait_ge(hmean, h // 2 * 2 + 2)
                        nc.scalar.activation(grs[:, h, :], pS[:, h * T:h * T + T], ACT.Ln,
                                             bias=col("eps5", 0)).then_inc(hdev, 1)
                    for h in range(4):
                        act.wait_ge(hdev, h + 1)
                        nc.scalar.activation(grs[:, h, :], grs[:, h, :], ACT.Exp, scale=-0.5).then_inc(hrstd, 1)
                    for j in range(4):
                        act.wait_ge(go_full, j + 1)
                        nc.scalar.activation(hhi[:, 2 * j:2 * j + 2, :], y[:, 2 * j:2 * j + 2, :], ACT.Copy).then_inc(go_hi, 1)
                if b in (SK - 1, NC - 1):
                    n = "n5" if b == SK - 1 else "n6"
                    for j in range(4):
                        act.wait_ge(centered[n], j + 1)
                        nc.scalar.activation(sq[:, 2 * j:2 * j + 2, :], tb[:, 2 * j:2 * j + 2, :], ACT.Square
                                             ).then_inc(squares[n], 1)
                    norm_dev(n, "eps5")
                    if n == "n5":
                        split_hi(n, x)
                if b in RH and b > KK:
                    swap(b, 64)
                if SV <= b < SWA:
                    j = b - SV
                    ps = result(FIRST_RESULT[b])
                    nc.scalar.activation(sv[:, :, 256 * j:256 * j + 256], ps[:, :].rearrange("p (t n) -> p t n", t=2),
                                         ACT.Copy).then_inc(drained_act, 1)
                if SWA <= b < SOUT and (b - SWA) % 4 == 3:
                    pair = (b - SWA) // 4
                    ps = result(FIRST_RESULT[b])
                    if pair:
                        act.wait_ge(sg_ready, pair)
                    nc.scalar.activation(sth[:, :], ps[:, :], ACT.Tanh, scale=0.5).then_inc(sth_ready, 1)
                    if pair >= 2:
                        act.wait_ge(d_of, 4 * pair - 4)
                    nc.scalar.activation(sgs[:, pair % 2, :, :].rearrange("p a b -> p (a b)"), ps[:, :], ACT.Copy,
                                         scale=0.5).then_inc(drained_act, 1)

                def dil_slot(s):
                    if 0 <= s < 16:
                        n = 384 * (s % 2 + 1)
                        act.wait_ge(d_max, s + 1)
                        if s >= 2:
                            act.wait_ge(d_tr, s - 1)
                        nc.scalar.activation(dp[:, s % 2, 0:n], dsc[:, s % 2, 0:n], ACT.Exp, scale=-1.0,
                                             bias=dnmax[:, s % 4:s % 4 + 1],
                                             accum_out=dden[:, s % 4:s % 4 + 1]).then_inc(d_exp, 1)
                    u = s - 1
                    if 0 <= u < 16:
                        n = 384 * (u % 2 + 1)
                        act.wait_ge(d_tr, u + 1)
                        if u >= 2:
                            act.wait_ge(d_pv, u - 1)
                        nc.scalar.activation(dpT[:, u % 2, 0:n], pT[:, 0:n], ACT.Copy).then_inc(d_pT, 1)
                    u = s - 2
                    if 0 <= u < 16:
                        h, t = u // 2, u % 2
                        act.wait_ge(d_of, u + 1)
                        nc.scalar.activation(ohi[:, h, t * P:t * P + P], of[:, u % 2, :], ACT.Copy).then_inc(d_hi, 1)

                if SWA + 4 <= c < SOUT:
                    dil_slot(c - SWA - 4)
                if c == SOUT:
                    for s in range(12, 18):
                        dil_slot(s)

        @block.vector
        def _(dve):
            dve_count = [0]

            def own(ins):
                ins.then_inc(dve_self, 1)
                dve_count[0] += 1
                dve.wait_ge(dve_self, dve_count[0])

            def low(c):
                if c >= NC:
                    return
                b = dve_part(c)
                dve.wait_ge(hi_ready, c + 1)
                if c >= SPL:
                    dve.wait_ge(product_done, CHUNK_MARK[c - SPL])
                nc.vector.tensor_tensor(wlo[c % SPL][:, 0:b], raw[RAW_OF["w", c] % RAW][:, 0:b],
                                        whi[c % SPL][:, 0:b].bitcast(f32), ALU.subtract).then_inc(lo_dve, 1)

            def result(r):
                dve.wait_ge(product_done, RESULT_MARK[r])
                return res[r % NB]

            def mod_cols(a):
                first = 0 if a == 7 else 2 * a - 2
                dve.wait_ge(ada_used, a + 1)
                nc.vector.tensor_tensor(mod[:, first:2 * a + 2], pmod[:, first:2 * a + 2],
                                        col("b_ada", first, 2 * a + 2 - first), ALU.add).then_inc(mod_ready, 1)

            def ada_sum(a):
                wait_raw(dve, ("ada", a))
                w = raw[RAW_OF["ada", a] % RAW][:, :].rearrange("p (k n) -> p k n", k=KT)
                acc = tb[:, a, :]
                own(nc.vector.tensor_scalar(acc, w[:, 0, :], cact[:, 0:1], None, ALU.mult))
                for k in range(1, 5):
                    ins = nc.vector.scalar_tensor_tensor(acc, w[:, k, :], cact[:, k:k + 1], acc, ALU.mult, ALU.add)
                    if k < 4:
                        own(ins)
                    else:
                        ins.then_inc(ada_summed, 1)

            def norm_rstd(n):
                dve.wait_ge(rstd_known[n], 1)

            def split_lo(n, src, bias=None, k_range=range(KT)):
                for k in k_range:
                    dve.wait_ge(in_hi[n], k + 1)
                    hi = hhi[:, k, :].bitcast(f32)
                    if bias is None:
                        nc.vector.tensor_tensor(hlo[:, k, :], src[:, k, :], hi, ALU.subtract).then_inc(in_lo[n], 1)
                    else:
                        nc.vector.scalar_tensor_tensor(hlo[:, k, :], src[:, k, :], bias(k), hi, ALU.add, ALU.subtract
                                                       ).then_inc(in_lo[n], 1)

            def scale_split(n, which, shift):
                for k in range(KT + 1):
                    if k < KT:
                        nc.vector.scalar_tensor_tensor(tb[:, k, :], x[:, k, :], pcol[:, which, k:k + 1], rstd[:, :],
                                                       ALU.mult, ALU.mult).then_inc(scaled[n], 1)
                    if k:
                        split_lo(n, tb, lambda i: mod[:, shift + i:shift + i + 1], range(k - 1, k))

            def rope(c, dst, table):
                ps = result(FIRST_RESULT[c])
                dve.wait_ge(moved_half, RH[c])
                nc.vector.tensor_tensor(dst, ps[:, :].rearrange("p (a b) -> p a b", a=2),
                                        table[:, 0:1, :].to_broadcast([P, 2, T]), ALU.mult).then_inc(drained_dve, 1)
                dve.wait_ge(drained_dve, RESULT_DRAIN[FIRST_RESULT[c]][1])
                dve.wait_ge(sin_done, RI[c] + 1)
                nc.vector.tensor_tensor(dst, dst, xsw, ALU.add).then_inc(roped, 1)

            def topk_round(t, i):
                nk, a = P * (t + 1), P * t
                src = score[:, a:a + nk] if i == 0 else left[:, (i + 1) % 2, 0:nk]
                own(nc.vector.max(best8[:, :], src))
                own(nc.vector.match_replace(left[:, i % 2, 0:nk], best8[:, :], src, TAKEN))
                if i == 7:
                    own(nc.vector.tensor_scalar(biasC[:, a:a + nk], left[:, 1, 0:nk], -2.0e38, NEG, ALU.is_gt, ALU.mult))

            def idx_sum(e):
                t, h = e // 4, e % 4
                nk, a = P * (t + 1), P * t
                dve.wait_ge(idx_relu, e + 1)
                if h == 0:
                    nc.vector.tensor_scalar(score[:, a:a + nk], relu[:, e % 2, 0:nk], wis[:, t, h:h + 1], None, ALU.mult
                                            ).then_inc(idx_acc, 1)
                else:
                    dve.wait_ge(idx_acc, e)
                    nc.vector.scalar_tensor_tensor(score[:, a:a + nk], relu[:, e % 2, 0:nk], wis[:, t, h:h + 1],
                                                   score[:, a:a + nk], ALU.mult, ALU.add).then_inc(idx_acc, 1)
                if h == 3:
                    dve.wait_ge(idx_acc, e + 1)
                    own(nc.vector.tensor_tensor(score[:, a:a + nk], score[:, a:a + nk], amask[:, a:a + nk], ALU.add))

            dve.wait_ge(const_in, 32)
            own(nc.vector.tensor_scalar(bgh[:, :], col("b_gate", 0, 24), 0.5, None, ALU.mult))
            own(nc.vector.tensor_scalar(ggh[:, :], col("gla_g", 0, 8), 0.5, None, ALU.mult))
            own(nc.vector.memset(fones, 1.0))
            dve.wait_ge(cact_ready, 1)
            for a in range(8):
                ada_sum(a)
            norm_rstd("n1")
            low(0)
            mod_cols(7)
            dve.wait_ge(mod_ready, 1)
            own(nc.vector.scalar_tensor_tensor(pcol[:, 0, :], mod[:, 8:16], 1.0, col("norm_g", 0, 8), ALU.add, ALU.mult))
            scale_split("n1", 0, 0)
            for c in range(1, SPL):
                low(c)

            for c in range(1, NC + 1):
                b = c - 1
                if BRANCH <= b < WOUT:
                    for j in range(4):
                        n = 4 * (b - BRANCH) + j
                        ps = result(FIRST_RESULT[b] + j)
                        if n == 0:
                            dve.wait_ge(drained_act, RESULT_DRAIN[FIRST_RESULT[BRANCH - 1]][1])
                            dve.wait_ge(ada_pooled, 12)
                        if b == BRANCH:
                            dst = y[:, 2 * j:2 * j + 2, :].rearrange("p a b -> p (a b)")
                        else:
                            dst = gtmp[:, n % 2, :]
                            if n >= 6:
                                dve.wait_ge(merged, n - 5)
                        g = 8 * (b - BRANCH) + 2 * j
                        nc.vector.scalar_tensor_tensor(dst, gates[:, g:g + 2, :].rearrange("p a b -> p (a b)"), 1.0,
                                                       ps[:, :], ALU.add, ALU.mult).then_inc(gated, 1)
                        dve.wait_ge(gated, n + 1)
                        nc.vector.engine_nop().then_inc(drained_dve, 1)
                low(c + 2)
                if b - 1 in ADA_USE:
                    mod_cols(ADA_USE[b - 1] + 1)
                if b == QC:
                    dve.wait_ge(mixc_in, 80)
                if b <= KK:
                    rope(b, qkv[("qc", "qi", "kk")[b]][:, :, :], rope1)
                if b == MISC:
                    for h in range(4):
                        own(nc.vector.scalar_tensor_tensor(biasA[:, h, :], biasA[:, h, :], 8.0, amask[:, :],
                                                           ALU.mult, ALU.add))
                    dve.wait_ge(drained_act, RESULT_DRAIN[FIRST_RESULT[MISC]][1])
                    nc.vector.tensor_scalar(wis[:, :, :], misc[:, :, 68:72], 0.5, None, ALU.mult).then_inc(wis_ready, 1)
                    dve.wait_ge(wis_ready, 1)
                if QA <= b < QA + 4:
                    idx_sum(2 * (b - QA))
                    idx_sum(2 * (b - QA) + 1)
                if b == KA:
                    dve.wait_ge(fT_done, 2)
                    nc.vector.tensor_scalar(fgate[:, 0, :], pT[0:4, 0:T], cols[0:4, COLS["b_forget"][0]:COLS["b_forget"][1]],
                                            None, ALU.add).then_inc(fz_ready, 1)
                    for i in range(8):
                        topk_round(0, i)
                if b == QB:
                    dve.wait_ge(flog_ready, 1)
                    own(nc.vector.scalar_tensor_tensor(fgate[:, 3, :], fgate[:, 0, :], 0.0, fgate[:, 3, :],
                                                       ALU.min, ALU.subtract))
                    nc.vector.tensor_tensor_scan(fgate[:, 4, :], fones, fgate[:, 3, :], 0.0, ALU.mult, ALU.add
                                                 ).then_inc(fcum_ready, 1)
                    for i in range(4):
                        topk_round(1, i)
                if b == KB:
                    for i in range(4, 8):
                        topk_round(1, i)
                if b in (KB, VB):
                    for h in ((0, 1) if b == KB else (2, 3)):
                        dve.wait_ge(bB_done, h + 1)
                        ps = pS[:, 512 * (h % 2):512 * (h % 2) + T]
                        own(nc.vector.tensor_tensor(biasB[:, h, 0:P], ps[:, 0:P], cmask[:, 0:P], ALU.add))
                        nc.vector.tensor_tensor(biasB[:, h, P:384], ps, cmask[:, P:384], ALU.add).then_inc(bB_ready, 1)
                    if b == VB:
                        dve.wait_ge(bB_ready, 4)

                def unit_slot(s):
                    if s % 8 == 3 and s > 8:
                        m = s // 8 - 1
                        dve.wait_ge(y_hi, m + 1)
                        nc.vector.tensor_tensor(ylo[:, m, :], pO, yhi[:, m, :].bitcast(f32), ALU.subtract).then_inc(y_lo, 1)
                    if s < 24:
                        m, t, h = s // 8, s % 8 // 4, s % 4
                        nk, a = P * (t + 1), P * t
                        bias = (biasA[:, h, a:a + nk], biasB[:, h, a:a + nk], biasC[:, a:a + nk])[m]
                        dve.wait_ge(qk_done, s + 1)
                        if s >= 2:
                            dve.wait_ge(exp_done, s - 1)
                        nc.vector.tensor_tensor_reduce(out=usc[:, s % 2, 0:nk], in0=pS[:, 512 * (s % 2):512 * (s % 2) + nk],
                                                       in1=bias, op0=ALU.add, op1=ALU.min, scale=-0.125, scalar=3.0e38,
                                                       accum_out=unmax[:, s % 4:s % 4 + 1]).then_inc(smax_done, 1)
                    u = s - 1
                    if 0 <= u < 24:
                        nk = P * (u % 8 // 4 + 1)
                        dve.wait_ge(exp_done, u + 1)
                        own(nc.vector.reciprocal(urec[:, u % 4:u % 4 + 1], uden[:, u % 4:u % 4 + 1]))
                        nc.vector.tensor_scalar(up[:, u % 3, 0:nk], up[:, u % 3, 0:nk], urec[:, u % 4:u % 4 + 1],
                                                None, ALU.mult).then_inc(norm_done, 1)

                if ZG <= c < BRANCH:
                    unit_slot(2 * (c - ZG))
                    unit_slot(2 * (c - ZG) + 1)
                if c == BRANCH:
                    for s in (24, 25, 26, 27):
                        unit_slot(s)
                if b == WOUT - 1:
                    for j in range(4):
                        dve.wait_ge(mg_hi, j + 1)
                        nc.vector.scalar_tensor_tensor(hlo[:, 2 * j:2 * j + 2, :], y[:, 2 * j:2 * j + 2, :], 0.5,
                                                       hhi[:, 2 * j:2 * j + 2, :].bitcast(f32), ALU.mult, ALU.subtract
                                                       ).then_inc(mg_lo, 1)
                if b == UP - 2:
                    dve.wait_ge(mod_ready, 7)
                    own(nc.vector.tensor_tensor(pcol[:, 1, :], mod[:, 16:24], col("norm_g", 8, 8), ALU.mult))
                    own(nc.vector.scalar_tensor_tensor(pcol[:, 2, :], mod[:, 32:40], 1.0, col("norm_g", 16, 8),
                                                       ALU.add, ALU.mult))
                if b == UP - 1 or b == GQ - 1:
                    n, which = ("n2", 1) if b == UP - 1 else ("n4", 3)
                    norm_rstd(n)
                    dve.wait_ge(drained_act, RESULT_DRAIN[FIRST_RESULT[b] + results_of(b) - 1][1])
                    for k in range(KT):
                        own(nc.vector.scalar_tensor_tensor(y[:, k, :], y[:, k, :], pcol[:, which, k:k + 1], rstd[:, :],
                                                           ALU.mult, ALU.mult))
                        nc.vector.tensor_tensor(x[:, k, :], x[:, k, :], y[:, k, :], ALU.add).then_inc(scaled[n], 1)
                        if b == GQ - 1 and k:
                            dve.wait_ge(scaled[n], k)
                            split_lo(n, x, None, range(k - 1, k))
                    if b == GQ - 1:
                        split_lo(n, x, None, range(KT - 1, KT))
                if b == UP - 1:
                    norm_rstd("n3")
                    scale_split("n3", 2, 24)
                if UP <= b < DOWN:
                    j = (b - UP) // 2
                    if (b - UP) % 2 == 0:
                        dve.wait_ge(drained_act, RESULT_DRAIN[FIRST_RESULT[b]][1])
                        if j >= 2:
                            dve.wait_ge(gelu_done, j - 1)
                        for i in range(2):
                            f = 2 * j + i
                            a, o = aseq[:, j % 2, i, :], conv[:, j % 2, i, :]
                            own(nc.vector.tensor_scalar(o, a[:, 0:T], col("conv_w", f), col("conv_b", f), ALU.mult, ALU.add))
                            own(nc.vector.scalar_tensor_tensor(o, a[:, 1:T + 1], col("conv_w", FT + f), o, ALU.mult, ALU.add))
                            ins = nc.vector.scalar_tensor_tensor(o, a[:, 2:T + 2], col("conv_w", 2 * FT + f), o,
                                                                 ALU.mult, ALU.add)
                            if i:
                                ins.then_inc(conv_done, 1)
                            else:
                                own(ins)
                    else:
                        ps = result(FIRST_RESULT[b])
                        dve.wait_ge(gelu_done, j + 1)
                        g = gelu[:, j % 2, :, :].rearrange("p a b -> p (a b)")
                        nc.vector.tensor_tensor(g, g, ps[:, :], ALU.mult).then_inc(drained_dve, 1)
                        dve.wait_ge(drained_dve, RESULT_DRAIN[FIRST_RESULT[b]][1])
                        nc.vector.engine_nop().then_inc(u_full, 1)
                        dve.wait_ge(u_hi, j + 1)
                        nc.vector.tensor_tensor(ulo[:, 2 * j:2 * j + 2, :], gelu[:, j % 2, :, :],
                                                uhi[:, 2 * j:2 * j + 2, :].bitcast(f32), ALU.subtract).then_inc(u_lo, 1)
                if b == DOWN:
                    dve.wait_ge(mod_ready, 9)
                    own(nc.vector.tensor_tensor(pcol[:, 3, :], mod[:, 40:48], col("norm_g", 24, 8), ALU.mult))
                if b == GV - 1:
                    for h in range(4):
                        dve.wait_ge(la_done, 4)
                        nc.vector.tensor_scalar(glz[:, h * T:h * T + T], pS[:, h * T:h * T + T], col("b_a2", h), None,
                                                ALU.add).then_inc(z_ready, 1)
                    dve.wait_ge(z_ready, 4)
                if b == GV - 1:
                    dve.wait_ge(loga_ready, 1)
                    dve.wait_ge(pad_set, 3)
                    own(nc.vector.scalar_tensor_tensor(glz, glz, 0.0, gla, ALU.min, ALU.subtract))
                    nc.vector.tensor_tensor_scan(cum[:, :], keep[:, :], glz, 0.0, ALU.mult, ALU.add).then_inc(cum_ready, 1)
                    dve.wait_ge(cum_ready, 1)
                    cc = cum[:, :].rearrange("p (n c) -> p n c", c=64)
                    nc.vector.tensor_tensor(gdf.rearrange("p (n c) -> p n c", c=64),
                                            cc[:, :, 63:64].to_broadcast([P, 16, 64]), cc, ALU.subtract).then_inc(gdiff, 1)
                    cs = cum[:, :].rearrange("p (n c) -> p n c", c=16)
                    nc.vector.tensor_tensor(gdg.rearrange("p (n c) -> p n c", c=16), cs,
                                            cs[:, :, 7:8].to_broadcast([P, 64, 16]), ALU.subtract).then_inc(gdiff, 1)
                    for i in range(4):
                        n, a = 16 * (i + 1), EK[i]
                        nc.vector.tensor_tensor(ekI[:, a:a + 16 * n].rearrange("p (m c) -> p m c", c=n),
                                                cc[:, :, 16 * i + 7:16 * i + 8].to_broadcast([P, 16, n]),
                                                cc[:, :, 0:n], ALU.subtract).then_inc(gdiff, 1)
                if b == GV:
                    fq = gq[:, :, :].rearrange("p h t -> p (h t)")
                    fk = gk[:, :, :].rearrange("p h t -> p (h t)")
                    dve.wait_ge(gexp, 3)
                    nc.vector.tensor_tensor(kdec[:, :], kdec[:, :], fk, ALU.mult).then_inc(gfac, 1)
                    nc.vector.tensor_tensor(qdec[:, :], qdec[:, :], fq, ALU.mult).then_inc(gfac, 1)
                    dve.wait_ge(gexp, 4)
                    nc.vector.tensor_tensor(qI[:, :], qI[:, :], fq, ALU.mult).then_inc(gfac, 1)
                if b == GV + 1:
                    dve.wait_ge(gexp, 5)
                    kk = gk[:, :, :].rearrange("p h t -> p (h t)").rearrange("p (m c) -> p m c", c=64)
                    for i in range(4):
                        n, a = 16 * (i + 1), EK[i]
                        v = ekI[:, a:a + 16 * n].rearrange("p (m c) -> p m c", c=n)
                        nc.vector.tensor_tensor(v, v, kk[:, :, 0:n], ALU.mult).then_inc(gfac, 1)
                if b == GV + 3:
                    dve.wait_ge(att_done, 1)
                    dve.wait_ge(glac_in, 32)
                    for half in range(2):
                        po = 64 * half
                        for i in range(4):
                            n = 16 * (i + 1)
                            src = pX[po:po + n, :].rearrange("p (h c i) -> p h c i", h=4, c=2)[:, :, :, 16 * i:16 * i + 16]
                            dst = att[po:po + n, :, half:4:2, 16 * i:16 * i + 16]
                            for h in range(4):
                                nc.vector.tensor_tensor(dst[:, h, :, :], src[:, h, :, :],
                                                        tri[po:po + n, None, 16 * i:16 * i + 16].to_broadcast([n, 2, 16]),
                                                        ALU.mult).then_inc(att_ready, 1)
                if GG <= b < GOUT:
                    j = b - GG
                    if j < 3:
                        for h in range(4):
                            dve.wait_ge(upd_done, 4 * j + 2 * (h // 2) + 2)
                            ups = pT[:, T * h:T * h + T]
                            if j == 0:
                                nc.vector.tensor_copy(state[:, h, :], ups).then_inc(state_ready, 1)
                            else:
                                dve.wait_ge(o_done, j + 1)
                                dve.wait_ge(state_ready, 4 * j)
                                nc.vector.scalar_tensor_tensor(state[:, h, :], state[:, h, :],
                                                               elast[:, 4 * h + j:4 * h + j + 1], ups,
                                                               ALU.mult, ALU.add).then_inc(state_ready, 1)
                    dve.wait_ge(drained_act, RESULT_DRAIN[FIRST_RESULT[b]][1])
                    g = gs[:, 2 * j:2 * j + 2, :].rearrange("p a b -> p (a b)")
                    nc.vector.scalar_tensor_tensor(g, gth[:, :], 1.0, g, ALU.add, ALU.mult).then_inc(gs_ready, 1)
                    dve.wait_ge(o_ready, j + 1)
                    sqj = sq[:, :, 64 * j:64 * j + 64].rearrange("p (h d) i -> p h d i", d=2)
                    nc.vector.tensor_tensor(tb[:, 0:4, 64 * j:64 * j + 64], sqj[:, :, 0, :], sqj[:, :, 1, :], ALU.add
                                            ).then_inc(osq, 1)
                if b == GOUT - 1:
                    dve.wait_ge(gs_ready, 4)
                    for j in range(4):
                        own(nc.vector.tensor_tensor(y[:, 2 * j:2 * j + 2, :], y[:, 2 * j:2 * j + 2, :],
                                                    gs[:, 2 * j:2 * j + 2, :], ALU.mult))
                    for j in range(4):
                        dve.wait_ge(hrstd, j + 1)
                        nc.vector.tensor_tensor(y[:, 2 * j:2 * j + 2, :], y[:, 2 * j:2 * j + 2, :],
                                                grs[:, j:j + 1, :].to_broadcast([P, 2, T]), ALU.mult).then_inc(go_full, 1)
                    for j in range(4):
                        dve.wait_ge(go_hi, j + 1)
                        nc.vector.tensor_tensor(hlo[:, 2 * j:2 * j + 2, :], y[:, 2 * j:2 * j + 2, :],
                                                hhi[:, 2 * j:2 * j + 2, :].bitcast(f32), ALU.subtract).then_inc(go_lo, 1)
                if GOUT <= b < SK or b >= SOUT:
                    n, j = ("n5", b - GOUT) if b < SK else ("n6", b - SOUT)
                    ps = result(FIRST_RESULT[b])
                    xx = x[:, 2 * j:2 * j + 2, :].rearrange("p a b -> p (a b)")
                    nc.vector.scalar_tensor_tensor(xx, xx, ALPHA, ps[:, :], ALU.mult, ALU.add).then_inc(summed[n], 1)
                    dve.wait_ge(summed[n], j + 1)
                    nc.vector.engine_nop().then_inc(drained_dve, 1)
                if b in (SK - 1, NC - 1):
                    n, l = ("n5", 0) if b == SK - 1 else ("n6", 1)
                    dve.wait_ge(mean_known[n], 1)
                    if n == "n6":
                        dve.wait_ge(roped, len(RH))
                    for j in range(4):
                        nc.vector.tensor_tensor(tb[:, 2 * j:2 * j + 2, :], x[:, 2 * j:2 * j + 2, :],
                                                stat[:, None, :].to_broadcast([P, 2, T]), ALU.subtract
                                                ).then_inc(centered[n], 1)
                    norm_rstd(n)
                    for k in range(KT):
                        g = 8 * l + k
                        own(nc.vector.scalar_tensor_tensor(x[:, k, :], tb[:, k, :], col("ln_g", g), rstd[:, :],
                                                           ALU.mult, ALU.mult))
                        ins = nc.vector.tensor_scalar(x[:, k, :], x[:, k, :], col("ln_b", g), None, ALU.add)
                        if n == "n5":
                            ins.then_inc(scaled[n], 1)
                            if k:
                                dve.wait_ge(scaled[n], k)
                                split_lo(n, x, None, range(k - 1, k))
                        elif k % 2:
                            ins.then_inc(out_ready, 1)
                        else:
                            own(ins)
                    if n == "n5":
                        dve.wait_ge(scaled[n], KT)
                        split_lo(n, x, None, range(KT - 1, KT))
                if b in RH and b > KK:
                    if b == SK:
                        dve.wait_ge(swac_in, 32)
                    if b < SV:
                        rope(b, sk[:, 2 * (b - SK):2 * (b - SK) + 2, :], rope2)
                    else:
                        pair, g = (b - SWA) // 4, (b - SWA) % 4
                        if pair >= 2:
                            dve.wait_ge(d_qk, 4 * pair - 4)
                        rope(b, sqr[:, pair % 2, 2 * g:2 * g + 2, :], rope2)
                if SWA <= b < SOUT and (b - SWA) % 4 == 3:
                    pair = (b - SWA) // 4
                    dve.wait_ge(drained_act, RESULT_DRAIN[FIRST_RESULT[b]][1])
                    g = sgs[:, pair % 2, :, :].rearrange("p a b -> p (a b)")
                    nc.vector.scalar_tensor_tensor(g, sth[:, :], 1.0, g, ALU.add, ALU.mult).then_inc(sg_ready, 1)
                    dve.wait_ge(sg_ready, pair + 1)

                def dil_slot(s):
                    if 0 <= s < 16:
                        t = s % 2
                        n = 384 * (t + 1)
                        dve.wait_ge(d_qk, s + 1)
                        if s >= 2:
                            dve.wait_ge(d_exp, s - 1)
                        nc.vector.tensor_tensor_reduce(out=dsc[:, s % 2, 0:n], in0=pS[:, 0:n],
                                                       in1=dmask[:, 384 * t:384 * t + n], op0=ALU.add, op1=ALU.min,
                                                       scale=-(P ** -0.5), scalar=3.0e38,
                                                       accum_out=dnmax[:, s % 4:s % 4 + 1]).then_inc(d_max, 1)
                        dve.wait_ge(d_exp, s + 1)
                        own(nc.vector.reciprocal(drec[:, s % 4:s % 4 + 1], dden[:, s % 4:s % 4 + 1]))
                        nc.vector.tensor_scalar(dp[:, s % 2, 0:n], dp[:, s % 2, 0:n], drec[:, s % 4:s % 4 + 1], None,
                                                ALU.mult).then_inc(d_norm, 1)
                    u = s - 2
                    if 0 <= u < 16:
                        h, t = u // 2, u % 2
                        pair = h // 2
                        dve.wait_ge(d_pv, u + 1)
                        if u >= 2:
                            dve.wait_ge(d_lo, u - 1)
                        nc.vector.tensor_tensor(of[:, u % 2, :], pX[:, T + P * (u % 2):T + P * (u % 2) + P],
                                                sgs[:, pair % 2, h % 2, t * P:t * P + P], ALU.mult).then_inc(d_of, 1)
                        dve.wait_ge(d_hi, u + 1)
                        nc.vector.tensor_tensor(olo[:, h, t * P:t * P + P], of[:, u % 2, :],
                                                ohi[:, h, t * P:t * P + P].bitcast(f32), ALU.subtract).then_inc(d_lo, 1)

                if SWA + 4 <= c < SOUT:
                    dil_slot(c - SWA - 4)
                if c == SOUT:
                    for s in range(12, 18):
                        dil_slot(s)

        @block.tensor
        def _(pe):
            mm = nc.tensor.matmul

            def ada(a):
                if a < 8:
                    wait_raw(pe, ("ada", a))
                    pe.wait_ge(ada_summed, a + 1)
                    w = raw[RAW_OF["ada", a] % RAW][:, :].rearrange("p (k n) -> p k n", k=KT)
                    acc = tb[:, a, :]
                else:
                    pe.wait_ge(ada_pooled, a - 7)
                    pe.wait_ge(mod_ready, (a - 6) // 2)
                    acc = adasum[:, a % 4, :]
                if a == 0:
                    pe.wait_ge(dev_known["n1"], 1)
                for i in range(2):
                    out = pmod[:, 2 * a + i:2 * a + i + 1]
                    if a < 8:
                        for k in range(5, KT):
                            mm(out, w[:, k, i * P:i * P + P], cact[:, k:k + 1], start=k == 5, stop=False)
                    last = mm(out, acc[:, i * P:i * P + P], ones[:, :], start=a >= 8, stop=True)
                last.then_inc(ada_used, 1)

            def three(out, ah, al, bh, bl, first, last):
                mm(out, ah, bh, start=first, stop=False)
                mm(out, al, bh, start=False, stop=False)
                return mm(out, ah, bl, start=False, stop=last)

            def bank(r):
                if r >= NB:
                    who, n = RESULT_DRAIN[r - NB]
                    pe.wait_ge(drained[who], n)
                return res[r % NB]

            def weights(c):
                pe.wait_ge(lo_dve, c + 1)
                pe.wait_ge(lo_pool, c + 1)
                kt, w = kt_of(c)
                return (whi[c % SPL][:, 0:kt * w].rearrange("p (k n) -> p k n", k=kt),
                        wlo[c % SPL][:, 0:kt * w].rearrange("p (k n) -> p k n", k=kt))

            def fm(c, ih, il, ready=None, half=None):
                wh, wl = weights(c)
                ps = bank(FIRST_RESULT[c])
                for i in range(2):
                    for k in range(KT):
                        if ready and i == 0:
                            ready(k)
                        last = three(ps[:, i * T:i * T + T], wh[:, k, i * P:i * P + P], wl[:, k, i * P:i * P + P],
                                     ih[:, k, :], il[:, k, :], k == 0, k == KT - 1)
                    if i == 0 and half:
                        half()
                last.then_inc(product_done, 1)

            def tm(c, ih, il):
                wh, wl = weights(c)
                w = kt_of(c)[1]
                ps = bank(FIRST_RESULT[c])
                for t in range(2):
                    for k in range(KT):
                        last = three(ps[:, t * 256:t * 256 + w], ih[:, k, t * P:t * P + P], il[:, k, t * P:t * P + P],
                                     wh[:, k, :], wl[:, k, :], k == 0, k == KT - 1)
                last.then_inc(product_done, 1)

            def mean(n, src, ks, need, count=1):
                for k in ks:
                    pe.wait_ge(need, (k // (KT // count)) + 1 if count != KT else k + 1)
                    last = mm(stat, meanw[:, :], src[:, k, :], start=k == 0, stop=k == KT - 1)
                if k == KT - 1:
                    last.then_inc(mean_known[n], 1)

            def units(s):
                if s < 24:
                    m, t, h = s // 8, s % 8 // 4, s % 4
                    nk, po = P * (t + 1), 64 * (h % 2)
                    q = qkv[("qa", "qb", "qc")[m]]
                    k = (qkv["ka"][po:po + 64, h // 2, 0:nk], qkv["kb"][po:po + 64, h // 2, 0:nk],
                         qkv["kk"][po:po + 64, 0, 0:nk])[m]
                    if s < 2:
                        pe.wait_ge(bB_ready, 3 + s)
                    if s == 0:
                        pe.wait_ge(drained_act, RESULT_DRAIN[FIRST_RESULT[VB]][1])
                    if s >= 2:
                        pe.wait_ge(smax_done, s - 1)
                    mm(pS[:, 512 * (s % 2):512 * (s % 2) + nk], q[po:po + 64, h // 2, t * P:t * P + P], k,
                       start=True, stop=True).then_inc(qk_done, 1)
                u = s - 2
                if 0 <= u < 24:
                    nk = u % 8 // 4 + 1
                    pe.wait_ge(norm_done, u + 1)
                    if u:
                        pe.wait_ge(pT_ready, u)
                    for i in range(nk):
                        last = nc.tensor.transpose(pT[:, 256 * (u % 2) + P * i:256 * (u % 2) + P * i + P],
                                                   up[:, u % 3, P * i:P * i + P], ident[:, :])
                    last.then_inc(tr_done, 1)
                u = s - 3
                if 0 <= u < 24:
                    m, t, h = u // 8, u % 8 // 4, u % 4
                    po = 64 * (h % 2)
                    pe.wait_ge(pT_ready, u + 1)
                    if u % 8 == 0 and m:
                        pe.wait_ge(y_lo, m)
                    for i in range(t + 1):
                        v = (qkv["va"], qkv["vb"])[m][:, i, 64 * h:64 * h + 64] if m < 2 else misc[:, i, 0:64]
                        last = mm(pO[po:po + 64, T * (h // 2) + t * P:T * (h // 2) + t * P + P], v,
                                  upT[:, u % 2, P * i:P * i + P], start=i == 0, stop=i == t)
                    last.then_inc(pv_done, 1)

            def dilated(s):
                if 0 <= s < 16:
                    h, t = s // 2, s % 2
                    pair, hh, nk = h // 2, h % 2, P * (t + 1)
                    pe.wait_ge(roped, RI[SWA + 4 * pair + 2] + 1)
                    if s:
                        pe.wait_ge(d_max, s)
                    for g in range(3):
                        last = mm(pS[:, g * nk:g * nk + nk], sqr[:, pair % 2, 2 * g + hh, t * P:t * P + P],
                                  sk[:, 2 * g + h // 4, 0:nk], start=True, stop=True)
                    last.then_inc(d_qk, 1)
                u = s - 1
                if 0 <= u < 16:
                    n = 3 * (u % 2 + 1)
                    pe.wait_ge(d_norm, u + 1)
                    if u:
                        pe.wait_ge(d_pT, u)
                    for i in range(n):
                        last = nc.tensor.transpose(pT[:, P * i:P * i + P], dp[:, u % 2, P * i:P * i + P], ident[:, :])
                    last.then_inc(d_tr, 1)
                u = s - 2
                if 0 <= u < 16:
                    h, t = u // 2, u % 2
                    nk = t + 1
                    pe.wait_ge(d_pT, u + 1)
                    if u:
                        pe.wait_ge(d_of, u)
                    for i in range(3 * nk):
                        g, kt = i // nk, i % nk
                        v = sv[:, kt, 256 * g + P * (h // 4):256 * g + P * (h // 4) + P]
                        last = mm(pX[:, T + P * (u % 2):T + P * (u % 2) + P], v, dpT[:, u % 2, P * i:P * i + P],
                                  start=i == 0, stop=i == 3 * nk - 1)
                    last.then_inc(d_pv, 1)

            pe.wait_ge(const_set, 3)
            pe.wait_ge(cact_ready, 1)
            mean("n1", sq, range(KT), squares["n1"], KT)
            for a in range(8):
                ada(a)
            for c in range(NC):
                if c < BRANCH:
                    if c in (MISC, VA, VB):
                        tm(c, hhi, hlo)
                    else:
                        half = (lambda c=c: units(2 * (c - ZG))) if c >= ZG else None
                        fm(c, hhi, hlo, (lambda k: pe.wait_ge(in_lo["n1"], k + 1)) if c == 0 else None, half)
                    if c in ADA_USE:
                        ada(ADA_USE[c])
                        ada(ADA_USE[c] + 1)
                    if QA <= c < QA + 4:
                        for e in (2 * (c - QA), 2 * (c - QA) + 1):
                            t, h = e // 4, e % 4
                            nk, po = P * (t + 1), 64 * (h % 2)
                            if e == 0:
                                pe.wait_ge(roped, 3)
                            if e >= 2:
                                pe.wait_ge(idx_relu, e - 1)
                            mm(pS[:, 512 * (e % 2):512 * (e % 2) + nk], qkv["qi"][po:po + 64, h // 2, t * P:t * P + P],
                               qkv["kk"][po:po + 64, 1, 0:nk], start=True, stop=True).then_inc(idx_done, 1)
                    if c == KA:
                        pe.wait_ge(const_in, 32)
                        pe.wait_ge(drained_act, RESULT_DRAIN[FIRST_RESULT[MISC]][1])
                        for t in range(2):
                            nc.tensor.transpose(pT[0:4, P * t:P * t + P], misc[:, t, 64:68], ident[:, :]).then_inc(fT_done, 1)
                    if c in (KB, VB):
                        pe.wait_ge(fcum_ready, 1)
                        pe.wait_ge(idx_relu, 8)
                        pe.wait_ge(mixc_in, 80)
                        for h in ((0, 1) if c == KB else (2, 3)):
                            if h >= 2:
                                pe.wait_ge(bB_ready, h - 1)
                            mm(pS[:, 512 * (h % 2):512 * (h % 2) + T], sel[:, P * h:P * h + P], fgate[:, 4, :],
                               start=True, stop=True).then_inc(bB_done, 1)
                    if c >= ZG:
                        units(2 * (c - ZG) + 1)
                elif c < WOUT:
                    b = c - BRANCH
                    wh, wl = weights(c)
                    if b == 2:
                        pe.wait_ge(y_lo, 3)
                    for j in range(4):
                        ps = bank(FIRST_RESULT[c] + j)
                        for i in range(2):
                            n = 2 * j + i
                            for k in range(2):
                                last = three(ps[:, i * T:i * T + T], wh[:, k, n * P:n * P + P], wl[:, k, n * P:n * P + P],
                                             yhi[:, b, k * T:k * T + T], ylo[:, b, k * T:k * T + T], k == 0, k == 1)
                        last.then_inc(product_done, 1)
                        if b == 0 and j < 3:
                            units(24 + j)
                    if c in ADA_USE:
                        ada(ADA_USE[c])
                        ada(ADA_USE[c] + 1)
                elif c < UP:
                    fm(c, hhi, hlo, (lambda k: pe.wait_ge(mg_lo, k // 2 + 1)) if c == WOUT else None)
                    if c == WOUT + 1:
                        pe.wait_ge(mod_ready, 7)
                    if c > WOUT:
                        j = c - WOUT - 1
                        mean("n2", sq, (2 * j, 2 * j + 1), squares["n2"], 4)
                    if c == UP - 1:
                        mean("n2", sq, (6, 7), squares["n2"], 4)
                        pe.wait_ge(dev_known["n2"], 1)
                        mean("n3", sq, range(KT), squares["n3"], KT)
                elif c < DOWN:
                    fm(c, hhi, hlo, (lambda k: pe.wait_ge(in_lo["n3"], k + 1)) if c == UP else None)
                    if c in ADA_USE:
                        ada(ADA_USE[c])
                        ada(ADA_USE[c] + 1)
                elif c < GQ:
                    j, kg = (c - DOWN) // 3, (c - DOWN) % 3
                    wh, wl = weights(c)
                    kt = kt_of(c)[0]
                    r = 2 * j + FIRST_RESULT[DOWN]
                    for i in range(2):
                        ps = bank(r + i) if kg == 0 else res[(r + i) % NB]
                        for k in range(kt):
                            kk = 8 * kg + k
                            if j == 0 and i == 0 and kk % 2 == 0:
                                pe.wait_ge(u_lo, kk // 2 + 1)
                            last = three(ps[:, 0:T], wh[:, k, i * P:i * P + P], wl[:, k, i * P:i * P + P],
                                         uhi[:, kk, :], ulo[:, kk, :], kk == 0, kk == FT - 1)
                        if i == 1 or kg == 2:
                            last.then_inc(product_done, 1)
                    if kg == 1 and j:
                        mean("n4", sq, (2 * j - 2, 2 * j - 1), squares["n4"], KT)
                    if c == GQ - 1:
                        mean("n4", sq, (6, 7), squares["n4"], KT)
                elif c < GOUT:
                    if c == GA or GV <= c < GG:
                        tm(c, hhi, hlo)
                    else:
                        fm(c, hhi, hlo, (lambda k: pe.wait_ge(in_lo["n4"], k + 1)) if c == GQ else None)
                    if c == GA:
                        pe.wait_ge(drained_act, RESULT_DRAIN[FIRST_RESULT[GA]][1])
                        for t in range(2):
                            nc.tensor.transpose(pT[0:16, P * t:P * t + P], alr[:, t, :], ident[:, :]).then_inc(alr_T, 1)
                        pe.wait_ge(alrT_ready, 1)
                        pe.wait_ge(glac_in, 32)
                        for h in range(4):
                            mm(pS[:, h * T:h * T + T], wa2[:, h * P:h * P + P], alrT[:, :], start=True, stop=True
                               ).then_inc(la_done, 1)
                    if c == GV + 2:
                        pe.wait_ge(gfac, 1)
                        for t in range(2):
                            for h in range(4):
                                nc.tensor.transpose(pT[:, 512 * t + P * h:512 * t + P * h + P],
                                                    kdec[:, h * T + t * P:h * T + t * P + P], ident[:, :]).then_inc(kd_T, 1)
                    if c == GV + 3:
                        pe.wait_ge(gfac, 7)
                        for h in range(4):
                            for ch in range(4):
                                po, m = 64 * (ch % 2), 4 * h + ch
                                for i in range(4):
                                    n = 16 * (i + 1)
                                    last = mm(pX[po:po + n, P * h + 64 * (ch // 2) + 16 * i:P * h + 64 * (ch // 2) + 16 * i + 16],
                                              ekI[:, EK[i] + m * n:EK[i] + m * n + n], qI[:, 64 * m + 16 * i:64 * m + 16 * i + 16],
                                              start=True, stop=True)
                        last.then_inc(att_done, 1)
                    if GG <= c < GOUT:
                        j = c - GG
                        t, po = j // 2, 64 * (j % 2)
                        if j == 0:
                            pe.wait_ge(att_ready, 32)
                            pe.wait_ge(gfac, 2)
                            pe.wait_ge(kdT_ready, 2)
                            pe.wait_ge(drained_act, RESULT_DRAIN[FIRST_RESULT[GG - 1]][1])
                        if j >= 2:
                            pe.wait_ge(o_ready, j - 1)
                        for h in range(4):
                            if j:
                                pe.wait_ge(state_ready, 4 * (j - 1) + h + 1)
                            for d in range(2):
                                o = pS[:, 512 * (j % 2) + 64 * (2 * h + d):512 * (j % 2) + 64 * (2 * h + d) + 64]
                                if j:
                                    mm(o, state[:, h, d * P:d * P + P], qdec[:, h * T + 64 * j:h * T + 64 * j + 64],
                                       start=True, stop=False)
                                last = mm(o, gv[:, t, 256 * h + P * d:256 * h + P * d + P], att[:, h, j, :],
                                          start=j == 0, stop=True)
                        last.then_inc(o_done, 1)
                        if j < 3:
                            for h in range(4):
                                mm(pT[:, T * h:T * h + T], kdT[po:po + 64, t, h, :], gv[po:po + 64, t, 256 * h:256 * h + 256],
                                   start=True, stop=True).then_inc(upd_done, 1)
                    if c == GOUT - 1:
                        pe.wait_ge(osq, 4)
                        for h in range(4):
                            mm(pS[:, h * T:h * T + T], headw[:, :], tb[:, h, :], start=True, stop=True).then_inc(hmean, 1)
                elif c < SK:
                    fm(c, hhi, hlo, (lambda k: pe.wait_ge(go_lo, k // 2 + 1)) if c == GOUT else None)
                    if c > GOUT:
                        j = c - GOUT - 1
                        mean("n5", x, (2 * j, 2 * j + 1), summed["n5"], 4)
                    if c == SK - 1:
                        mean("n5", x, (6, 7), summed["n5"], 4)
                        pe.wait_ge(centered["n5"], 4)
                        mean("n5", sq, range(KT), squares["n5"], 4)
                elif c < SOUT:
                    if SV <= c < SWA:
                        tm(c, hhi, hlo)
                    else:
                        fm(c, hhi, hlo, (lambda k: pe.wait_ge(in_lo["n5"], k + 1)) if c == SK else None)
                    if c >= SWA + 4:
                        if c == SWA + 4:
                            pe.wait_ge(drained_act, RESULT_DRAIN[FIRST_RESULT[SWA - 1]][1])
                        dilated(c - SWA - 4)
                    if c == SOUT - 1:
                        for s in range(12, 18):
                            dilated(s)
                else:
                    fm(c, ohi, olo, (lambda k: pe.wait_ge(d_lo, 2 * k + 2)) if c == SOUT else None)
                    if c > SOUT:
                        j = c - SOUT - 1
                        mean("n6", x, (2 * j, 2 * j + 1), summed["n6"], 4)
                    if c == NC - 1:
                        mean("n6", x, (6, 7), summed["n6"], 4)
                        pe.wait_ge(centered["n6"], 4)
                        mean("n6", sq, range(KT), squares["n6"], 4)


RI, RH = {}, {}
_moves = 0
for _c in [QC, QI, KK, SK, SK + 1, SK + 2] + [SWA + 4 * _p + _g for _p in range(4) for _g in range(3)]:
    RI[_c] = len(RI)
    _moves += 4 if _c <= KK else 2
    RH[_c] = _moves
EK = [16 * 16 * i * (i + 1) // 2 for i in range(4)]


def kernel(**inp):
    import numpy as np
    import concourse.bacc as bacc
    from concourse import mybir as mb
    from concourse.bass_utils import run_bass_kernel_spmd

    a = {k: np.asarray(v) for k, v in inp.items()}
    f4 = np.float32

    def fm(v):
        return np.ascontiguousarray(v.reshape(-1, P).T)

    forget = np.zeros((P, 1), f4)
    forget[0:4, 0] = a["b_forget"][0]
    cols = np.concatenate([
        fm(a["c"][0]), fm(a["b_ada"][0]), fm(a["norm_g"][0]), fm(a["b_gate"][0]), fm(a["conv_w"][0]),
        fm(a["conv_b"][0]), fm(a["gla_b_a2_2"][0]), fm(a["gla_norm_g_2"][0]), fm(a["ln_g_2"]), fm(a["ln_b_2"]),
        forget, np.full((P, 1), 1e-6, f4), np.full((P, 1), 1e-5, f4)], axis=1)

    def rope_table(dim):
        half = dim // 2
        inv = (f4(10000.0) ** (-np.arange(half, dtype=f4) * f4(2.0) / f4(dim))).astype(f4)
        p = np.arange(P) % dim
        ang = inv[p % half][:, None] * np.arange(T, dtype=f4)[None, :]
        sign = np.where(p < half, -1.0, 1.0).astype(f4)[:, None]
        return np.stack([np.cos(ang), np.sin(ang) * sign], axis=1).astype(f4)

    q = np.arange(P)[:, None]

    def two_tiles(ok):
        return [np.where(ok(q + P * t, np.arange(P * (t + 1))[None, :]), 0.0, NEG).astype(f4) for t in range(2)]

    amask = np.concatenate(two_tiles(lambda i, j: j // 64 <= i // 64), axis=1)
    cmask = np.concatenate(two_tiles(lambda i, j: j <= i), axis=1)
    dil = [two_tiles(lambda i, j, d=d, w=w: (j <= i) & (i - j <= w) & ((i - j) % d == 0))
           for w, d in ((128, 1), (512, 4), (2048, 16))]
    dmask = np.concatenate([m[t] for t in range(2) for m in dil], axis=1)
    tri = (np.arange(P)[:, None] % 64 <= np.arange(64)[None, :]).astype(f4)
    sel = np.zeros((4, 4, P), f4)
    for h in range(4):
        sel[h, h, :] = -8.0
    rel = [np.clip(q + P * t - np.arange(P * (t + 1))[None, :], -128, 128) + 128 for t in range(2)]
    table = a["rel_table"][0]
    relb = np.ascontiguousarray(np.concatenate([table[:, r] for r in rel], axis=2).transpose(1, 0, 2))

    arrays = {
        "xT": np.ascontiguousarray(a["x"][0].T.reshape(KT, P, T).transpose(1, 0, 2)),
        "cols": cols, "ident": np.eye(P, dtype=f4), "rope1": rope_table(64), "rope2": rope_table(128),
        "amask": amask, "cmask": cmask, "tri": tri, "dmask": dmask, "sel": sel.reshape(4, 512), "relb": relb,
        "w_a2": a["gla_w_a2_2"][0],
        "w_ada": a["w_ada"][0], "w_in": a["w_in"][0], "w_branch": a["w_branch"][0], "w_out": a["w_out"][0],
        "w_up": a["w_up"][0], "w_down": a["w_down"][0], "gla_in": a["gla_w_in_2"][0], "gla_out": a["gla_w_out_2"][0],
        "w_kv": a["w_kv_2"], "swa_in": a["swa_w_in_2"][0], "swa_out": a["swa_w_out_2"][0],
    }
    order = ["xT", "cols", "ident", "rope1", "rope2", "amask", "cmask", "tri", "dmask", "sel", "relb", "w_a2",
             "w_ada", "w_in", "w_branch", "w_out", "w_up", "w_down", "gla_in", "gla_out", "w_kv", "swa_in", "swa_out"]
    nc = bacc.Bacc("TRN2", target_bir_lowering=False, num_devices=1, dynamic_dma_scratch_size=8192)
    sent = {f"in_{n}": np.ascontiguousarray(arrays[n]) for n in order}
    args = [nc.dram_tensor(n, v.shape, mb.dt.float32, kind="ExternalInput").ap() for n, v in sent.items()]
    out = nc.dram_tensor("outT", (P, KT, T), mb.dt.float32, kind="ExternalOutput").ap()
    build(nc, *args, out)
    r = run_bass_kernel_spmd(nc, [sent], core_ids=[0])
    got = r.results[0]["outT"]
    return np.ascontiguousarray(got.transpose(1, 0, 2).reshape(D, T).T)[None]
```

```python
import concourse.bass as bass
from concourse import mybir
from contextlib import ExitStack

D, T, P = 1024, 256, 128
KT = D // P
D_FF = 2816
FT = D_FF // P
NEG = -1.0e30
TAKEN = -3.0e38
ALPHA = 4.0 ** 0.25
RAW, SPL, NB = 4, 3, 3
CW = 2048

COLS = {}
_at = 0
for _n, _w in (("c", 8), ("b_ada", 48), ("norm_g", 32), ("b_gate", 24), ("conv_w", 66), ("conv_b", 22),
               ("b_a2", 4), ("gla_g", 8), ("ln_g", 16), ("ln_b", 16), ("b_forget", 1), ("eps6", 1), ("eps5", 1)):
    COLS[_n] = (_at, _at + _w)
    _at += _w
NCOL = _at

QC, QI, KK, MISC, QA, KA, VA, QB, KB, VB = range(10)
ZG = 10
BRANCH = ZG + 12
WOUT = BRANCH + 3
UP = WOUT + 4
DOWN = UP + 22
GQ = DOWN + 12
GK = GQ + 2
GA = GK + 2
GV = GA + 1
GG = GV + 4
GOUT = GG + 4
SK = GOUT + 4
SV = SK + 3
SWA = SV + 3
SOUT = SWA + 16
NC = SOUT + 4
MW = 72
NADA = 24
ADA_STEPS = [0, 1, 2, 3, 4, 5, 6, 6, 7, 8, 8, 9] + list(range(10, 22)) + [UP + 2 + 3 * i + j for i in range(4) for j in range(2)]
ADA_START = {8 + i: ADA_STEPS[2 * i] for i in range(16)}
ADA_END = {8 + i: ADA_STEPS[2 * i + 1] for i in range(16)}
ADA_USE = {ADA_END[a + 1] + 3: a for a in range(8, 24, 2)}
ADA_AT = {0: 0, 1: 1, 2: 2, 3: "y", 8: 0, 9: 1, 10: 2, 11: 0, 12: 1, 13: 2, 14: 1, 15: "y", 16: "sq", 17: "y", 18: "sq", 19: "y",
          20: "y", 21: "sq", 22: "y", 23: "sq"}


ADA_GPS = (0, 1)


def ada_dve(a):
    return KT if a < 5 else 6 if a < 7 else 5


def kt_of(c):
    if c == MISC:
        return KT, MW
    if c == GA:
        return KT, 16
    if BRANCH <= c < WOUT:
        return 2, 1024
    if DOWN <= c < GQ:
        return (8, 8, 6)[(c - DOWN) % 3], 256
    return KT, 256


def results_of(c):
    if BRANCH <= c < WOUT:
        return 4
    if DOWN <= c < GQ:
        return 2 if (c - DOWN) % 3 == 2 else 0
    return 1


def drainer_of(c):
    if c < MISC or BRANCH <= c < WOUT or (UP <= c < DOWN and (c - UP) % 2 == 1):
        return "dve"
    if GOUT <= c < SV or c >= SOUT or (SWA <= c < SOUT and (c - SWA) % 4 != 3):
        return "dve"
    return "act"


LATE = (WOUT - 1, UP - 1, GQ - 1, GOUT - 1, SK - 1, SOUT - 1)
LO_POOL = (3, 6)

PAIRS = (0, 3, 1, 2)
ARRIVAL = (0, 1, 2, 4, 3, 5, 7, 6)

CHUNK_MARK, FIRST_RESULT, RESULT_MARK, RESULT_DRAIN = [], [], [], []
_m, _n = 0, {"act": 0, "dve": 0}
for _c in range(NC):
    FIRST_RESULT.append(len(RESULT_MARK))
    for _i in range(results_of(_c)):
        _m += 1
        RESULT_MARK.append(_m)
        _n[drainer_of(_c)] += 1
        RESULT_DRAIN.append((drainer_of(_c), _n[drainer_of(_c)]))
    if not results_of(_c):
        _m += 1
    CHUNK_MARK.append(_m)

STREAM = [("ada", a) for a in range(8)]
for _c in range(NC):
    STREAM.append(("w", _c))
    STREAM += [("ada", _a) for _a in range(8, NADA) if ADA_START[_a] + 2 == _c]
RING = [e for e in STREAM if e[0] == "w" or 4 <= e[1] < 8]
RAW_OF = {e: i for i, e in enumerate(RING)}


def pieces(c, W):
    w_in, w_branch, w_out, w_up, w_down, gla_in, gla_out, w_kv, swa_in, swa_out = W

    def cols(m, a, n):
        return m[:, a:a + n].rearrange("(k p) n -> p k n", p=P)

    if c == QC:
        return [(0, cols(w_in, 1540, 256))]
    if c == QI:
        return [(0, cols(w_in, 1924, 256))]
    if c == KK:
        return [(0, cols(w_in, 1796, 64)), (64, cols(w_in, 1796, 64)),
                (128, cols(w_in, 2180, 64)), (192, cols(w_in, 2180, 64))]
    if c == MISC:
        return [(0, cols(w_in, 1860, 64)), (64, cols(w_in, 1536, 4)), (68, cols(w_in, 2244, 4))]
    if c < ZG:
        return [(0, cols(w_in, 256 * (c - QA), 256))]
    if c < BRANCH:
        return [(0, cols(w_in, 2248 + 256 * (c - ZG), 256))]
    if c < WOUT:
        return [(0, cols(w_branch[c - BRANCH], 0, 1024))]
    if c < UP:
        return [(0, cols(w_out, 256 * (c - WOUT), 256))]
    if c < DOWN:
        j, g = (c - UP) // 2, (c - UP) % 2
        return [(0, cols(w_up, D_FF * g + 256 * j, 256))]
    if c < GQ:
        j, kg = (c - DOWN) // 3, (c - DOWN) % 3
        kt = kt_of(c)[0]
        return [(0, w_down[kg * 8 * P:(kg * 8 + kt) * P, 256 * j:256 * j + 256]
                 .rearrange("(k p) n -> p k n", p=P))]
    if c < GA:
        return [(0, cols(gla_in, 256 * (c - GQ), 256))]
    if c == GA:
        return [(0, cols(gla_in, 3072, 16))]
    if c < GOUT:
        return [(0, cols(gla_in, 1024 + 256 * (c - GV), 256))]
    if c < SK:
        return [(0, cols(gla_out, 256 * (c - GOUT), 256))]
    if c < SWA:
        return [(0, cols(w_kv, 256 * (c - SK), 256))]
    if c < SOUT:
        pair, g = (c - SWA) // 4, (c - SWA) % 4
        return [(0, cols(swa_in, 1024 * g + 256 * pair, 256))]
    return [(0, cols(swa_out, 256 * (c - SOUT), 256))]


def build(nc, xT, cols_d, ident_d, rope1_d, rope2_d, amask_d, cmask_d, tri_d, dmask_d, sel_d, rel_d, w_a2_d,
          w_ada, w_in, w_branch, w_out, w_up, w_down, gla_in, gla_out, w_kv, swa_in, swa_out, out_d):
    f32, f32r = mybir.dt.float32, mybir.dt.float32r
    ALU, ACT = mybir.AluOpType, mybir.ActivationFunctionType
    W = (w_in, w_branch, w_out, w_up, w_down, gla_in, gla_out, w_kv, swa_in, swa_out)
    ctx = ExitStack()
    with ctx:
        def sb(name, shape, dt=f32, at=ctx):
            return at.enter_context(nc.sbuf_tensor(name, shape, dt))

        def sem(name):
            return ctx.enter_context(nc.semaphore(name))

        raw = [sb(f"raw{i}", [P, CW]) for i in range(RAW)]
        whi = [sb(f"whi{i}", [P, CW], f32r) for i in range(SPL)]
        wlo = [sb(f"wlo{i}", [P, CW], f32r) for i in range(SPL)]
        hhi = sb("hhi", [P, KT, T], f32r)
        hlo = sb("hlo", [P, KT, T], f32r)
        x = sb("x", [P, KT, T])
        y = sb("y", [P, KT, T])
        sq = sb("sq", [P, KT, T])
        tb = sb("tb", [P, KT, T])
        cols = sb("cols", [P, NCOL])
        ident = sb("ident", [P, P])
        meanw = sb("meanw", [P, P])
        headw = sb("headw", [P, P])
        mod = sb("mod", [P, 48])
        cact = sb("cact", [P, 8])
        ones = sb("ones", [P, 1])
        one = sb("one", [P, 1])
        adasum = sb("adasum", [P, 4, T])
        pcol = sb("pcol", [P, 4, 8])
        bgh = sb("bgh", [P, 24])
        ggh = sb("ggh", [P, 8])
        rstd = sb("rstd", [P, T])
        logvar = sb("logvar", [P, T])

        with ExitStack() as st:
            gates = sb("gates", [P, 24, T], at=st)
            qkv = {n: sb(f"m_{n}", [P, 2, T], at=st) for n in ("qa", "ka", "va", "qb", "kb", "vb", "qc", "qi", "kk")}
            misc = sb("misc", [P, 2, MW], at=st)
            wis = sb("wis", [P, 2, 4], at=st)
            rope1 = sb("rope1", [P, 2, T], at=st)
            amask = sb("amask", [P, 384], at=st)
            cmask = sb("cmask", [P, 384], at=st)
            sel = sb("sel", [4, 512], at=st)
            biasA = sb("biasA", [P, 4, 384], at=st)
            best8 = sb("best8", [P, 8], at=st)
            usc = sb("usc", [P, 2, T], at=st)
            up = sb("up", [P, 3, T], at=st)
            upT = sb("upT", [P, 2, T], at=st)
            unmax = sb("unmax", [P, 4], at=st)
            uden = sb("uden", [P, 4], at=st)
            urec = sb("urec", [P, 4], at=st)
            yhi = sb("yhi", [P, 3, 512], f32r, at=st)
            ylo = sb("ylo", [P, 3, 512], f32r, at=st)
        biasB = tb[:, 0:6, :].rearrange("p a b -> p (a b)").rearrange("p (h n) -> p h n", h=4)
        biasC = tb[:, 6:8, :].rearrange("p a b -> p (a b)")[:, 0:384]
        xsw = sq[:, 0:2, :]
        relu = sq[:, 2:4, :]
        left = sq[:, 4:6, :]
        score = sq[:, 6:8, :].rearrange("p a b -> p (a b)")[:, 0:384]
        gtmp = sq[:, 0:4, :].rearrange("p a b -> p (a b)").rearrange("p (r n) -> p r n", r=2)
        fgate = y[0:4, 0:5, :]
        fones = y[0:4, 5, :]

        with ExitStack() as st:
            uhi = sb("uhi", [P, FT, T], f32r, at=st)
            ulo = sb("ulo", [P, FT, T], f32r, at=st)
            aseq = sb("aseq", [P, 2, 2, T + 2], at=st)
            conv = sb("conv", [P, 2, 2, T], at=st)
            gelu = sb("gelu", [P, 2, 2, T], at=st)

        with ExitStack() as st:
            gq = sb("gq", [P, 4, T], at=st)
            gk = sb("gk", [P, 4, T], at=st)
            alrT = sb("alrT", [16, T], at=st)
            wa2 = sb("wa2", [16, 512], at=st)
            keep = sb("keep", [P, 1024], at=st)
            cum = sb("cum", [P, 1024], at=st)
            ekI = sb("ekI", [P, 2560], at=st)
            qI = sb("qI", [P, 1024], at=st)
            qdec = sb("qdec", [P, 1024], at=st)
            kdec = sb("kdec", [P, 1024], at=st)
            kdT = sb("kdT", [P, 2, 4, P], at=st)
            elast = sb("elast", [P, 16], at=st)
            gv = sb("gv", [P, 2, 1024], at=st)
            gs = sb("gs", [P, KT, T], at=st)
            tri = sb("tri", [P, 64], at=st)
            att = sb("att", [P, 4, 4, 64], at=st)
            state = sb("state", [P, 4, T], at=st)
            gth = sb("gth", [P, 512], at=st)
            grs = ekI[:, 0:1024].rearrange("p (h t) -> p h t", h=4)
        glz = sq[:, 0:4, :].rearrange("p a b -> p (a b)")
        gla = sq[:, 4:8, :].rearrange("p a b -> p (a b)")
        gdf = tb[:, 0:4, :].rearrange("p a b -> p (a b)")
        gdg = tb[:, 4:8, :].rearrange("p a b -> p (a b)")

        with ExitStack() as st:
            sk = sb("sk", [P, 6, T], at=st)
            sv = sb("sv", [P, 2, 768], at=st)
            sqr = sb("sqr", [P, 2, 6, T], at=st)
            sgs = sb("sgs", [P, 2, 2, T], at=st)
            sth = sb("sth", [P, 512], at=st)
            dmask = sb("dmask", [P, 1152], at=st)
            rope2 = sb("rope2", [P, 2, T], at=st)
            dsc = sb("dsc", [P, 2, 768], at=st)
            dp = sb("dp", [P, 2, 768], at=st)
            dpT = sb("dpT", [P, 2, 768], at=st)
            dnmax = sb("dnmax", [P, 4], at=st)
            dden = sb("dden", [P, 4], at=st)
            drec = sb("drec", [P, 4], at=st)
            of = sb("of", [P, 2, P], at=st)
            ohi = sb("ohi", [P, KT, T], f32r, at=st)
            olo = sb("olo", [P, KT, T], f32r, at=st)

        res = [ctx.enter_context(nc.psum_tensor(f"res{i}", [P, 512], f32)) for i in range(NB)]
        pS = ctx.enter_context(nc.psum_tensor("pS", [P, 1024], f32))
        pT = ctx.enter_context(nc.psum_tensor("pT", [P, 1024], f32))
        pX = ctx.enter_context(nc.psum_tensor("pX", [P, 512], f32))
        stat = pX[:, 0:T]
        pmod = pX[:, T:T + 48]
        pO = pT[:, 512:1024]

        raw_full = [sem(f"raw_full{i}") for i in range(RAW)]
        hi_ready, lo_dve, lo_pool = sem("hi_ready"), sem("lo_dve"), sem("lo_pool")
        product_done, drained_act, drained_dve = sem("product_done"), sem("drained_act"), sem("drained_dve")
        drained = {"act": drained_act, "dve": drained_dve}
        ada_full = [sem(f"ada_full{i}") for i in range(4)]
        ada_first, ada_summed, ada_pooled, ada_used, mod_ready = (
            sem(n) for n in ("ada_first", "ada_summed", "ada_pooled", "ada_used", "mod_ready"))
        x_in, const_in, mixc_in, glac_in, swac_in = (sem(n) for n in ("x_in", "const_in", "mixc_in", "glac_in", "swac_in"))
        const_set, cact_ready = sem("const_set"), sem("cact_ready")
        dve_self, act_self, pool_self = sem("dve_self"), sem("act_self"), sem("pool_self")
        NORMS = ("n1", "n2", "n3", "n4", "n5", "n6")
        squares = {n: sem(f"{n}_squares") for n in NORMS}
        mean_known = {n: sem(f"{n}_mean") for n in NORMS}
        dev_known = {n: sem(f"{n}_dev") for n in NORMS}
        rstd_known = {n: sem(f"{n}_rstd") for n in NORMS}
        scaled = {n: sem(f"{n}_scaled") for n in NORMS}
        in_hi = {n: sem(f"{n}_hi") for n in NORMS}
        in_lo = {n: sem(f"{n}_lo") for n in NORMS}
        centered = {n: sem(f"{n}_centered") for n in ("n5", "n6")}
        summed = {n: sem(f"{n}_summed") for n in ("n5", "n6")}
        in_lo_pool = {n: sem(f"{n}_lo_pool") for n in ("n1", "n3", "n5")}
        y_scaled = {n: sem(f"{n}_y_scaled") for n in ("n2", "n4")}
        x_pool = {n: sem(f"{n}_x_pool") for n in ("n2", "n4")}
        x_ready = sem("x_ready")
        moved_half = sem("moved_half")
        sin_done = sem("sin_done")
        roped = sem("roped")
        wis_ready = sem("wis_ready")
        idx_done, idx_relu, idx_acc = sem("idx_done"), sem("idx_relu"), sem("idx_acc")
        fT_done, fz_ready, flog_ready, fcum_ready = sem("fT_done"), sem("fz_ready"), sem("flog_ready"), sem("fcum_ready")
        topk_done = sem("topk_done")
        bB_done, bB_ready = sem("bB_done"), sem("bB_ready")
        qk_done, smax_done, exp_done, norm_done = sem("qk_done"), sem("smax_done"), sem("exp_done"), sem("norm_done")
        tr_done, pT_ready, pv_done, y_hi, y_lo = sem("tr_done"), sem("pT_ready"), sem("pv_done"), sem("y_hi"), sem("y_lo")
        gated, merged, mg_hi, mg_lo = sem("gated"), sem("merged"), sem("mg_hi"), sem("mg_lo")
        a_ready, conv_done, gelu_done, u_full, u_hi, u_lo = (
            sem(n) for n in ("a_ready", "conv_done", "gelu_done", "u_full", "u_hi", "u_lo"))
        la_done, z_ready, loga_ready, cum_ready = (
            sem(n) for n in ("la_done", "z_ready", "loga_ready", "cum_ready"))
        gdiff, gexp, gfac, kd_T, kdT_ready, att_done, att_ready = (
            sem(n) for n in ("gdiff", "gexp", "gfac", "kd_T", "kdT_ready", "att_done", "att_ready"))
        o_done, o_ready, upd_done, state_ready, osq, hmean, hdev, hrstd, gs_ready, gth_ready = (
            sem(n) for n in ("o_done", "o_ready", "upd_done", "state_ready", "osq", "hmean", "hdev", "hrstd", "gs_ready", "gth_ready"))
        go_hi, go_lo, go_full = sem("go_hi"), sem("go_lo"), sem("go_full")
        sv_ready, sg_ready, sth_ready = sem("sv_ready"), sem("sg_ready"), sem("sth_ready")
        d_qk, d_max, d_exp, d_norm, d_tr, d_pT, d_pv, d_of, d_hi, d_lo = (
            sem(f"d_{n}") for n in ("qk", "max", "exp", "norm", "tr", "pT", "pv", "of", "hi", "lo"))
        out_ready, out_stored = sem("out_ready"), sem("out_stored")
        pad_set = sem("pad_set")

        block = ctx.enter_context(nc.Block())

        def col(name, k, n=1):
            a = COLS[name][0] + k
            return cols[:, a:a + n]

        def wait_raw(eng, e):
            i = RAW_OF[e]
            n = sum(16 * (len(pieces(RING[j][1], W)) if RING[j][0] == "w" else 1)
                    for j in range(i % RAW, i + 1, RAW))
            eng.wait_ge(raw_full[i % RAW], n)

        def ada_buffer(a):
            if a not in ADA_AT:
                return raw[RAW_OF["ada", a] % RAW][:, :]
            at = ADA_AT[a]
            return (y if at == "y" else sq if at == "sq" else gates[:, 8 * at:8 * at + 8, :]
                    )[:, :, :].rearrange("p a b -> p (a b)")

        def wait_ada(eng, a):
            if a in ADA_AT:
                eng.wait_ge(ada_full[a % 4], 16 * len([i for i in range(a % 4, a + 1, 4) if i in ADA_AT]))
            else:
                wait_raw(eng, ("ada", a))

        def x_updated(n, i):
            return (x_pool[n], 1) if i == 1 else (scaled[n], max(i, 1))

        @block.sync
        def _(sp):
            sp.dma_start(cols[:, :], cols_d).then_inc(const_in, 16)
            sp.dma_start(ident[:, :], ident_d).then_inc(const_in, 16)
            for kind, n in STREAM:
                if kind == "ada" and n in ADA_AT:
                    if n == 3:
                        for k in range(0, KT, 4):
                            sp.dma_start(x[:, k:k + 4, :], xT[:, k:k + 4, :]).then_inc(x_in, 16)
                    if 8 <= n < 11:
                        sp.wait_ge(ada_used, n - 7)
                    if n >= 11:
                        sp.wait_ge(ada_pooled, n - 10 if n < 14 else n - 9)
                    if n == 16:
                        sp.wait_ge(topk_done, 1)
                    if n == 15:
                        sp.wait_ge(bB_done, 4)
                    if n == 20:
                        sp.wait_ge(scaled["n2"], 3)
                        sp.wait_ge(x_pool["n2"], 1)
                    if n == 21:
                        sp.wait_ge(mean_known["n3"], 1)
                    sp.dma_start(ada_buffer(n).rearrange("p (k n) -> p k n", k=KT),
                                 w_ada[:, 256 * n:256 * n + 256].rearrange("(k p) n -> p k n", p=P)
                                 ).then_inc(ada_full[n % 4], 16)
                    continue
                if (kind, n) == ("w", 1):
                    for dst, src in ((rope1[:, :, :], rope1_d), (amask[:, :], amask_d), (cmask[:, :], cmask_d),
                                     (sel[:, :], sel_d), (biasA[:, :, :], rel_d)):
                        sp.dma_start(dst, src).then_inc(mixc_in, 16)
                i = RAW_OF[kind, n]
                if i >= RAW:
                    before, m = RING[i - RAW]
                    if before == "ada":
                        sp.wait_ge(ada_used, m + 1)
                    else:
                        sp.wait_ge(lo_dve, m + 1)
                        sp.wait_ge(lo_pool, m + 1)
                dst = raw[i % RAW]
                if kind == "ada":
                    sp.dma_start(dst[:, :].rearrange("p (k n) -> p k n", k=KT),
                                 w_ada[:, 256 * n:256 * n + 256].rearrange("(k p) n -> p k n", p=P)
                                 ).then_inc(raw_full[i % RAW], 16)
                else:
                    kt, w = kt_of(n)
                    view = dst[:, 0:kt * w].rearrange("p (k n) -> p k n", k=kt)
                    for at, src in pieces(n, W):
                        sp.dma_start(view[:, :, at:at + src.shape[2]], src).then_inc(raw_full[i % RAW], 16)
            for k in range(KT // 2):
                sp.wait_ge(out_ready, 2 * k + 2)
                sp.dma_start(out_d[:, 2 * k:2 * k + 2, :], x[:, 2 * k:2 * k + 2, :]).then_inc(out_stored, 16)
            sp.wait_ge(out_stored, 16 * (KT // 2))

        def dve_part(c):
            kt, w = kt_of(c)
            if c == QC:
                return kt * w // 2
            if c < WOUT:
                return kt * w * 7 // 8 // 2 * 2
            return kt * w * 3 // 4 // 2 * 2

        @block.gpsimd
        def _(pool):
            pool_count = [0]

            def own(ins):
                ins.then_inc(pool_self, 1)
                pool_count[0] += 1
                pool.wait_ge(pool_self, pool_count[0])

            def low(c):
                if c >= NC:
                    return
                kt, w = kt_of(c)
                a, b = dve_part(c), kt * w
                pool.wait_ge(hi_ready, c + 1)
                if c >= SPL:
                    pool.wait_ge(product_done, CHUNK_MARK[c - SPL])
                nc.gpsimd.tensor_tensor(wlo[c % SPL][:, a:b], raw[RAW_OF["w", c] % RAW][:, a:b],
                                        whi[c % SPL][:, a:b].bitcast(f32), ALU.subtract).then_inc(lo_pool, 1)

            rope_n = [0]

            def sine(c, table):
                if c == QC:
                    pool.wait_ge(mixc_in, 80)
                if c == SK:
                    pool.wait_ge(swac_in, 32)
                pool.wait_ge(moved_half, RH[c])
                nc.gpsimd.tensor_tensor(xsw, xsw, table[:, 1:2, :].to_broadcast([P, 2, T]), ALU.mult).then_inc(sin_done, 1)

            def ada_half(a, second):
                r = ada_buffer(a)
                w = r.rearrange("p (k n) -> p k n", k=KT)
                if not second:
                    wait_ada(pool, a)
                    own(nc.gpsimd.tensor_tensor(w, w, cact[:, :, None].to_broadcast([P, KT, T]), ALU.mult))
                    return
                own(nc.gpsimd.tensor_tensor(r[:, 0:1024], r[:, 0:1024], r[:, 1024:2048], ALU.add))
                own(nc.gpsimd.tensor_tensor(r[:, 0:512], r[:, 0:512], r[:, 512:1024], ALU.add))
                if a < 8:
                    nc.gpsimd.tensor_tensor(tb[:, a, :], r[:, 0:256], r[:, 256:512], ALU.add).then_inc(ada_first, 1)
                    return
                if a >= 12:
                    pool.wait_ge(ada_used, a - 3)
                nc.gpsimd.tensor_tensor(adasum[:, a % 4, :], r[:, 0:256], r[:, 256:512], ALU.add).then_inc(ada_pooled, 1)

            def add_pair(n):
                pool.wait_ge(y_scaled[n], 1)
                a = 2 * PAIRS[1]
                nc.gpsimd.tensor_tensor(x[:, a:a + 2, :], x[:, a:a + 2, :], y[:, a:a + 2, :], ALU.add).then_inc(x_pool[n], 1)

            def split_lo_pool(n, to, bias):
                for k in LO_POOL:
                    pool.wait_ge(scaled[n], k + 1)
                    pool.wait_ge(in_hi[n], k + 1)
                    own(nc.gpsimd.tensor_scalar(to[:, k, :], tb[:, k, :], bias(k), None, ALU.add))
                    nc.gpsimd.tensor_tensor(hlo[:, k, :], to[:, k, :], hhi[:, k, :].bitcast(f32),
                                            ALU.subtract).then_inc(in_lo_pool[n], 1)

            nc.gpsimd.memset(meanw[:, :], 1.0 / D).then_inc(const_set, 1)
            nc.gpsimd.memset(headw[:, :], 1.0 / 256).then_inc(const_set, 1)
            nc.gpsimd.memset(ones[:, :], 1.0).then_inc(const_set, 1)
            pool.wait_ge(cact_ready, 1)
            for a in ADA_GPS:
                ada_half(a, False)
                ada_half(a, True)
            low(0)
            split_lo_pool("n1", tb, lambda i: mod[:, i:i + 1])
            for c in range(1, SPL):
                low(c)
            for c in range(1, NC + 1):
                if BRANCH < c - 1 < WOUT:
                    for j in range(4):
                        n = 4 * (c - 1 - BRANCH) + j
                        pool.wait_ge(gated, n + 1)
                        nc.gpsimd.tensor_tensor(y[:, 2 * j:2 * j + 2, :], y[:, 2 * j:2 * j + 2, :],
                                                gtmp[:, n % 2, :].rearrange("p (a b) -> p a b", a=2), ALU.add
                                                ).then_inc(merged, 1)
                for i, step in enumerate(ADA_STEPS):
                    if step == c - 1:
                        ada_half(8 + i // 2, i % 2)
                if c - 1 not in LATE:
                    low(c + 2)
                if c - 1 == UP - 1:
                    add_pair("n2")
                    split_lo_pool("n3", tb, lambda i: mod[:, 24 + i:25 + i])
                if c - 1 == GQ - 1:
                    add_pair("n4")
                if c - 1 == SK - 1:
                    split_lo_pool("n5", x, lambda i: col("ln_b", i))
                if c - 1 in LATE:
                    low(c + 2)
                if SV <= c - 1 < SWA:
                    pool.wait_ge(scaled["n5"], KT)
                    rest = [i for i in range(KT) if i not in LO_POOL]
                    for k in rest[2 * (c - 1 - SV):2 * (c - 1 - SV) + 2]:
                        nc.gpsimd.tensor_scalar(x[:, k, :], tb[:, k, :], col("ln_b", k), None, ALU.add).then_inc(x_ready, 1)
                if c - 1 <= KK:
                    sine(c - 1, rope1)
                if c - 1 == UP - 1:
                    pool.wait_ge(product_done, CHUNK_MARK[UP - 1])
                    nc.gpsimd.memset(aseq[:, :, :, 0:2], 0.0).then_inc(pad_set, 1)
                if c - 1 == GQ - 1:
                    pool.wait_ge(product_done, CHUNK_MARK[GQ - 1])
                    pool.dma_start(wa2[:, :], w_a2_d).then_inc(glac_in, 16)
                    pool.dma_start(tri[:, :], tri_d).then_inc(glac_in, 16)
                    own(nc.gpsimd.memset(keep[:, :], 1.0))
                    nc.gpsimd.memset(keep[:, :].rearrange("p (n c) -> p n c", c=64)[:, :, 0:1], 0.0).then_inc(pad_set, 1)
                    nc.gpsimd.memset(att[:, :, :, :], 0.0).then_inc(pad_set, 1)
                if c - 1 == SK - 1:
                    pool.wait_ge(product_done, CHUNK_MARK[SK - 1])
                    pool.dma_start(rope2[:, :, :], rope2_d).then_inc(swac_in, 16)
                    pool.dma_start(dmask[:, :], dmask_d).then_inc(swac_in, 16)
                if c - 1 in RH and c - 1 > KK:
                    sine(c - 1, rope2)

        @block.scalar
        def _(act):
            act_count = [0]

            def own(ins):
                ins.then_inc(act_self, 1)
                act_count[0] += 1
                act.wait_ge(act_self, act_count[0])

            def high(c):
                if c >= NC:
                    return
                kt, w = kt_of(c)
                wait_raw(act, ("w", c))
                if c >= SPL:
                    act.wait_ge(product_done, CHUNK_MARK[c - SPL])
                    act.wait_ge(lo_pool, c - SPL + 1)
                    act.wait_ge(lo_dve, c - SPL + 1)
                nc.scalar.activation(whi[c % SPL][:, 0:kt * w], raw[RAW_OF["w", c] % RAW][:, 0:kt * w],
                                     ACT.Copy).then_inc(hi_ready, 1)

            def result(r):
                act.wait_ge(product_done, RESULT_MARK[r])
                return res[r % NB]

            def swap(c, block_rows):
                ps = result(FIRST_RESULT[c])
                if RI[c] > 0:
                    act.wait_ge(roped, RI[c])
                n = P // block_rows
                for i in range(n):
                    a, b = i * block_rows, (i ^ 1) * block_rows
                    nc.scalar.activation(xsw[a:a + block_rows, :, :].rearrange("p a b -> p (a b)"),
                                         ps[b:b + block_rows, :], ACT.Copy).then_inc(moved_half, 1)

            def norm_dev(n, eps):
                own(nc.scalar.activation(one[:, :], col("eps5", 0), ACT.Ln))
                act.wait_ge(mean_known[n], 2 if n in centered else 1)
                nc.scalar.activation(logvar[:, :], stat, ACT.Ln, bias=col(eps, 0)).then_inc(dev_known[n], 1)
                act.wait_ge(dev_known[n], 1)
                nc.scalar.activation(rstd[:, :], logvar[:, :], ACT.Exp, scale=-0.5).then_inc(rstd_known[n], 1)

            def split_hi(n, src, bias=None, first=0):
                for k in range(KT):
                    act.wait_ge(scaled[n], first + k + 1)
                    if bias is None:
                        nc.scalar.activation(hhi[:, k, :], src[:, k, :], ACT.Copy).then_inc(in_hi[n], 1)
                    else:
                        nc.scalar.activation(hhi[:, k, :], src[:, k, :], ACT.Identity, bias=bias(k)).then_inc(in_hi[n], 1)

            act.wait_ge(const_in, 32)
            nc.scalar.activation(cact[:, :], col("c", 0, 8), ACT.Silu).then_inc(cact_ready, 1)
            act.wait_ge(x_in, 32)
            for k in range(KT):
                nc.scalar.activation(sq[:, k, :], x[:, k, :], ACT.Square).then_inc(squares["n1"], 1)
            norm_dev("n1", "eps6")
            high(0)
            split_hi("n1", tb, lambda k: mod[:, k:k + 1])
            for c in range(1, SPL):
                high(c)

            TAIL = 3
            for c in range(1, NC + 1):
                b = c - 1
                if b == GA:
                    ps = result(FIRST_RESULT[b])
                    nc.scalar.activation(alrT[:, :], ps[0:16, 0:T], ACT.Copy).then_inc(drained_act, 1)
                if b not in LATE:
                    high(c + 2)
                if b <= KK:
                    swap(b, 32)
                elif b < ZG:
                    ps = result(FIRST_RESULT[b])
                    if b == MISC:
                        for t in range(2):
                            nc.scalar.activation(misc[:, t, :], ps[:, t * 256:t * 256 + MW], ACT.Copy
                                                 ).then_inc(drained_act if t else act_self, 1)
                        act_count[0] += 1
                    else:
                        dst = qkv[("qa", "ka", "va", "qb", "kb", "vb")[b - QA]]
                        nc.scalar.activation(dst[:, :, :].rearrange("p a b -> p (a b)"), ps[:, :], ACT.Copy
                                             ).then_inc(drained_act, 1)
                    if QA <= b < QA + 4:
                        for e in (2 * (b - QA), 2 * (b - QA) + 1):
                            nk = P * (e // 4 + 1)
                            act.wait_ge(idx_done, e + 1)
                            if e == 0:
                                act.wait_ge(roped, 3)
                            if e >= 2:
                                act.wait_ge(idx_acc, e - 1)
                            nc.scalar.activation(relu[:, e % 2, 0:nk], pS[:, 512 * (e % 2):512 * (e % 2) + nk],
                                                 ACT.Relu, scale=0.125).then_inc(idx_relu, 1)
                    if b == VA:
                        act.wait_ge(fz_ready, 1)
                        own(nc.scalar.activation(fgate[:, 1, :], fgate[:, 0, :], ACT.Abs))
                        own(nc.scalar.activation(fgate[:, 2, :], fgate[:, 1, :], ACT.Exp, scale=-1.0))
                        nc.scalar.activation(fgate[:, 3, :], fgate[:, 2, :], ACT.Ln, bias=1.0).then_inc(flog_ready, 1)
                elif b < BRANCH:
                    ps = result(FIRST_RESULT[b])
                    if b == ZG:
                        act.wait_ge(ada_pooled, 6)
                    if b == ZG + 4:
                        act.wait_ge(ada_pooled, 7)
                    for i in range(2):
                        n = 2 * (b - ZG) + i
                        nc.scalar.activation(gates[:, n, :], ps[:, i * T:i * T + T], ACT.Tanh,
                                             bias=bgh[:, n:n + 1], scale=0.5).then_inc(drained_act if i else act_self, 1)
                    act_count[0] += 1

                def unit_slot(s):
                    if s % 8 == 3 and s > 8:
                        m = s // 8 - 1
                        act.wait_ge(pv_done, 8 * m + 8)
                        nc.scalar.activation(yhi[:, m, :], pO, ACT.Copy).then_inc(y_hi, 1)
                    if s < 24:
                        t = s % 8 // 4
                        nk = P * (t + 1)
                        act.wait_ge(smax_done, s + 1)
                        if s >= 3:
                            act.wait_ge(tr_done, s - 2)
                        nc.scalar.activation(up[:, s % 3, 0:nk], usc[:, s % 2, 0:nk], ACT.Exp, scale=-1.0,
                                             bias=unmax[:, s % 4:s % 4 + 1],
                                             accum_out=uden[:, s % 4:s % 4 + 1]).then_inc(exp_done, 1)
                    u = s - 2
                    if 0 <= u < 24:
                        nk = P * (u % 8 // 4 + 1)
                        act.wait_ge(tr_done, u + 1)
                        if u >= 2:
                            act.wait_ge(pv_done, u - 1)
                        nc.scalar.activation(upT[:, u % 2, 0:nk], pT[:, 256 * (u % 2):256 * (u % 2) + nk], ACT.Copy
                                             ).then_inc(pT_ready, 1)

                if ZG <= c < BRANCH:
                    unit_slot(2 * (c - ZG))
                    unit_slot(2 * (c - ZG) + 1)
                if c == BRANCH:
                    for s in (24, 25, 26, 27):
                        unit_slot(s)
                if b == WOUT - 1:
                    for j in range(4):
                        act.wait_ge(merged, 5 + j)
                        nc.scalar.activation(hhi[:, 2 * j:2 * j + 2, :], y[:, 2 * j:2 * j + 2, :], ACT.Copy, scale=0.5
                                             ).then_inc(mg_hi, 1)
                if WOUT <= b < UP:
                    j = b - WOUT
                    ps = result(FIRST_RESULT[b])
                    nc.scalar.activation(sq[:, 2 * j:2 * j + 2, :].rearrange("p a b -> p (a b)"), ps[:, :], ACT.Square
                                         ).then_inc(squares["n2"], 1)
                    act.wait_ge(mg_lo, 4)
                    nc.scalar.activation(y[:, 2 * j:2 * j + 2, :].rearrange("p a b -> p (a b)"), ps[:, :], ACT.Copy
                                         ).then_inc(drained_act, 1)
                if b == UP - 1:
                    norm_dev("n2", "eps6")
                    for i, j in enumerate(PAIRS):
                        act.wait_ge(*x_updated("n2", i))
                        nc.scalar.activation(sq[:, 2 * j:2 * j + 2, :], x[:, 2 * j:2 * j + 2, :], ACT.Square
                                             ).then_inc(squares["n3"], 1)
                    norm_dev("n3", "eps6")
                    split_hi("n3", tb, lambda k: mod[:, 24 + k:25 + k])
                if UP <= b < DOWN:
                    j = (b - UP) // 2
                    if (b - UP) % 2 == 0:
                        ps = result(FIRST_RESULT[b])
                        if j == 0:
                            act.wait_ge(pad_set, 1)
                        if j >= 2:
                            act.wait_ge(conv_done, j - 1)
                        nc.scalar.activation(aseq[:, j % 2, :, 2:T + 2], ps[:, :].rearrange("p (a b) -> p a b", a=2),
                                             ACT.Copy).then_inc(drained_act, 1)
                    else:
                        act.wait_ge(conv_done, j + 1)
                        if j >= 2:
                            act.wait_ge(u_lo, j - 1)
                        nc.scalar.activation(gelu[:, j % 2, :, :], conv[:, j % 2, :, :], ACT.Gelu_apprx_tanh
                                             ).then_inc(gelu_done, 1)
                        act.wait_ge(u_full, j + 1)
                        nc.scalar.activation(uhi[:, 2 * j:2 * j + 2, :], gelu[:, j % 2, :, :], ACT.Copy).then_inc(u_hi, 1)
                if DOWN <= b < GQ and (b - DOWN) % 3 == 2:
                    j = (b - DOWN) // 3
                    if j == 0:
                        act.wait_ge(ada_pooled, 16)
                    for i in range(2):
                        ps = result(FIRST_RESULT[b] + i)
                        nc.scalar.activation(sq[:, 2 * j + i, :], ps[:, 0:T], ACT.Square).then_inc(squares["n4"], 1)
                        nc.scalar.activation(y[:, 2 * j + i, :], ps[:, 0:T], ACT.Copy).then_inc(drained_act, 1)
                if b == GQ - 1:
                    norm_dev("n4", "eps6")
                    for i, j in enumerate(PAIRS):
                        act.wait_ge(*x_updated("n4", i))
                        nc.scalar.activation(hhi[:, 2 * j:2 * j + 2, :], x[:, 2 * j:2 * j + 2, :], ACT.Copy
                                             ).then_inc(in_hi["n4"], 1)
                if GQ <= b < GA:
                    j = (b - GQ) % 2
                    ps = result(FIRST_RESULT[b])
                    dst = gq if b < GK else gk
                    nc.scalar.activation(dst[:, 2 * j:2 * j + 2, :].rearrange("p a b -> p (a b)"), ps[:, :], ACT.Copy,
                                         scale=P ** -0.5 if b < GK else 1.0).then_inc(drained_act, 1)
                if b == GA:
                    act.wait_ge(z_ready, 4)
                    own(nc.scalar.activation(gla, glz, ACT.Abs))
                    own(nc.scalar.activation(gla, gla, ACT.Exp, scale=-1.0))
                    nc.scalar.activation(gla, gla, ACT.Ln, bias=1.0).then_inc(loga_ready, 1)
                if GV <= b < GG:
                    j = b - GV
                    ps = result(FIRST_RESULT[b])
                    nc.scalar.activation(gv[:, :, 256 * j:256 * j + 256], ps[:, :].rearrange("p (t n) -> p t n", t=2),
                                         ACT.Copy).then_inc(drained_act, 1)
                if b == GV:
                    act.wait_ge(cum_ready, 1)
                    nc.scalar.activation(qdec[:, :], cum[:, :], ACT.Exp, scale=1.0 / 16).then_inc(gexp, 1)
                    nc.scalar.activation(elast[:, :], cum[:, :].rearrange("p (n c) -> p n c", c=64)[:, :, 63],
                                         ACT.Exp, scale=1.0 / 16).then_inc(gexp, 1)
                    act.wait_ge(gdiff, 1)
                    nc.scalar.activation(kdec[:, :], gdf, ACT.Exp, scale=1.0 / 16).then_inc(gexp, 1)
                    act.wait_ge(gdiff, 2)
                    nc.scalar.activation(qI[:, :], gdg, ACT.Exp, scale=1.0 / 16).then_inc(gexp, 1)
                if b == GV + 1:
                    act.wait_ge(gdiff, 6)
                    nc.scalar.activation(ekI[:, :], ekI[:, :], ACT.Exp, scale=1.0 / 16).then_inc(gexp, 1)
                if b == GV + 3:
                    for t in range(2):
                        act.wait_ge(kd_T, 4 * t + 4)
                        nc.scalar.activation(kdT[:, t, :, :].rearrange("p h n -> p (h n)"), pT[:, 512 * t:512 * t + 512],
                                             ACT.Copy).then_inc(kdT_ready, 1)
                if GG <= b < GOUT:
                    j = b - GG
                    ps = result(FIRST_RESULT[b])
                    if j:
                        act.wait_ge(gs_ready, j)
                    nc.scalar.activation(gth[:, :], ps[:, :], ACT.Tanh, scale=0.5).then_inc(gth_ready, 1)
                    for i in range(2):
                        nc.scalar.activation(gs[:, 2 * j + i, :], ps[:, i * T:i * T + T], ACT.Copy,
                                             scale=ggh[:, 2 * j + i:2 * j + i + 1]
                                             ).then_inc(drained_act if i else act_self, 1)
                    act_count[0] += 1
                    act.wait_ge(o_done, j + 1)
                    nc.scalar.activation(y[:, :, 64 * j:64 * j + 64], pS[:, 512 * (j % 2):512 * (j % 2) + 512]
                                         .rearrange("p (n i) -> p n i", n=8), ACT.Copy).then_inc(act_self, 1)
                    nc.scalar.activation(sq[:, :, 64 * j:64 * j + 64], pS[:, 512 * (j % 2):512 * (j % 2) + 512]
                                         .rearrange("p (n i) -> p n i", n=8), ACT.Square).then_inc(o_ready, 1)
                    act_count[0] += 1
                    act.wait_ge(act_self, act_count[0])
                    act.wait_ge(o_ready, j + 1)
                if b == GOUT - 1:
                    own(nc.scalar.activation(one[:, :], col("eps5", 0), ACT.Ln))
                    for i in range(2):
                        act.wait_ge(hmean, 2 * i + 2)
                        g = grs[:, 2 * i:2 * i + 2, :].rearrange("p h t -> p (h t)")
                        nc.scalar.activation(g, pS[:, 512 * i:512 * i + 512], ACT.Ln, bias=col("eps5", 0)).then_inc(hdev, 1)
                    for i in range(2):
                        act.wait_ge(hdev, i + 1)
                        g = grs[:, 2 * i:2 * i + 2, :].rearrange("p h t -> p (h t)")
                        nc.scalar.activation(g, g, ACT.Exp, scale=-0.5).then_inc(hrstd, 1)
                    for j in range(4):
                        act.wait_ge(go_full, j + 1)
                        nc.scalar.activation(hhi[:, 2 * j:2 * j + 2, :], y[:, 2 * j:2 * j + 2, :], ACT.Copy).then_inc(go_hi, 1)
                if b in (SK - 1, NC - 1):
                    n = "n5" if b == SK - 1 else "n6"
                    for j in range(4):
                        act.wait_ge(centered[n], j + 1)
                        nc.scalar.activation(sq[:, 2 * j:2 * j + 2, :], tb[:, 2 * j:2 * j + 2, :], ACT.Square
                                             ).then_inc(squares[n], 1)
                    norm_dev(n, "eps5")
                    if n == "n5":
                        split_hi(n, tb, lambda k: col("ln_b", k))
                    else:
                        for k in range(KT):
                            act.wait_ge(scaled[n], k + 1)
                            nc.scalar.activation(x[:, k, :], tb[:, k, :], ACT.Identity, bias=col("ln_b", 8 + k)
                                                 ).then_inc(out_ready, 1)
                if b in RH and b > KK:
                    swap(b, 64)
                if SV <= b < SWA:
                    j = b - SV
                    ps = result(FIRST_RESULT[b])
                    nc.scalar.activation(sv[:, :, 256 * j:256 * j + 256], ps[:, :].rearrange("p (t n) -> p t n", t=2),
                                         ACT.Copy).then_inc(drained_act, 1)
                if SWA <= b < SOUT and (b - SWA) % 4 == 3:
                    pair = (b - SWA) // 4
                    ps = result(FIRST_RESULT[b])
                    if pair:
                        act.wait_ge(sg_ready, pair)
                    nc.scalar.activation(sth[:, :], ps[:, :], ACT.Tanh, scale=0.5).then_inc(sth_ready, 1)
                    if pair >= 2:
                        act.wait_ge(d_of, 4 * pair - 4)
                    nc.scalar.activation(sgs[:, pair % 2, :, :].rearrange("p a b -> p (a b)"), ps[:, :], ACT.Copy,
                                         scale=0.5).then_inc(drained_act, 1)

                def dil_slot(s):
                    if 0 <= s < 16:
                        n = 384 * (s % 2 + 1)
                        act.wait_ge(d_max, s + 1)
                        if s >= 2:
                            act.wait_ge(d_tr, s - 1)
                        nc.scalar.activation(dp[:, s % 2, 0:n], dsc[:, s % 2, 0:n], ACT.Exp, scale=-1.0,
                                             bias=dnmax[:, s % 4:s % 4 + 1],
                                             accum_out=dden[:, s % 4:s % 4 + 1]).then_inc(d_exp, 1)
                    u = s - 1
                    if 0 <= u < 16:
                        n = 384 * (u % 2 + 1)
                        act.wait_ge(d_tr, u + 1)
                        if u >= 2:
                            act.wait_ge(d_pv, u - 1)
                        nc.scalar.activation(dpT[:, u % 2, 0:n], pT[:, 0:n], ACT.Copy).then_inc(d_pT, 1)
                    u = s - 2
                    if 0 <= u < 16:
                        h, t = u // 2, u % 2
                        act.wait_ge(d_of, u + 1)
                        nc.scalar.activation(ohi[:, h, t * P:t * P + P], of[:, u % 2, :], ACT.Copy).then_inc(d_hi, 1)

                if SWA + 4 <= c < SOUT:
                    dil_slot(c - SWA - 4)
                if c == SOUT:
                    for s in range(12, 18):
                        dil_slot(s)
                if b in LATE:
                    high(c + 2)

        @block.vector
        def _(dve):
            dve_count = [0]

            def own(ins):
                ins.then_inc(dve_self, 1)
                dve_count[0] += 1
                dve.wait_ge(dve_self, dve_count[0])

            def low(c):
                if c >= NC:
                    return
                b = dve_part(c)
                dve.wait_ge(hi_ready, c + 1)
                if c >= SPL:
                    dve.wait_ge(product_done, CHUNK_MARK[c - SPL])
                nc.vector.tensor_tensor(wlo[c % SPL][:, 0:b], raw[RAW_OF["w", c] % RAW][:, 0:b],
                                        whi[c % SPL][:, 0:b].bitcast(f32), ALU.subtract).then_inc(lo_dve, 1)

            def result(r):
                dve.wait_ge(product_done, RESULT_MARK[r])
                return res[r % NB]

            def mod_cols(a):
                first = 0 if a == 7 else 2 * a - 2
                dve.wait_ge(ada_used, a + 1)
                nc.vector.tensor_tensor(mod[:, first:2 * a + 2], pmod[:, first:2 * a + 2],
                                        col("b_ada", first, 2 * a + 2 - first), ALU.add).then_inc(mod_ready, 1)

            def ada_sum(a):
                wait_ada(dve, a)
                w = ada_buffer(a).rearrange("p (k n) -> p k n", k=KT)
                acc = tb[:, a, :]
                own(nc.vector.tensor_scalar(acc, w[:, 0, :], cact[:, 0:1], None, ALU.mult))
                for k in range(1, ada_dve(a)):
                    ins = nc.vector.scalar_tensor_tensor(acc, w[:, k, :], cact[:, k:k + 1], acc, ALU.mult, ALU.add)
                    if k < ada_dve(a) - 1:
                        own(ins)
                    else:
                        ins.then_inc(ada_summed, 1)

            def norm_rstd(n):
                dve.wait_ge(rstd_known[n], 1)

            def split_lo(n, src, bias=None, k_range=range(KT)):
                for k in k_range:
                    dve.wait_ge(in_hi[n], k + 1)
                    hi = hhi[:, k, :].bitcast(f32)
                    if bias is None:
                        nc.vector.tensor_tensor(hlo[:, k, :], src[:, k, :], hi, ALU.subtract).then_inc(in_lo[n], 1)
                    else:
                        nc.vector.scalar_tensor_tensor(hlo[:, k, :], src[:, k, :], bias(k), hi, ALU.add, ALU.subtract
                                                       ).then_inc(in_lo[n], 1)

            def go_low(j):
                dve.wait_ge(go_hi, j + 1)
                nc.vector.tensor_tensor(hlo[:, 2 * j:2 * j + 2, :], y[:, 2 * j:2 * j + 2, :],
                                        hhi[:, 2 * j:2 * j + 2, :].bitcast(f32), ALU.subtract).then_inc(go_lo, 1)

            def low_pair(i):
                j = PAIRS[i]
                dve.wait_ge(*x_updated("n4", i))
                dve.wait_ge(in_hi["n4"], i + 1)
                nc.vector.tensor_tensor(hlo[:, 2 * j:2 * j + 2, :], x[:, 2 * j:2 * j + 2, :],
                                        hhi[:, 2 * j:2 * j + 2, :].bitcast(f32), ALU.subtract).then_inc(in_lo["n4"], 1)

            def scale_split(n, which, shift):
                for k in range(KT + 1):
                    if k < KT:
                        nc.vector.scalar_tensor_tensor(tb[:, k, :], x[:, k, :], pcol[:, which, k:k + 1], rstd[:, :],
                                                       ALU.mult, ALU.mult).then_inc(scaled[n], 1)
                    if k and k - 1 not in LO_POOL:
                        split_lo(n, tb, lambda i: mod[:, shift + i:shift + i + 1], range(k - 1, k))

            def rope(c, dst, table):
                ps = result(FIRST_RESULT[c])
                dve.wait_ge(moved_half, RH[c])
                nc.vector.tensor_tensor(dst, ps[:, :].rearrange("p (a b) -> p a b", a=2),
                                        table[:, 0:1, :].to_broadcast([P, 2, T]), ALU.mult).then_inc(drained_dve, 1)
                dve.wait_ge(drained_dve, RESULT_DRAIN[FIRST_RESULT[c]][1])
                dve.wait_ge(sin_done, RI[c] + 1)
                nc.vector.tensor_tensor(dst, dst, xsw, ALU.add).then_inc(roped, 1)

            def topk_round(t, i):
                nk, a = P * (t + 1), P * t
                src = score[:, a:a + nk] if i == 0 else left[:, (i + 1) % 2, 0:nk]
                own(nc.vector.max(best8[:, :], src))
                own(nc.vector.match_replace(left[:, i % 2, 0:nk], best8[:, :], src, TAKEN))
                if i == 7:
                    own(nc.vector.tensor_scalar(biasC[:, a:a + nk], left[:, 1, 0:nk], -2.0e38, NEG, ALU.is_gt, ALU.mult))

            def idx_sum(e):
                t, h = e // 4, e % 4
                nk, a = P * (t + 1), P * t
                dve.wait_ge(idx_relu, e + 1)
                if h == 0:
                    nc.vector.tensor_scalar(score[:, a:a + nk], relu[:, e % 2, 0:nk], wis[:, t, h:h + 1], None, ALU.mult
                                            ).then_inc(idx_acc, 1)
                else:
                    dve.wait_ge(idx_acc, e)
                    nc.vector.scalar_tensor_tensor(score[:, a:a + nk], relu[:, e % 2, 0:nk], wis[:, t, h:h + 1],
                                                   score[:, a:a + nk], ALU.mult, ALU.add).then_inc(idx_acc, 1)
                if h == 3:
                    dve.wait_ge(idx_acc, e + 1)
                    own(nc.vector.tensor_tensor(score[:, a:a + nk], score[:, a:a + nk], amask[:, a:a + nk], ALU.add))

            dve.wait_ge(const_in, 32)
            own(nc.vector.tensor_scalar(bgh[:, :], col("b_gate", 0, 24), 0.5, None, ALU.mult))
            own(nc.vector.tensor_scalar(ggh[:, :], col("gla_g", 0, 8), 0.5, None, ALU.mult))
            dve.wait_ge(cact_ready, 1)
            for a in range(len(ADA_GPS), 8):
                ada_sum(a)
            norm_rstd("n1")
            low(0)
            mod_cols(7)
            dve.wait_ge(mod_ready, 1)
            own(nc.vector.scalar_tensor_tensor(pcol[:, 0, :], mod[:, 8:16], 1.0, col("norm_g", 0, 8), ALU.add, ALU.mult))
            scale_split("n1", 0, 0)
            own(nc.vector.memset(fones, 1.0))
            for c in range(1, SPL):
                low(c)

            for c in range(1, NC + 1):
                b = c - 1
                if BRANCH <= b < WOUT:
                    for j in range(4):
                        n = 4 * (b - BRANCH) + j
                        ps = result(FIRST_RESULT[b] + j)
                        if n == 0:
                            dve.wait_ge(drained_act, RESULT_DRAIN[FIRST_RESULT[BRANCH - 1]][1])
                            dve.wait_ge(ada_pooled, 12)
                        if b == BRANCH:
                            dst = y[:, 2 * j:2 * j + 2, :].rearrange("p a b -> p (a b)")
                        else:
                            dst = gtmp[:, n % 2, :]
                            if n >= 6:
                                dve.wait_ge(merged, n - 5)
                        g = 8 * (b - BRANCH) + 2 * j
                        nc.vector.scalar_tensor_tensor(dst, gates[:, g:g + 2, :].rearrange("p a b -> p (a b)"), 1.0,
                                                       ps[:, :], ALU.add, ALU.mult).then_inc(gated, 1)
                        dve.wait_ge(gated, n + 1)
                        nc.vector.engine_nop().then_inc(drained_dve, 1)
                if b not in LATE:
                    low(c + 2)
                if b - 1 in ADA_USE:
                    mod_cols(ADA_USE[b - 1] + 1)
                if b == QC:
                    dve.wait_ge(mixc_in, 80)
                if b <= KK:
                    rope(b, qkv[("qc", "qi", "kk")[b]][:, :, :], rope1)
                if b == MISC:
                    for h in range(4):
                        own(nc.vector.scalar_tensor_tensor(biasA[:, h, :], biasA[:, h, :], 8.0, amask[:, :],
                                                           ALU.mult, ALU.add))
                    dve.wait_ge(drained_act, RESULT_DRAIN[FIRST_RESULT[MISC]][1])
                    nc.vector.tensor_scalar(wis[:, :, :], misc[:, :, 68:72], 0.5, None, ALU.mult).then_inc(wis_ready, 1)
                    dve.wait_ge(wis_ready, 1)
                if QA <= b < QA + 4:
                    idx_sum(2 * (b - QA))
                    idx_sum(2 * (b - QA) + 1)
                if b == KA:
                    dve.wait_ge(fT_done, 2)
                    nc.vector.tensor_scalar(fgate[:, 0, :], pT[0:4, 0:T], cols[0:4, COLS["b_forget"][0]:COLS["b_forget"][1]],
                                            None, ALU.add).then_inc(fz_ready, 1)
                    for i in range(8):
                        topk_round(0, i)
                if b == QB:
                    dve.wait_ge(flog_ready, 1)
                    own(nc.vector.scalar_tensor_tensor(fgate[:, 3, :], fgate[:, 0, :], 0.0, fgate[:, 3, :],
                                                       ALU.min, ALU.subtract))
                    nc.vector.tensor_tensor_scan(fgate[:, 4, :], fones, fgate[:, 3, :], 0.0, ALU.mult, ALU.add
                                                 ).then_inc(fcum_ready, 1)
                    for i in range(4):
                        topk_round(1, i)
                if b in (KB, VB):
                    for h in ((0, 1) if b == KB else (2, 3)):
                        dve.wait_ge(bB_done, h + 1)
                        ps = pS[:, 512 * (h % 2):512 * (h % 2) + T]
                        own(nc.vector.tensor_tensor(biasB[:, h, 0:P], ps[:, 0:P], cmask[:, 0:P], ALU.add))
                        nc.vector.tensor_tensor(biasB[:, h, P:384], ps, cmask[:, P:384], ALU.add).then_inc(bB_ready, 1)
                    if b == VB:
                        dve.wait_ge(bB_ready, 4)

                def unit_slot(s):
                    if s % 8 == 3 and s > 8:
                        m = s // 8 - 1
                        dve.wait_ge(y_hi, m + 1)
                        nc.vector.tensor_tensor(ylo[:, m, :], pO, yhi[:, m, :].bitcast(f32), ALU.subtract).then_inc(y_lo, 1)
                    if s < 24:
                        m, t, h = s // 8, s % 8 // 4, s % 4
                        nk, a = P * (t + 1), P * t
                        bias = (biasA[:, h, a:a + nk], biasB[:, h, a:a + nk], biasC[:, a:a + nk])[m]
                        dve.wait_ge(qk_done, s + 1)
                        if s >= 2:
                            dve.wait_ge(exp_done, s - 1)
                        nc.vector.tensor_tensor_reduce(out=usc[:, s % 2, 0:nk], in0=pS[:, 512 * (s % 2):512 * (s % 2) + nk],
                                                       in1=bias, op0=ALU.add, op1=ALU.min, scale=-0.125, scalar=3.0e38,
                                                       accum_out=unmax[:, s % 4:s % 4 + 1]).then_inc(smax_done, 1)
                    u = s - 1
                    if 0 <= u < 24:
                        nk = P * (u % 8 // 4 + 1)
                        dve.wait_ge(exp_done, u + 1)
                        own(nc.vector.reciprocal(urec[:, u % 4:u % 4 + 1], uden[:, u % 4:u % 4 + 1]))
                        nc.vector.tensor_scalar(up[:, u % 3, 0:nk], up[:, u % 3, 0:nk], urec[:, u % 4:u % 4 + 1],
                                                None, ALU.mult).then_inc(norm_done, 1)

                if ZG <= c < BRANCH:
                    unit_slot(2 * (c - ZG))
                    unit_slot(2 * (c - ZG) + 1)
                if b in (ZG, ZG + 1):
                    for i in range(4 + 2 * (b - ZG), 6 + 2 * (b - ZG)):
                        topk_round(1, i)
                    if b == ZG + 1:
                        nc.vector.engine_nop().then_inc(topk_done, 1)
                if c == BRANCH:
                    for s in (24, 25, 26, 27):
                        unit_slot(s)
                if b == WOUT - 1:
                    for j in range(4):
                        dve.wait_ge(mg_hi, j + 1)
                        nc.vector.scalar_tensor_tensor(hlo[:, 2 * j:2 * j + 2, :], y[:, 2 * j:2 * j + 2, :], 0.5,
                                                       hhi[:, 2 * j:2 * j + 2, :].bitcast(f32), ALU.mult, ALU.subtract
                                                       ).then_inc(mg_lo, 1)
                if b == UP - 2:
                    dve.wait_ge(mod_ready, 7)
                    own(nc.vector.tensor_tensor(pcol[:, 1, :], mod[:, 16:24], col("norm_g", 8, 8), ALU.mult))
                    own(nc.vector.scalar_tensor_tensor(pcol[:, 2, :], mod[:, 32:40], 1.0, col("norm_g", 16, 8),
                                                       ALU.add, ALU.mult))
                if b == UP - 1 or b == GQ - 1:
                    n, which = ("n2", 1) if b == UP - 1 else ("n4", 3)
                    norm_rstd(n)
                    dve.wait_ge(drained_act, RESULT_DRAIN[FIRST_RESULT[b] + results_of(b) - 1][1])
                    for i, j in enumerate(PAIRS):
                        for k in (2 * j, 2 * j + 1):
                            ins = nc.vector.scalar_tensor_tensor(y[:, k, :], y[:, k, :], pcol[:, which, k:k + 1], rstd[:, :],
                                                                 ALU.mult, ALU.mult)
                            if i == 1 and k % 2:
                                ins.then_inc(y_scaled[n], 1)
                            else:
                                own(ins)
                        if i != 1:
                            nc.vector.tensor_tensor(x[:, 2 * j:2 * j + 2, :], x[:, 2 * j:2 * j + 2, :],
                                                    y[:, 2 * j:2 * j + 2, :], ALU.add).then_inc(scaled[n], 1)
                        if n == "n4" and i == 2:
                            low_pair(0)
                    if n == "n4":
                        for i in (1, 2, 3):
                            low_pair(i)
                if b == UP - 1:
                    norm_rstd("n3")
                    scale_split("n3", 2, 24)
                if UP <= b < DOWN:
                    j = (b - UP) // 2
                    if (b - UP) % 2 == 0:
                        dve.wait_ge(drained_act, RESULT_DRAIN[FIRST_RESULT[b]][1])
                        if j >= 2:
                            dve.wait_ge(gelu_done, j - 1)
                        for i in range(2):
                            f = 2 * j + i
                            a, o = aseq[:, j % 2, i, :], conv[:, j % 2, i, :]
                            own(nc.vector.tensor_scalar(o, a[:, 0:T], col("conv_w", f), col("conv_b", f), ALU.mult, ALU.add))
                            own(nc.vector.scalar_tensor_tensor(o, a[:, 1:T + 1], col("conv_w", FT + f), o, ALU.mult, ALU.add))
                            ins = nc.vector.scalar_tensor_tensor(o, a[:, 2:T + 2], col("conv_w", 2 * FT + f), o,
                                                                 ALU.mult, ALU.add)
                            if i:
                                ins.then_inc(conv_done, 1)
                            else:
                                own(ins)
                    else:
                        ps = result(FIRST_RESULT[b])
                        dve.wait_ge(gelu_done, j + 1)
                        g = gelu[:, j % 2, :, :].rearrange("p a b -> p (a b)")
                        nc.vector.tensor_tensor(g, g, ps[:, :], ALU.mult).then_inc(drained_dve, 1)
                        dve.wait_ge(drained_dve, RESULT_DRAIN[FIRST_RESULT[b]][1])
                        nc.vector.engine_nop().then_inc(u_full, 1)
                        dve.wait_ge(u_hi, j + 1)
                        nc.vector.tensor_tensor(ulo[:, 2 * j:2 * j + 2, :], gelu[:, j % 2, :, :],
                                                uhi[:, 2 * j:2 * j + 2, :].bitcast(f32), ALU.subtract).then_inc(u_lo, 1)
                if b == DOWN:
                    dve.wait_ge(mod_ready, 9)
                    own(nc.vector.tensor_tensor(pcol[:, 3, :], mod[:, 40:48], col("norm_g", 24, 8), ALU.mult))
                if b == GV - 1:
                    for h in range(4):
                        dve.wait_ge(la_done, 4)
                        nc.vector.tensor_scalar(glz[:, h * T:h * T + T], pS[:, h * T:h * T + T], col("b_a2", h), None,
                                                ALU.add).then_inc(z_ready, 1)
                    dve.wait_ge(z_ready, 4)
                if b == GV - 1:
                    dve.wait_ge(loga_ready, 1)
                    dve.wait_ge(pad_set, 3)
                    own(nc.vector.scalar_tensor_tensor(glz, glz, 0.0, gla, ALU.min, ALU.subtract))
                    nc.vector.tensor_tensor_scan(cum[:, :], keep[:, :], glz, 0.0, ALU.mult, ALU.add).then_inc(cum_ready, 1)
                    dve.wait_ge(cum_ready, 1)
                    cc = cum[:, :].rearrange("p (n c) -> p n c", c=64)
                    nc.vector.tensor_tensor(gdf.rearrange("p (n c) -> p n c", c=64),
                                            cc[:, :, 63:64].to_broadcast([P, 16, 64]), cc, ALU.subtract).then_inc(gdiff, 1)
                    cs = cum[:, :].rearrange("p (n c) -> p n c", c=16)
                    nc.vector.tensor_tensor(gdg.rearrange("p (n c) -> p n c", c=16), cs,
                                            cs[:, :, 7:8].to_broadcast([P, 64, 16]), ALU.subtract).then_inc(gdiff, 1)
                    for i in range(4):
                        n, a = 16 * (i + 1), EK[i]
                        nc.vector.tensor_tensor(ekI[:, a:a + 16 * n].rearrange("p (m c) -> p m c", c=n),
                                                cc[:, :, 16 * i + 7:16 * i + 8].to_broadcast([P, 16, n]),
                                                cc[:, :, 0:n], ALU.subtract).then_inc(gdiff, 1)
                if b == GV:
                    fq = gq[:, :, :].rearrange("p h t -> p (h t)")
                    fk = gk[:, :, :].rearrange("p h t -> p (h t)")
                    dve.wait_ge(gexp, 3)
                    nc.vector.tensor_tensor(kdec[:, :], kdec[:, :], fk, ALU.mult).then_inc(gfac, 1)
                    nc.vector.tensor_tensor(qdec[:, :], qdec[:, :], fq, ALU.mult).then_inc(gfac, 1)
                    dve.wait_ge(gexp, 4)
                    nc.vector.tensor_tensor(qI[:, :], qI[:, :], fq, ALU.mult).then_inc(gfac, 1)
                if b == GV + 1:
                    dve.wait_ge(gexp, 5)
                    kk = gk[:, :, :].rearrange("p h t -> p (h t)").rearrange("p (m c) -> p m c", c=64)
                    for i in range(4):
                        n, a = 16 * (i + 1), EK[i]
                        v = ekI[:, a:a + 16 * n].rearrange("p (m c) -> p m c", c=n)
                        nc.vector.tensor_tensor(v, v, kk[:, :, 0:n], ALU.mult).then_inc(gfac, 1)
                if b == GV + 3:
                    dve.wait_ge(att_done, 1)
                    dve.wait_ge(glac_in, 32)
                    for half in range(2):
                        po = 64 * half
                        for i in range(4):
                            n = 16 * (i + 1)
                            src = pX[po:po + n, :].rearrange("p (h c i) -> p h c i", h=4, c=2)[:, :, :, 16 * i:16 * i + 16]
                            dst = att[po:po + n, :, half:4:2, 16 * i:16 * i + 16]
                            for h in range(4):
                                nc.vector.tensor_tensor(dst[:, h, :, :], src[:, h, :, :],
                                                        tri[po:po + n, None, 16 * i:16 * i + 16].to_broadcast([n, 2, 16]),
                                                        ALU.mult).then_inc(att_ready, 1)
                if GG <= b < GOUT:
                    j = b - GG
                    if j < 3:
                        for h in range(4):
                            dve.wait_ge(upd_done, 4 * j + 2 * (h // 2) + 2)
                            ups = pT[:, T * h:T * h + T]
                            if j == 0:
                                nc.vector.tensor_copy(state[:, h, :], ups).then_inc(state_ready, 1)
                            else:
                                dve.wait_ge(o_done, j + 1)
                                dve.wait_ge(state_ready, 4 * j)
                                nc.vector.scalar_tensor_tensor(state[:, h, :], state[:, h, :],
                                                               elast[:, 4 * h + j:4 * h + j + 1], ups,
                                                               ALU.mult, ALU.add).then_inc(state_ready, 1)
                    dve.wait_ge(drained_act, RESULT_DRAIN[FIRST_RESULT[b]][1])
                    g = gs[:, 2 * j:2 * j + 2, :].rearrange("p a b -> p (a b)")
                    nc.vector.scalar_tensor_tensor(g, gth[:, :], 1.0, g, ALU.add, ALU.mult).then_inc(gs_ready, 1)
                    dve.wait_ge(o_ready, j + 1)
                    sqj = sq[:, :, 64 * j:64 * j + 64].rearrange("p (h d) i -> p h d i", d=2)
                    nc.vector.tensor_tensor(tb[:, 0:4, 64 * j:64 * j + 64], sqj[:, :, 0, :], sqj[:, :, 1, :], ALU.add
                                            ).then_inc(osq, 1)
                if b == GOUT - 1:
                    dve.wait_ge(gs_ready, 4)
                    for j in range(4):
                        own(nc.vector.tensor_tensor(y[:, 2 * j:2 * j + 2, :], y[:, 2 * j:2 * j + 2, :],
                                                    gs[:, 2 * j:2 * j + 2, :], ALU.mult))
                    for j in range(4):
                        dve.wait_ge(hrstd, j // 2 + 1)
                        nc.vector.tensor_tensor(y[:, 2 * j:2 * j + 2, :], y[:, 2 * j:2 * j + 2, :],
                                                grs[:, j:j + 1, :].to_broadcast([P, 2, T]), ALU.mult).then_inc(go_full, 1)
                        if j:
                            go_low(j - 1)
                    go_low(3)
                if GOUT <= b < SK or b >= SOUT:
                    n, j = ("n5", b - GOUT) if b < SK else ("n6", b - SOUT)
                    if b == SOUT:
                        dve.wait_ge(x_ready, KT - len(LO_POOL))
                    ps = result(FIRST_RESULT[b])
                    xx = x[:, 2 * j:2 * j + 2, :].rearrange("p a b -> p (a b)")
                    nc.vector.scalar_tensor_tensor(xx, xx, ALPHA, ps[:, :], ALU.mult, ALU.add).then_inc(summed[n], 1)
                    dve.wait_ge(summed[n], j + 1)
                    nc.vector.engine_nop().then_inc(drained_dve, 1)
                if b in (SK - 1, NC - 1):
                    n, l = ("n5", 0) if b == SK - 1 else ("n6", 1)
                    dve.wait_ge(mean_known[n], 1)
                    if n == "n6":
                        dve.wait_ge(roped, len(RH))
                    for j in range(4):
                        nc.vector.tensor_tensor(tb[:, 2 * j:2 * j + 2, :], x[:, 2 * j:2 * j + 2, :],
                                                stat[:, None, :].to_broadcast([P, 2, T]), ALU.subtract
                                                ).then_inc(centered[n], 1)
                    norm_rstd(n)
                    for k in range(KT + 1):
                        if k < KT:
                            nc.vector.scalar_tensor_tensor(tb[:, k, :], tb[:, k, :], col("ln_g", 8 * l + k), rstd[:, :],
                                                           ALU.mult, ALU.mult).then_inc(scaled[n], 1)
                        if n == "n5" and k and k - 1 not in LO_POOL:
                            split_lo(n, tb, lambda i: col("ln_b", i), range(k - 1, k))
                if b in RH and b > KK:
                    if b == SK:
                        dve.wait_ge(swac_in, 32)
                    if b < SV:
                        rope(b, sk[:, 2 * (b - SK):2 * (b - SK) + 2, :], rope2)
                    else:
                        pair, g = (b - SWA) // 4, (b - SWA) % 4
                        if pair >= 2:
                            dve.wait_ge(d_qk, 4 * pair - 4)
                        rope(b, sqr[:, pair % 2, 2 * g:2 * g + 2, :], rope2)
                if SWA <= b < SOUT and (b - SWA) % 4 == 3:
                    pair = (b - SWA) // 4
                    dve.wait_ge(drained_act, RESULT_DRAIN[FIRST_RESULT[b]][1])
                    g = sgs[:, pair % 2, :, :].rearrange("p a b -> p (a b)")
                    nc.vector.scalar_tensor_tensor(g, sth[:, :], 1.0, g, ALU.add, ALU.mult).then_inc(sg_ready, 1)
                    dve.wait_ge(sg_ready, pair + 1)

                def dil_slot(s):
                    if 0 <= s < 16:
                        t = s % 2
                        n = 384 * (t + 1)
                        dve.wait_ge(d_qk, s + 1)
                        if s >= 2:
                            dve.wait_ge(d_exp, s - 1)
                        nc.vector.tensor_tensor_reduce(out=dsc[:, s % 2, 0:n], in0=pS[:, 0:n],
                                                       in1=dmask[:, 384 * t:384 * t + n], op0=ALU.add, op1=ALU.min,
                                                       scale=-(P ** -0.5), scalar=3.0e38,
                                                       accum_out=dnmax[:, s % 4:s % 4 + 1]).then_inc(d_max, 1)
                        dve.wait_ge(d_exp, s + 1)
                        own(nc.vector.reciprocal(drec[:, s % 4:s % 4 + 1], dden[:, s % 4:s % 4 + 1]))
                        nc.vector.tensor_scalar(dp[:, s % 2, 0:n], dp[:, s % 2, 0:n], drec[:, s % 4:s % 4 + 1], None,
                                                ALU.mult).then_inc(d_norm, 1)
                    u = s - 2
                    if 0 <= u < 16:
                        h, t = u // 2, u % 2
                        pair = h // 2
                        dve.wait_ge(d_pv, u + 1)
                        if u >= 2:
                            dve.wait_ge(d_lo, u - 1)
                        nc.vector.tensor_tensor(of[:, u % 2, :], pX[:, T + P * (u % 2):T + P * (u % 2) + P],
                                                sgs[:, pair % 2, h % 2, t * P:t * P + P], ALU.mult).then_inc(d_of, 1)
                        dve.wait_ge(d_hi, u + 1)
                        nc.vector.tensor_tensor(olo[:, h, t * P:t * P + P], of[:, u % 2, :],
                                                ohi[:, h, t * P:t * P + P].bitcast(f32), ALU.subtract).then_inc(d_lo, 1)

                if SWA + 4 <= c < SOUT:
                    dil_slot(c - SWA - 4)
                if c == SOUT:
                    for s in range(12, 18):
                        dil_slot(s)
                if b in LATE:
                    low(c + 2)

        @block.tensor
        def _(pe):
            mm = nc.tensor.matmul

            def ada(a):
                if a in ADA_GPS:
                    pe.wait_ge(ada_first, a + 1)
                    acc = tb[:, a, :]
                elif a < 8:
                    wait_ada(pe, a)
                    w = ada_buffer(a).rearrange("p (k n) -> p k n", k=KT)
                    acc = tb[:, a, :]
                else:
                    pe.wait_ge(ada_pooled, a - 7)
                    pe.wait_ge(mod_ready, (a - 6) // 2)
                    acc = adasum[:, a % 4, :]
                if a == 0:
                    pe.wait_ge(dev_known["n1"], 1)
                for i in range(2):
                    out = pmod[:, 2 * a + i:2 * a + i + 1]
                    n = KT
                    if a < 8 and a not in ADA_GPS:
                        n = ada_dve(a)
                        for k in range(n, KT):
                            mm(out, w[:, k, i * P:i * P + P], cact[:, k:k + 1], start=k == n, stop=False)
                        if i == 0:
                            pe.wait_ge(ada_summed, a + 1 - len(ADA_GPS))
                    last = mm(out, acc[:, i * P:i * P + P], ones[:, :], start=n == KT, stop=True)
                last.then_inc(ada_used, 1)

            def three(out, ah, al, bh, bl, first, last):
                mm(out, ah, bh, start=first, stop=False)
                mm(out, al, bh, start=False, stop=False)
                return mm(out, ah, bl, start=False, stop=last)

            def bank(r):
                if r >= NB:
                    who, n = RESULT_DRAIN[r - NB]
                    pe.wait_ge(drained[who], n)
                return res[r % NB]

            def wait_weights(c):
                pe.wait_ge(lo_dve, c + 1)
                pe.wait_ge(lo_pool, c + 1)

            def weights(c):
                wait_weights(c)
                return weights_of(c)

            def weights_of(c):
                kt, w = kt_of(c)
                return (whi[c % SPL][:, 0:kt * w].rearrange("p (k n) -> p k n", k=kt),
                        wlo[c % SPL][:, 0:kt * w].rearrange("p (k n) -> p k n", k=kt))

            def half_product(c, i, k, ps, ih, il, at=None):
                at = k if at is None else at
                wh, wl = weights_of(c)
                return three(ps[:, i * T:i * T + T], wh[:, k, i * P:i * P + P], wl[:, k, i * P:i * P + P],
                             ih[:, k, :], il[:, k, :], at == 0, at == KT - 1)

            def fm(c, ih, il, half=None, ready=None):
                wait_weights(c)
                ps = bank(FIRST_RESULT[c])
                for i in range(2):
                    for at, k in enumerate(ARRIVAL if ready else range(KT)):
                        if ready and i == 0:
                            ready(k)
                        last = half_product(c, i, k, ps, ih, il, at)
                    if i == 0 and half:
                        half()
                last.then_inc(product_done, 1)

            def warm(n):
                for _ in range(n):
                    mm(pS[:, 512:640], ident[:, :], ident[:, :], start=True, stop=True)

            def fm_first(c, ih, il, ready, order=range(KT)):
                wait_weights(c)
                wait_weights(c + 1)
                ps = bank(FIRST_RESULT[c]), bank(FIRST_RESULT[c + 1])
                for i, k in enumerate(order):
                    ready(k)
                    for d in range(2):
                        half_product(c + d, 0, k, ps[d], ih, il, i)
                for d in range(2):
                    for k in range(KT):
                        last = half_product(c + d, 1, k, ps[d], ih, il)
                    last.then_inc(product_done, 1)

            def tm(c, ih, il):
                wh, wl = weights(c)
                w = kt_of(c)[1]
                ps = bank(FIRST_RESULT[c])
                for t in range(2):
                    for k in range(KT):
                        last = three(ps[:, t * 256:t * 256 + w], ih[:, k, t * P:t * P + P], il[:, k, t * P:t * P + P],
                                     wh[:, k, :], wl[:, k, :], k == 0, k == KT - 1)
                last.then_inc(product_done, 1)

            def in_low(n, k):
                if k in LO_POOL:
                    return in_lo_pool[n], LO_POOL.index(k) + 1
                return in_lo[n], len([i for i in range(k + 1) if i not in LO_POOL])

            def mean(n, src, ks, need, count=1):
                for k in ks:
                    pe.wait_ge(need, (k // (KT // count)) + 1 if count != KT else k + 1)
                    last = mm(stat, meanw[:, :], src[:, k, :], start=k == 0, stop=k == KT - 1)
                if k == KT - 1:
                    last.then_inc(mean_known[n], 1)

            def units(s):
                if s < 24:
                    m, t, h = s // 8, s % 8 // 4, s % 4
                    nk, po = P * (t + 1), 64 * (h % 2)
                    q = qkv[("qa", "qb", "qc")[m]]
                    k = (qkv["ka"][po:po + 64, h // 2, 0:nk], qkv["kb"][po:po + 64, h // 2, 0:nk],
                         qkv["kk"][po:po + 64, 0, 0:nk])[m]
                    if s < 2:
                        pe.wait_ge(bB_ready, 3 + s)
                    if s == 0:
                        pe.wait_ge(drained_act, RESULT_DRAIN[FIRST_RESULT[VB]][1])
                    if s >= 2:
                        pe.wait_ge(smax_done, s - 1)
                    mm(pS[:, 512 * (s % 2):512 * (s % 2) + nk], q[po:po + 64, h // 2, t * P:t * P + P], k,
                       start=True, stop=True).then_inc(qk_done, 1)
                u = s - 2
                if 0 <= u < 24:
                    nk = u % 8 // 4 + 1
                    pe.wait_ge(norm_done, u + 1)
                    if u:
                        pe.wait_ge(pT_ready, u)
                    for i in range(nk):
                        last = nc.tensor.transpose(pT[:, 256 * (u % 2) + P * i:256 * (u % 2) + P * i + P],
                                                   up[:, u % 3, P * i:P * i + P], ident[:, :])
                    last.then_inc(tr_done, 1)
                u = s - 3
                if 0 <= u < 24:
                    m, t, h = u // 8, u % 8 // 4, u % 4
                    po = 64 * (h % 2)
                    pe.wait_ge(pT_ready, u + 1)
                    if u % 8 == 0 and m:
                        pe.wait_ge(y_lo, m)
                    for i in range(t + 1):
                        v = (qkv["va"], qkv["vb"])[m][:, i, 64 * h:64 * h + 64] if m < 2 else misc[:, i, 0:64]
                        last = mm(pO[po:po + 64, T * (h // 2) + t * P:T * (h // 2) + t * P + P], v,
                                  upT[:, u % 2, P * i:P * i + P], start=i == 0, stop=i == t)
                    last.then_inc(pv_done, 1)

            def dilated(s):
                if 0 <= s < 16:
                    h, t = s // 2, s % 2
                    pair, hh, nk = h // 2, h % 2, P * (t + 1)
                    pe.wait_ge(roped, RI[SWA + 4 * pair + 2] + 1)
                    if s:
                        pe.wait_ge(d_max, s)
                    for g in range(3):
                        last = mm(pS[:, g * nk:g * nk + nk], sqr[:, pair % 2, 2 * g + hh, t * P:t * P + P],
                                  sk[:, 2 * g + h // 4, 0:nk], start=True, stop=True)
                    last.then_inc(d_qk, 1)
                u = s - 1
                if 0 <= u < 16:
                    n = 3 * (u % 2 + 1)
                    pe.wait_ge(d_norm, u + 1)
                    if u:
                        pe.wait_ge(d_pT, u)
                    for i in range(n):
                        last = nc.tensor.transpose(pT[:, P * i:P * i + P], dp[:, u % 2, P * i:P * i + P], ident[:, :])
                    last.then_inc(d_tr, 1)
                u = s - 2
                if 0 <= u < 16:
                    h, t = u // 2, u % 2
                    nk = t + 1
                    pe.wait_ge(d_pT, u + 1)
                    if u:
                        pe.wait_ge(d_of, u)
                    for i in range(3 * nk):
                        g, kt = i // nk, i % nk
                        v = sv[:, kt, 256 * g + P * (h // 4):256 * g + P * (h // 4) + P]
                        last = mm(pX[:, T + P * (u % 2):T + P * (u % 2) + P], v, dpT[:, u % 2, P * i:P * i + P],
                                  start=i == 0, stop=i == 3 * nk - 1)
                    last.then_inc(d_pv, 1)

            pe.wait_ge(const_set, 3)
            pe.wait_ge(cact_ready, 1)
            mean("n1", sq, range(KT), squares["n1"], KT)
            for a in range(8):
                ada(a)
            warm(10)
            for c in range(NC):
                if c < BRANCH:
                    if c == QC:
                        fm(c, hhi, hlo, None, lambda k: pe.wait_ge(*in_low("n1", k)))
                    elif c in (MISC, VA, VB):
                        tm(c, hhi, hlo)
                    else:
                        half = (lambda c=c: units(2 * (c - ZG))) if c >= ZG else None
                        fm(c, hhi, hlo, half)
                    if c in ADA_USE:
                        ada(ADA_USE[c])
                        ada(ADA_USE[c] + 1)
                    if QA <= c < QA + 4:
                        for e in (2 * (c - QA), 2 * (c - QA) + 1):
                            t, h = e // 4, e % 4
                            nk, po = P * (t + 1), 64 * (h % 2)
                            if e == 0:
                                pe.wait_ge(roped, 3)
                            if e >= 2:
                                pe.wait_ge(idx_relu, e - 1)
                            mm(pS[:, 512 * (e % 2):512 * (e % 2) + nk], qkv["qi"][po:po + 64, h // 2, t * P:t * P + P],
                               qkv["kk"][po:po + 64, 1, 0:nk], start=True, stop=True).then_inc(idx_done, 1)
                    if c == KA:
                        pe.wait_ge(const_in, 32)
                        pe.wait_ge(drained_act, RESULT_DRAIN[FIRST_RESULT[MISC]][1])
                        for t in range(2):
                            nc.tensor.transpose(pT[0:4, P * t:P * t + P], misc[:, t, 64:68], ident[:, :]).then_inc(fT_done, 1)
                    if c in (KB, VB):
                        pe.wait_ge(fcum_ready, 1)
                        pe.wait_ge(idx_relu, 8)
                        pe.wait_ge(mixc_in, 80)
                        for h in ((0, 1) if c == KB else (2, 3)):
                            if h >= 2:
                                pe.wait_ge(bB_ready, h - 1)
                            mm(pS[:, 512 * (h % 2):512 * (h % 2) + T], sel[:, P * h:P * h + P], fgate[:, 4, :],
                               start=True, stop=True).then_inc(bB_done, 1)
                    if c >= ZG:
                        units(2 * (c - ZG) + 1)
                elif c < WOUT:
                    b = c - BRANCH
                    wh, wl = weights(c)
                    if b == 2:
                        pe.wait_ge(y_lo, 3)
                    for j in range(4):
                        ps = bank(FIRST_RESULT[c] + j)
                        for i in range(2):
                            n = 2 * j + i
                            for k in range(2):
                                last = three(ps[:, i * T:i * T + T], wh[:, k, n * P:n * P + P], wl[:, k, n * P:n * P + P],
                                             yhi[:, b, k * T:k * T + T], ylo[:, b, k * T:k * T + T], k == 0, k == 1)
                        last.then_inc(product_done, 1)
                        if b == 0 and j < 3:
                            units(24 + j)
                    if c in ADA_USE:
                        ada(ADA_USE[c])
                        ada(ADA_USE[c] + 1)
                elif c < UP:
                    if c == WOUT:
                        warm(8)
                        fm_first(c, hhi, hlo, lambda k: pe.wait_ge(mg_lo, k // 2 + 1))
                    elif c > WOUT + 1:
                        fm(c, hhi, hlo)
                    if c == WOUT + 2:
                        pe.wait_ge(mod_ready, 7)
                    if c > WOUT + 1:
                        mean("n2", sq, range(4) if c == WOUT + 2 else (4, 5), squares["n2"], 4)
                    if c == UP - 1:
                        mean("n2", sq, (6, 7), squares["n2"], 4)
                        pe.wait_ge(dev_known["n2"], 1)
                        warm(22)
                        for i, j in enumerate(PAIRS):
                            pe.wait_ge(squares["n3"], i + 1)
                            for k in (2 * j, 2 * j + 1):
                                last = mm(stat, meanw[:, :], sq[:, k, :], start=i == 0 and k % 2 == 0, stop=i == 3 and k % 2 == 1)
                        last.then_inc(mean_known["n3"], 1)
                        warm(13)
                elif c < DOWN:
                    if c == UP:
                        fm_first(c, hhi, hlo, lambda k: pe.wait_ge(*in_low("n3", k)), ARRIVAL)
                    elif c > UP + 1:
                        fm(c, hhi, hlo)
                    if c in ADA_USE:
                        ada(ADA_USE[c])
                        ada(ADA_USE[c] + 1)
                elif c < GQ:
                    j, kg = (c - DOWN) // 3, (c - DOWN) % 3
                    wh, wl = weights(c)
                    kt = kt_of(c)[0]
                    r = 2 * j + FIRST_RESULT[DOWN]
                    for i in range(2):
                        ps = bank(r + i) if kg == 0 else res[(r + i) % NB]
                        for k in range(kt):
                            kk = 8 * kg + k
                            if j == 0 and i == 0 and kk % 2 == 0:
                                pe.wait_ge(u_lo, kk // 2 + 1)
                            last = three(ps[:, 0:T], wh[:, k, i * P:i * P + P], wl[:, k, i * P:i * P + P],
                                         uhi[:, kk, :], ulo[:, kk, :], kk == 0, kk == FT - 1)
                        if i == 1 or kg == 2:
                            last.then_inc(product_done, 1)
                    if kg == 1 and j:
                        mean("n4", sq, (2 * j - 2, 2 * j - 1), squares["n4"], KT)
                    if c == GQ - 1:
                        mean("n4", sq, (6, 7), squares["n4"], KT)
                        warm(36)
                elif c < GOUT:
                    if GV <= c < GG:
                        tm(c, hhi, hlo)
                    elif c == GA:
                        wh, wl = weights(c)
                        ps = bank(FIRST_RESULT[c])
                        for k in range(KT):
                            last = three(ps[0:16, 0:T], wh[:, k, :], wl[:, k, :], hhi[:, k, :], hlo[:, k, :], k == 0, k == KT - 1)
                        last.then_inc(product_done, 1)
                    else:
                        if c == GQ:
                            fm_first(c, hhi, hlo, lambda k: pe.wait_ge(in_lo["n4"], PAIRS.index(k // 2) + 1),
                                     [2 * j + i for j in PAIRS for i in range(2)])
                        elif c > GQ + 1:
                            fm(c, hhi, hlo)
                    if c == GA:
                        pe.wait_ge(drained_act, RESULT_DRAIN[FIRST_RESULT[GA]][1])
                        pe.wait_ge(glac_in, 32)
                        for h in range(4):
                            mm(pS[:, h * T:h * T + T], wa2[:, h * P:h * P + P], alrT[:, :], start=True, stop=True
                               ).then_inc(la_done, 1)
                    if c == GV + 3:
                        pe.wait_ge(gfac, 1)
                        for t in range(2):
                            for h in range(4):
                                nc.tensor.transpose(pT[:, 512 * t + P * h:512 * t + P * h + P],
                                                    kdec[:, h * T + t * P:h * T + t * P + P], ident[:, :]).then_inc(kd_T, 1)
                    if c == GV + 3:
                        pe.wait_ge(gfac, 7)
                        for h in range(4):
                            for ch in range(4):
                                po, m = 64 * (ch % 2), 4 * h + ch
                                for i in range(4):
                                    n = 16 * (i + 1)
                                    last = mm(pX[po:po + n, P * h + 64 * (ch // 2) + 16 * i:P * h + 64 * (ch // 2) + 16 * i + 16],
                                              ekI[:, EK[i] + m * n:EK[i] + m * n + n], qI[:, 64 * m + 16 * i:64 * m + 16 * i + 16],
                                              start=True, stop=True)
                        last.then_inc(att_done, 1)
                    if GG <= c < GOUT:
                        j = c - GG
                        t, po = j // 2, 64 * (j % 2)
                        if j == 0:
                            pe.wait_ge(att_ready, 32)
                            pe.wait_ge(gfac, 2)
                            pe.wait_ge(kdT_ready, 2)
                            pe.wait_ge(drained_act, RESULT_DRAIN[FIRST_RESULT[GG - 1]][1])
                        if j >= 2:
                            pe.wait_ge(o_ready, j - 1)
                        for h in range(4):
                            if j:
                                pe.wait_ge(state_ready, 4 * (j - 1) + h + 1)
                            for d in range(2):
                                o = pS[:, 512 * (j % 2) + 64 * (2 * h + d):512 * (j % 2) + 64 * (2 * h + d) + 64]
                                if j:
                                    mm(o, state[:, h, d * P:d * P + P], qdec[:, h * T + 64 * j:h * T + 64 * j + 64],
                                       start=True, stop=False)
                                last = mm(o, gv[:, t, 256 * h + P * d:256 * h + P * d + P], att[:, h, j, :],
                                          start=j == 0, stop=True)
                        last.then_inc(o_done, 1)
                        if j < 3:
                            for h in range(4):
                                mm(pT[:, T * h:T * h + T], kdT[po:po + 64, t, h, :], gv[po:po + 64, t, 256 * h:256 * h + 256],
                                   start=True, stop=True).then_inc(upd_done, 1)
                    if c == GOUT - 1:
                        pe.wait_ge(osq, 4)
                        for h in range(4):
                            mm(pS[:, h * T:h * T + T], headw[:, :], tb[:, h, :], start=True, stop=True).then_inc(hmean, 1)
                        for i in range(18):
                            mm(pT[:, 512:640], ident[:, :], ident[:, :], start=True, stop=True)
                elif c < SK:
                    if c == GOUT:
                        fm_first(c, hhi, hlo, lambda k: pe.wait_ge(go_lo, k // 2 + 1))
                    elif c > GOUT + 1:
                        fm(c, hhi, hlo)
                    if c > GOUT + 1:
                        mean("n5", x, range(4) if c == GOUT + 2 else (4, 5), summed["n5"], 4)
                    if c == SK - 1:
                        mean("n5", x, (6, 7), summed["n5"], 4)
                        warm(8)
                        pe.wait_ge(centered["n5"], 4)
                        mean("n5", sq, range(KT), squares["n5"], 4)
                        warm(13)
                elif c < SOUT:
                    if SV <= c < SWA:
                        tm(c, hhi, hlo)
                    else:
                        if c == SK:
                            fm_first(c, hhi, hlo, lambda k: pe.wait_ge(*in_low("n5", k)), ARRIVAL)
                        elif c > SK + 1:
                            fm(c, hhi, hlo)
                    if c >= SWA + 4:
                        if c == SWA + 4:
                            pe.wait_ge(drained_act, RESULT_DRAIN[FIRST_RESULT[SWA - 1]][1])
                        dilated(c - SWA - 4)
                    if c == SOUT - 1:
                        for s in range(12, 18):
                            dilated(s)
                else:
                    if c == SOUT:
                        fm_first(c, ohi, olo, lambda k: pe.wait_ge(d_lo, 2 * k + 2))
                    elif c > SOUT + 1:
                        fm(c, ohi, olo)
                    if c > SOUT + 1:
                        mean("n6", x, range(4) if c == SOUT + 2 else (4, 5), summed["n6"], 4)
                    if c == NC - 1:
                        mean("n6", x, (6, 7), summed["n6"], 4)
                        warm(8)
                        pe.wait_ge(centered["n6"], 4)
                        mean("n6", sq, range(KT), squares["n6"], 4)


RI, RH = {}, {}
_moves = 0
for _c in [QC, QI, KK, SK, SK + 1, SK + 2] + [SWA + 4 * _p + _g for _p in range(4) for _g in range(3)]:
    RI[_c] = len(RI)
    _moves += 4 if _c <= KK else 2
    RH[_c] = _moves
EK = [16 * 16 * i * (i + 1) // 2 for i in range(4)]


def kernel(**inp):
    import numpy as np
    import concourse.bacc as bacc
    from concourse import mybir as mb
    from concourse.bass_utils import run_bass_kernel_spmd

    a = {k: np.asarray(v) for k, v in inp.items()}
    f4 = np.float32

    def fm(v):
        return np.ascontiguousarray(v.reshape(-1, P).T)

    forget = np.zeros((P, 1), f4)
    forget[0:4, 0] = a["b_forget"][0]
    cols = np.concatenate([
        fm(a["c"][0]), fm(a["b_ada"][0]), fm(a["norm_g"][0]), fm(a["b_gate"][0]), fm(a["conv_w"][0]),
        fm(a["conv_b"][0]), fm(a["gla_b_a2_2"][0]), fm(a["gla_norm_g_2"][0]), fm(a["ln_g_2"]), fm(a["ln_b_2"]),
        forget, np.full((P, 1), 1e-6, f4), np.full((P, 1), 1e-5, f4)], axis=1)

    def rope_table(dim):
        half = dim // 2
        inv = (f4(10000.0) ** (-np.arange(half, dtype=f4) * f4(2.0) / f4(dim))).astype(f4)
        p = np.arange(P) % dim
        ang = inv[p % half][:, None] * np.arange(T, dtype=f4)[None, :]
        sign = np.where(p < half, -1.0, 1.0).astype(f4)[:, None]
        return np.stack([np.cos(ang), np.sin(ang) * sign], axis=1).astype(f4)

    q = np.arange(P)[:, None]

    def two_tiles(ok):
        return [np.where(ok(q + P * t, np.arange(P * (t + 1))[None, :]), 0.0, NEG).astype(f4) for t in range(2)]

    amask = np.concatenate(two_tiles(lambda i, j: j // 64 <= i // 64), axis=1)
    cmask = np.concatenate(two_tiles(lambda i, j: j <= i), axis=1)
    dil = [two_tiles(lambda i, j, d=d, w=w: (j <= i) & (i - j <= w) & ((i - j) % d == 0))
           for w, d in ((128, 1), (512, 4), (2048, 16))]
    dmask = np.concatenate([m[t] for t in range(2) for m in dil], axis=1)
    tri = (np.arange(P)[:, None] % 64 <= np.arange(64)[None, :]).astype(f4)
    sel = np.zeros((4, 4, P), f4)
    for h in range(4):
        sel[h, h, :] = -8.0
    rel = [np.clip(q + P * t - np.arange(P * (t + 1))[None, :], -128, 128) + 128 for t in range(2)]
    table = a["rel_table"][0]
    relb = np.ascontiguousarray(np.concatenate([table[:, r] for r in rel], axis=2).transpose(1, 0, 2))

    arrays = {
        "xT": np.ascontiguousarray(a["x"][0].T.reshape(KT, P, T).transpose(1, 0, 2)),
        "cols": cols, "ident": np.eye(P, dtype=f4), "rope1": rope_table(64), "rope2": rope_table(128),
        "amask": amask, "cmask": cmask, "tri": tri, "dmask": dmask, "sel": sel.reshape(4, 512), "relb": relb,
        "w_a2": a["gla_w_a2_2"][0],
        "w_ada": a["w_ada"][0], "w_in": a["w_in"][0], "w_branch": a["w_branch"][0], "w_out": a["w_out"][0],
        "w_up": a["w_up"][0], "w_down": a["w_down"][0], "gla_in": a["gla_w_in_2"][0], "gla_out": a["gla_w_out_2"][0],
        "w_kv": a["w_kv_2"], "swa_in": a["swa_w_in_2"][0], "swa_out": a["swa_w_out_2"][0],
    }
    order = ["xT", "cols", "ident", "rope1", "rope2", "amask", "cmask", "tri", "dmask", "sel", "relb", "w_a2",
             "w_ada", "w_in", "w_branch", "w_out", "w_up", "w_down", "gla_in", "gla_out", "w_kv", "swa_in", "swa_out"]
    nc = bacc.Bacc("TRN2", target_bir_lowering=False, num_devices=1, dynamic_dma_scratch_size=8192)
    sent = {f"in_{n}": np.ascontiguousarray(arrays[n]) for n in order}
    args = [nc.dram_tensor(n, v.shape, mb.dt.float32, kind="ExternalInput").ap() for n, v in sent.items()]
    out = nc.dram_tensor("outT", (P, KT, T), mb.dt.float32, kind="ExternalOutput").ap()
    build(nc, *args, out)
    r = run_bass_kernel_spmd(nc, [sent], core_ids=[0])
    got = r.results[0]["outT"]
    return np.ascontiguousarray(got.transpose(1, 0, 2).reshape(D, T).T)[None]
```
